# Optimizing a Trainium2 kernel written in Bass

```python
import math
import jax
import jax.numpy as jnp
from jax import lax
import numpy as np

D_MODEL = 1024
BATCH = 1
SEQ = 512
DEPTH = 1

GRID_W = 64
CTX_LEN = 256
EPS = 1e-6
F32 = jnp.float32

POOL_WINDOWS = (2, 4, 8, 16)
D_POOL = D_MODEL
POOL_GROUP = D_POOL // len(POOL_WINDOWS)

D_MLSTM = D_MODEL
MLSTM_HEADS = 4
MLSTM_HEAD_DIM = D_MLSTM // MLSTM_HEADS
MLSTM_CHUNK = 64
QK_CONV = 4

D_SSD = D_MODEL
SSD_HEAD_DIM = 64
SSD_HEADS = D_SSD // SSD_HEAD_DIM
SSD_GROUPS = 4
SSD_STATE = 128
SSD_CHUNK = 64
SSD_CONV = 4
D_XBC = D_SSD + 2 * SSD_GROUPS * SSD_STATE

N_BRANCH = 3
D_BRANCH = D_MODEL

N_EXPERT_GROUPS = 4
EXPERTS_PER_GROUP = 8
N_EXPERTS = N_EXPERT_GROUPS * EXPERTS_PER_GROUP
TOP_K_IN_GROUP = 2
D_EXPERT = 512
MOE_BLOCK = 256

IN_SPLITS = (D_POOL,
             D_MLSTM, D_MLSTM, D_MLSTM, D_MLSTM,
             4 * MLSTM_HEADS,
             D_SSD, D_SSD,
             SSD_GROUPS * SSD_STATE, SSD_GROUPS * SSD_STATE,
             2 * SSD_HEADS,
             N_BRANCH * D_MODEL)
D_IN = sum(IN_SPLITS)

kernel_name = 'hybrid_pool_mlstm_ssd_hmoe_diffusion'

def rmsnorm(x, g):
    xf = x.astype(F32)
    y = xf * lax.rsqrt(jnp.mean(xf * xf, axis=-1, keepdims=True) + EPS)
    return (y * g.astype(F32)).astype(x.dtype)

def modulate(h, shift, scale):
    return h * (1 + scale) + shift

def split_cols(u, sizes):
    out, start = [], 0
    for s in sizes:
        out.append(u[..., start:start + s])
        start += s
    return out

def flip(t):
    return jnp.flip(t, axis=1)

def to_colmajor(t):
    b, l = t.shape[:2]
    rows = l // GRID_W
    return t.reshape(b, rows, GRID_W, *t.shape[2:]).swapaxes(1, 2).reshape(t.shape)

def to_rowmajor(t):
    b, l = t.shape[:2]
    rows = l // GRID_W
    return t.reshape(b, GRID_W, rows, *t.shape[2:]).swapaxes(1, 2).reshape(t.shape)

def short_conv(x, w, b):
    k = w.shape[0]
    l = x.shape[1]
    xp = jnp.pad(x, ((0, 0), (k // 2, k - 1 - k // 2), (0, 0)))
    y = b + w[0] * xp[:, 0:l]
    for j in range(1, k):
        y = y + w[j] * xp[:, j:j + l]
    return y

def window_mean_minus_self(x, w):
    l = x.shape[-2]
    t = np.arange(l)
    lo = np.clip(t - w // 2, 0, l - 1)
    hi = np.clip(t - w // 2 + w - 1, 0, l - 1)
    cnt = jnp.asarray((hi - lo + 1).astype(np.float32))[:, None]
    xf = x.astype(F32)
    cs = jnp.cumsum(xf, axis=-2)
    cs = jnp.concatenate([jnp.zeros_like(cs[..., :1, :]), cs], axis=-2)
    s = jnp.take(cs, hi + 1, axis=-2) - jnp.take(cs, lo, axis=-2)
    return s / cnt - xf

def pool_mixer(a, pool_w, pool_scale, grid):
    b, l, cw = a.shape
    if grid:
        a = a.reshape(b, l // GRID_W, GRID_W, cw)
    groups = jnp.split(a, len(POOL_WINDOWS), axis=-1)
    pooled = jnp.stack([window_mean_minus_self(g, w) for g, w in zip(groups, POOL_WINDOWS)], axis=-2)
    y = jnp.einsum('...gc,gcd->...gd', pooled, pool_w.astype(F32)).reshape(b, l, cw)
    return (y * pool_scale.astype(F32)).astype(a.dtype)

def mlstm_inputs(q, k, v, gates, conv_w, conv_b, gate_b):
    b, l, _ = q.shape
    qk = jax.nn.silu(short_conv(jnp.concatenate([q, k], axis=-1), conv_w, conv_b))
    q, k = jnp.split(qk, 2, axis=-1)
    heads = lambda t: t.astype(F32).reshape(b, l, MLSTM_HEADS, MLSTM_HEAD_DIM)
    q, k, v = heads(q), heads(k) * (MLSTM_HEAD_DIM ** -0.5), heads(v)
    g = gates.astype(F32).reshape(b, l, 4, MLSTM_HEADS) + gate_b.astype(F32)
    fwd = (g[:, :, 0], jax.nn.log_sigmoid(g[:, :, 2]))
    bwd = (g[:, :, 1], jax.nn.log_sigmoid(g[:, :, 3]))
    return q, k, v, fwd, bwd

def mlstm_scan(q, k, v, ig, lf, state):
    b, l, h, dh = q.shape
    nc = l // MLSTM_CHUNK
    causal = jnp.tril(jnp.ones((MLSTM_CHUNK, MLSTM_CHUNK), bool))

    def chunks(t):
        return jnp.moveaxis(t.reshape(b, nc, MLSTM_CHUNK, *t.shape[2:]), 1, 0)

    def step(carry, inp):
        c_st, n_st, m_st = carry
        qc, kc, vc, ic, fc = inp
        cum = jnp.cumsum(fc, axis=1)
        dmat = cum[:, :, None, :] - cum[:, None, :, :] + ic[:, None, :, :]
        dmat = jnp.where(causal[None, :, :, None], dmat, -jnp.inf)
        g = cum + m_st[:, None, :]
        m_t = jnp.maximum(g, dmat.max(axis=2))
        w = jnp.exp(dmat - m_t[:, :, None, :])
        sg = jnp.exp(g - m_t)
        a = w * jnp.einsum('bthd,bshd->btsh', qc, kc)
        num = jnp.einsum('btsh,bshe->bthe', a, vc) + sg[..., None] * jnp.einsum('bthd,bhde->bthe', qc, c_st)
        den = a.sum(axis=2) + sg * jnp.einsum('bthd,bhd->bth', qc, n_st)
        h_out = num / jnp.maximum(jnp.abs(den), jnp.exp(-m_t))[..., None]
        last = cum[:, -1]
        wl_log = last[:, None] - cum + ic
        m_new = jnp.maximum(last + m_st, wl_log.max(axis=1))
        wl = jnp.exp(wl_log - m_new[:, None])
        decay = jnp.exp(last + m_st - m_new)
        c_st = decay[..., None, None] * c_st + jnp.einsum('bsh,bshd,bshe->bhde', wl, kc, vc)
        n_st = decay[..., None] * n_st + jnp.einsum('bsh,bshd->bhd', wl, kc)
        return (c_st, n_st, m_new), h_out

    state, hs = lax.scan(step, state, (chunks(q), chunks(k), chunks(v), chunks(ig), chunks(lf)))
    return jnp.moveaxis(hs, 0, 1).reshape(b, l, h, dh), state

def mlstm_out(h, o, norm_g):
    b, l = o.shape[:2]
    hn = h * lax.rsqrt(jnp.mean(h * h, axis=-1, keepdims=True) + EPS)
    hn = hn.reshape(b, l, D_MLSTM) * norm_g.astype(F32)
    return (jax.nn.sigmoid(o.astype(F32)) * hn).astype(o.dtype)

def ssd_inputs(xs, bs, cs, dt_raw, conv_w, conv_b, dt_bias):
    b, l, _ = xs.shape
    xbc = jax.nn.silu(short_conv(jnp.concatenate([xs, bs, cs], axis=-1), conv_w, conv_b))
    xs, bs, cs = split_cols(xbc, (D_SSD, SSD_GROUPS * SSD_STATE, SSD_GROUPS * SSD_STATE))
    xh = xs.astype(F32).reshape(b, l, SSD_HEADS, SSD_HEAD_DIM)
    bg = bs.astype(F32).reshape(b, l, SSD_GROUPS, SSD_STATE)
    cg = cs.astype(F32).reshape(b, l, SSD_GROUPS, SSD_STATE)
    dt = jax.nn.softplus(dt_raw.astype(F32).reshape(b, l, 2, SSD_HEADS) + dt_bias.astype(F32))
    return xh, bg, cg, dt[:, :, 0], dt[:, :, 1]

def ssd_scan(x, dt, a_neg, bm, cm, s0):
    b, l, h, p = x.shape
    g, n = bm.shape[2:]
    hg = h // g
    q = SSD_CHUNK
    nc = l // q
    xc = x.reshape(b, nc, q, g, hg, p)
    dtc = dt.reshape(b, nc, q, g, hg)
    bc = bm.reshape(b, nc, q, g, n)
    cc = cm.reshape(b, nc, q, g, n)
    acs = jnp.cumsum(dtc * a_neg.reshape(g, hg), axis=2)
    causal = jnp.tril(jnp.ones((q, q), bool))
    seg = acs[:, :, :, None] - acs[:, :, None, :]
    lmat = jnp.exp(jnp.where(causal[:, :, None, None], seg, -jnp.inf))
    cb = jnp.einsum('bctgn,bcsgn->bctsg', cc, bc)
    xdt = xc * dtc[..., None]
    y_intra = jnp.einsum('bctsg,bctsgh,bcsghp->bctghp', cb, lmat, xdt)
    decay_to_end = jnp.exp(acs[:, :, -1:] - acs)
    chunk_states = jnp.einsum('bcsgn,bcsgh,bcsghp->bcghpn', bc, decay_to_end, xdt)
    chunk_decay = jnp.exp(acs[:, :, -1])

    def step(s, inp):
        st, dec = inp
        return dec[..., None, None] * s + st, s

    s_final, s_starts = lax.scan(step, s0.reshape(b, g, hg, p, n),
                                 (jnp.moveaxis(chunk_states, 1, 0), jnp.moveaxis(chunk_decay, 1, 0)))
    s_starts = jnp.moveaxis(s_starts, 0, 1)
    y_inter = jnp.einsum('bctgn,bcghpn,bctgh->bctghp', cc, s_starts, jnp.exp(acs))
    return (y_intra + y_inter).reshape(b, l, h, p), s_final.reshape(b, h, p, n)

def ssd_out(y, xh, d_skip, z, norm_g):
    b, l = z.shape[:2]
    y = (y + d_skip[:, None] * xh).reshape(b, l, D_SSD)
    return rmsnorm(y * jax.nn.silu(z.astype(F32)), norm_g).astype(z.dtype)

def merge_branches(branches, gate_pre, w_branch, w_out):
    br = jnp.stack(branches, axis=-2)
    proj = jnp.einsum('blid,ide->blie', br, w_branch)
    gate = jax.nn.sigmoid(gate_pre.astype(F32)).reshape(proj.shape).astype(proj.dtype)
    return (gate * proj).sum(axis=-2) @ w_out

def token_mixer(hc, hl, keep_ctx, w_in, pool_w, pool_scale, mlstm_conv_w, mlstm_conv_b, mlstm_gate_b,
                mlstm_norm_g, ssd_conv_w, ssd_conv_b, ssd_dt_bias, ssd_a_log, ssd_d, ssd_norm_g,
                w_branch, w_out):
    b = hl.shape[0]
    uc = hc @ w_in
    ul = hl @ w_in
    pa_c, q_c, k_c, v_c, o_c, ga_c, sx_c, sz_c, sb_c, sc_c, sdt_c, mg_c = split_cols(uc, IN_SPLITS)
    pa_l, q_l, k_l, v_l, o_l, ga_l, sx_l, sz_l, sb_l, sc_l, sdt_l, mg_l = split_cols(ul, IN_SPLITS)

    pool_l = pool_mixer(pa_l, pool_w, pool_scale, True)

    qc, kc, vc, gfc, gbc = mlstm_inputs(q_c, k_c, v_c, ga_c, mlstm_conv_w, mlstm_conv_b, mlstm_gate_b)
    ql, kl, vl, gfl, gbl = mlstm_inputs(to_colmajor(q_l), to_colmajor(k_l), to_colmajor(v_l),
                                        to_colmajor(ga_l), mlstm_conv_w, mlstm_conv_b, mlstm_gate_b)
    zero_m = (jnp.zeros((b, MLSTM_HEADS, MLSTM_HEAD_DIM, MLSTM_HEAD_DIM), F32),
              jnp.zeros((b, MLSTM_HEADS, MLSTM_HEAD_DIM), F32),
              jnp.zeros((b, MLSTM_HEADS), F32))
    h_cf, st_f = mlstm_scan(qc, kc, vc, gfc[0], gfc[1], zero_m)
    h_cb, st_b = mlstm_scan(flip(qc), flip(kc), flip(vc), flip(gbc[0]), flip(gbc[1]), zero_m)
    h_lf, _ = mlstm_scan(ql, kl, vl, gfl[0], gfl[1], st_f)
    h_lb, _ = mlstm_scan(flip(ql), flip(kl), flip(vl), flip(gbl[0]), flip(gbl[1]), st_b)
    mlstm_l = mlstm_out(to_rowmajor(h_lf + flip(h_lb)), o_l, mlstm_norm_g)

    a_neg = -jnp.exp(ssd_a_log.astype(F32))
    d_skip = ssd_d.astype(F32)
    xc_, bc_, cc_, dtf_c, dtb_c = ssd_inputs(sx_c, sb_c, sc_c, sdt_c, ssd_conv_w, ssd_conv_b, ssd_dt_bias)
    xl_, bl_, cl_, dtf_l, dtb_l = ssd_inputs(sx_l, sb_l, sc_l, sdt_l, ssd_conv_w, ssd_conv_b, ssd_dt_bias)
    zero_s = jnp.zeros((b, SSD_HEADS, SSD_HEAD_DIM, SSD_STATE), F32)
    y_cf, s_f = ssd_scan(xc_, dtf_c, a_neg[0], bc_, cc_, zero_s)
    y_cb, s_b = ssd_scan(flip(xc_), flip(dtb_c), a_neg[1], flip(bc_), flip(cc_), zero_s)
    y_lf, _ = ssd_scan(xl_, dtf_l, a_neg[0], bl_, cl_, s_f)
    y_lb, _ = ssd_scan(flip(xl_), flip(dtb_l), a_neg[1], flip(bl_), flip(cl_), s_b)
    ssd_l = ssd_out(y_lf + flip(y_lb), xl_, d_skip, sz_l, ssd_norm_g)

    out_l = merge_branches((pool_l, mlstm_l, ssd_l), mg_l, w_branch, w_out)
    if not keep_ctx:
        return None, out_l
    pool_c = pool_mixer(pa_c, pool_w, pool_scale, False)
    mlstm_c = mlstm_out(h_cf + flip(h_cb), o_c, mlstm_norm_g)
    ssd_c = ssd_out(y_cf + flip(y_cb), xc_, d_skip, sz_c, ssd_norm_g)
    out_c = merge_branches((pool_c, mlstm_c, ssd_c), mg_c, w_branch, w_out)
    return out_c, out_l

def hier_moe(h, w_rg, b_rg, w_re, b_re, w_gate, w_up, w_down):
    b, l, d = h.shape
    n_tok = b * l
    t = h.reshape(n_tok, d)
    lg = (t @ w_rg).astype(F32) + b_rg.astype(F32)
    grp_p = jax.nn.softmax(lg, axis=-1)
    _, grp = lax.top_k(lg, 1)
    p_grp = jnp.take_along_axis(grp_p, grp, axis=-1)
    le = ((t @ w_re).astype(F32) + b_re.astype(F32)).reshape(n_tok, N_EXPERT_GROUPS, EXPERTS_PER_GROUP)
    le = jnp.take_along_axis(le, grp[:, :, None], axis=1)[:, 0]
    top_v, top_i = lax.top_k(le, TOP_K_IN_GROUP)
    weight = p_grp * jax.nn.softmax(top_v, axis=-1)
    expert = grp * EXPERTS_PER_GROUP + top_i

    n_asg = n_tok * TOP_K_IN_GROUP
    flat_e = expert.reshape(-1)
    flat_w = weight.reshape(-1)
    flat_tok = jnp.repeat(jnp.arange(n_tok, dtype=jnp.int32), TOP_K_IN_GROUP)
    order = jnp.argsort(flat_e)
    se = flat_e[order]
    counts = jnp.bincount(flat_e, length=N_EXPERTS)
    starts = jnp.cumsum(counts) - counts
    padded = (counts + MOE_BLOCK - 1) // MOE_BLOCK * MOE_BLOCK
    pends = jnp.cumsum(padded)
    pstarts = pends - padded
    dest = pstarts[se] + (jnp.arange(n_asg, dtype=jnp.int32) - starts[se])
    cap = -(-n_asg // MOE_BLOCK) * MOE_BLOCK + N_EXPERTS * MOE_BLOCK
    n_blocks = cap // MOE_BLOCK
    buf_tok = jnp.full((cap,), n_tok, jnp.int32).at[dest].set(flat_tok[order])
    buf_w = jnp.zeros((cap,), F32).at[dest].set(flat_w[order])
    block_expert = jnp.clip(jnp.searchsorted(pends, jnp.arange(n_blocks) * MOE_BLOCK, side='right'),
                            0, N_EXPERTS - 1)
    t_pad = jnp.concatenate([t, jnp.zeros((1, d), t.dtype)], axis=0)
    xb = t_pad[buf_tok].reshape(n_blocks, MOE_BLOCK, d)

    def expert_block(args):
        xblk, e = args
        a = jax.nn.silu(xblk @ w_gate[e]) * (xblk @ w_up[e])
        return a @ w_down[e]

    yb = lax.map(expert_block, (xb, block_expert)).reshape(cap, d)
    y = jax.ops.segment_sum(yb * buf_w[:, None].astype(yb.dtype), buf_tok, num_segments=n_tok + 1)[:n_tok]
    return y.reshape(b, l, d)

def setup_inputs(seed: int = 0) -> dict:
    key = jax.random.key(seed)
    ks = jax.random.split(key, 32)
    nrm = lambda k, shape, s: jax.random.normal(k, shape, F32) * s
    D = D_MODEL
    dt0 = jnp.exp(jax.random.uniform(ks[17], (DEPTH, 2, SSD_HEADS), F32, math.log(1e-3), math.log(1e-1)))
    return {
        'x': nrm(ks[0], (BATCH, SEQ, D), 1.0),
        'c': nrm(ks[1], (BATCH, D), 1.0),
        'ctx': nrm(ks[2], (BATCH, CTX_LEN, D), 1.0),
        'c_ctx': nrm(ks[3], (D,), 1.0),
        'w_ada': nrm(ks[4], (DEPTH, D, 6 * D), 0.5 * D ** -0.5),
        'b_ada': nrm(ks[5], (DEPTH, 6 * D), 0.02),
        'g_norm_mix': 1.0 + nrm(ks[6], (DEPTH, D), 0.05),
        'g_norm_ffn': 1.0 + nrm(ks[7], (DEPTH, D), 0.05),
        'w_in': nrm(ks[8], (DEPTH, D, D_IN), D ** -0.5),
        'pool_w': nrm(ks[9], (DEPTH, len(POOL_WINDOWS), POOL_GROUP, POOL_GROUP), POOL_GROUP ** -0.5),
        'pool_scale': 1.0 + nrm(ks[10], (DEPTH, D_POOL), 0.05),
        'mlstm_conv_w': nrm(ks[11], (DEPTH, QK_CONV, 2 * D_MLSTM), QK_CONV ** -0.5),
        'mlstm_conv_b': nrm(ks[12], (DEPTH, 2 * D_MLSTM), 0.02),
        'mlstm_gate_b': jnp.concatenate([nrm(ks[13], (DEPTH, 2, MLSTM_HEADS), 0.1),
                                         3.0 + 3.0 * jax.random.uniform(ks[14], (DEPTH, 2, MLSTM_HEADS), F32)],
                                        axis=1),
        'mlstm_norm_g': 1.0 + nrm(ks[15], (DEPTH, D_MLSTM), 0.05),
        'ssd_conv_w': nrm(ks[16], (DEPTH, SSD_CONV, D_XBC), SSD_CONV ** -0.5),
        'ssd_conv_b': nrm(ks[18], (DEPTH, D_XBC), 0.02),
        'ssd_dt_bias': dt0 + jnp.log(-jnp.expm1(-dt0)),
        'ssd_a_log': jnp.log(jax.random.uniform(ks[19], (DEPTH, 2, SSD_HEADS), F32, 1.0, 16.0)),
        'ssd_d': 1.0 + nrm(ks[20], (DEPTH, SSD_HEADS), 0.1),
        'ssd_norm_g': 1.0 + nrm(ks[21], (DEPTH, D_SSD), 0.05),
        'w_branch': nrm(ks[22], (DEPTH, N_BRANCH, D_BRANCH, D), D_BRANCH ** -0.5),
        'w_out': nrm(ks[23], (DEPTH, D, D), D ** -0.5),
        'w_route_group': nrm(ks[24], (DEPTH, D, N_EXPERT_GROUPS), D ** -0.5),
        'b_route_group': nrm(ks[25], (DEPTH, N_EXPERT_GROUPS), 0.01),
        'w_route_expert': nrm(ks[26], (DEPTH, D, N_EXPERTS), D ** -0.5),
        'b_route_expert': nrm(ks[27], (DEPTH, N_EXPERTS), 0.01),
        'w_exp_gate': nrm(ks[28], (DEPTH, N_EXPERTS, D, D_EXPERT), D ** -0.5),
        'w_exp_up': nrm(ks[29], (DEPTH, N_EXPERTS, D, D_EXPERT), D ** -0.5),
        'w_exp_down': nrm(ks[30], (DEPTH, N_EXPERTS, D_EXPERT, D), D_EXPERT ** -0.5),
        'g_final': 1.0 + nrm(ks[31], (D,), 0.05),
    }

def reference(x, c, ctx, c_ctx, w_ada, b_ada, g_norm_mix, g_norm_ffn, w_in, pool_w, pool_scale,
              mlstm_conv_w, mlstm_conv_b, mlstm_gate_b, mlstm_norm_g, ssd_conv_w, ssd_conv_b,
              ssd_dt_bias, ssd_a_log, ssd_d, ssd_norm_g, w_branch, w_out, w_route_group, b_route_group,
              w_route_expert, b_route_expert, w_exp_gate, w_exp_up, w_exp_down, g_final):
    silu_c = jax.nn.silu(c)
    silu_cc = jax.nn.silu(c_ctx)
    lc = ctx.shape[1]
    xl, xc = x, ctx
    for layer in range(DEPTH):
        keep_ctx = layer < DEPTH - 1
        mod_l = [m[:, None, :] for m in jnp.split(silu_c @ w_ada[layer] + b_ada[layer], 6, axis=-1)]
        mod_c = jnp.split(silu_cc @ w_ada[layer] + b_ada[layer], 6, axis=-1)
        hl = modulate(rmsnorm(xl, g_norm_mix[layer]), mod_l[0], mod_l[1])
        hc = modulate(rmsnorm(xc, g_norm_mix[layer]), mod_c[0], mod_c[1])
        oc, ol = token_mixer(hc, hl, keep_ctx, w_in[layer], pool_w[layer], pool_scale[layer],
                             mlstm_conv_w[layer], mlstm_conv_b[layer], mlstm_gate_b[layer], mlstm_norm_g[layer],
                             ssd_conv_w[layer], ssd_conv_b[layer], ssd_dt_bias[layer], ssd_a_log[layer],
                             ssd_d[layer], ssd_norm_g[layer], w_branch[layer], w_out[layer])
        xl = xl + mod_l[2] * ol
        hl = modulate(rmsnorm(xl, g_norm_ffn[layer]), mod_l[3], mod_l[4])
        moe_w = (w_route_group[layer], b_route_group[layer], w_route_expert[layer], b_route_expert[layer],
                 w_exp_gate[layer], w_exp_up[layer], w_exp_down[layer])
        if keep_ctx:
            xc = xc + mod_c[2] * oc
            hc = modulate(rmsnorm(xc, g_norm_ffn[layer]), mod_c[3], mod_c[4])
            y = hier_moe(jnp.concatenate([hc, hl], axis=1), *moe_w)
            xc = xc + mod_c[5] * y[:, :lc]
            xl = xl + mod_l[5] * y[:, lc:]
        else:
            xl = xl + mod_l[5] * hier_moe(hl, *moe_w)
    return rmsnorm(xl, g_final)


_drawn_inputs = setup_inputs


def setup_inputs(seed=0):
    import zlib

    import numpy as np

    out = dict(_drawn_inputs(seed))
    spreads = {}
    factors = {'ctx': 3.621,
     'g_norm_mix': 3.237,
     'g_norm_ffn': 2.751,
     'pool_scale': 6.315,
     'mlstm_conv_b': 64.0,
     'mlstm_norm_g': 6.936,
     'ssd_conv_b': 8.0,
     'ssd_d': 127.038,
     'ssd_norm_g': 5.844,
     'b_route_group': 8.0,
     'b_route_expert': 8.0,
     'c_ctx': 2.715}
    for name, (base, spread) in spreads.items():
        noise = np.random.default_rng([zlib.crc32(name.encode()), seed]).standard_normal(out[name].shape)
        drawn = base * np.exp(spread * noise) if base else spread * noise
        out[name] = jnp.asarray(drawn.astype(out[name].dtype))
    for name, factor in factors.items():
        out[name] = (out[name] * factor).astype(out[name].dtype)
    return out
```

```python
import concourse.bass as bass
from concourse import mybir
from contextlib import ExitStack

D = 1024
T = 512
TC = 256
P = 128
KT = D // P
GRID_W = 64
GRID_H = T // GRID_W
NC_CTX = TC // P
NC_LAT = T // P
NC_ALL = NC_CTX + NC_LAT
HEADS = 4
HD = D // HEADS
SH = 16
SP_ = D // SH
SG_ = 4
SN = 128
HPG = SH // SG_
NE = 32
DE = 512
EPS = 1e-6
BIG = 1e30

COL_POOL, COL_Q, COL_K, COL_V, COL_O, COL_GA = 0, 1024, 2048, 3072, 4096, 5120
COL_SX = COL_GA + 16
COL_SZ = COL_SX + D
COL_SB = COL_SZ + D
COL_SC = COL_SB + SG_ * SN
COL_SDT = COL_SC + SG_ * SN
COL_MG = COL_SDT + 2 * SH

CH = 4096
NW = 2
NHI = 4
NCIN = 3
NCINC = 2
BS = 96
SUBS = -(-T // BS)
MAXB = 2 * T // BS + NE
WIDE = 96
GST = 80
NB = 4


def build(nc, x, c, ctx_in, c_ctx, w_ada, b_ada, g_norm_mix, g_norm_ffn, w_in, pool_w, pool_scale,
          mlstm_conv_w, mlstm_conv_b, mlstm_gate_b, mlstm_norm_g, ssd_conv_w, ssd_conv_b,
          ssd_dt_bias, ssd_a_log, ssd_d, ssd_norm_g, w_branch, w_out, w_route_group, b_route_group,
          w_route_expert, b_route_expert, w_exp_gate, w_exp_up, w_exp_down, g_final, out, upto=99):
    f32 = mybir.dt.float32
    bf16 = mybir.dt.bfloat16
    ALU = mybir.AluOpType
    ACT = mybir.ActivationFunctionType
    AX = mybir.AxisListType

    def cols(w, c0):
        return w[0][:, c0:c0 + 512].rearrange("(k p) n -> p k n", p=P)

    chunks = [("ada", cols(w_ada, 512 * n)) for n in range(4)]
    for name, c0, n in (("k", COL_K, 2), ("q", COL_Q, 2), ("v", COL_V, 2), ("o", COL_O, 2)):
        chunks += [(name, cols(w_in, c0 + 512 * i)) for i in range(n)]

    def branch_chunks(b):
        got = [(f"mg{b}", cols(w_in, COL_MG + D * b + 512 * i)) for i in range(2)]
        return got + [(f"wb{b}", w_branch[0, b][:, 512 * i:512 * i + 512].rearrange("(k p) n -> p k n", p=P))
                      for i in range(2)]

    chunks += branch_chunks(1)
    for name, c0, n in (("B", COL_SB, 1), ("C", COL_SC, 1), ("x", COL_SX, 2), ("z", COL_SZ, 2)):
        chunks += [(name, cols(w_in, c0 + 512 * i)) for i in range(n)]
    chunks += branch_chunks(2)
    chunks += [("pa", cols(w_in, COL_POOL + 512 * i)) for i in range(2)]
    chunks += branch_chunks(0)
    chunks += [("ada", cols(w_ada, 512 * n)) for n in range(4, 12)]
    chunks += [("wo", cols(w_out, 512 * i)) for i in range(2)]
    first_chunk = {}
    for n, (name, _) in enumerate(chunks):
        first_chunk.setdefault(name, n)
    ADA2 = first_chunk["wb0"] + 2

    stages = [("xT", 8, "V"), ("xTc", 8, "V"), ("k", 16, "A"), ("q", 8, "A"), ("v", 12, "A"),
              ("S", 24, "A"), ("o", 8, "A"), ("hT", 8, "V"), ("mg1", 8, "A"), ("wb1", 8, "V"),
              ("B", 8, "A"), ("BTr", 8, "V"), ("C", 4, "A"), ("x", 16, "A"), ("xTr", 16, "V"),
              ("z", 8, "A"), ("yT", 8, "V"), ("mg2", 8, "A"), ("wb2", 8, "V"),
              ("pa", 8, "A"), ("pw", 8, "A"), ("mg0", 8, "A"), ("wb0", 8, "V"), ("wo", 8, "V"),
              ("xtok", 8, "V"), ("htok", 8, "A")]
    items = []
    for name, n, e in stages:
        if name in ("BTr", "xTr"):
            continue
        if name in ("B", "x"):
            tr = "BTr" if name == "B" else "xTr"
            m_of = n // 2
            for m in range(m_of + 2):
                if m < m_of:
                    items += [(name, 2 * m, e), (name, 2 * m + 1, e)]
                if m >= 2:
                    items += [(tr, 2 * (m - 2), "V"), (tr, 2 * (m - 2) + 1, "V")]
        else:
            items += [(name, i, e) for i in range(n)]
    place = {(name, i): g for g, (name, i, e) in enumerate(items)}
    reads = {"A": 0, "V": 0}
    read_no = []
    for name, i, e in items:
        reads[e] += 1
        read_no.append((e, reads[e]))

    per_chunk = {"k": 8, "q": 4, "v": 6, "o": 4, "mg0": 4, "mg1": 4, "mg2": 4, "wb0": 4, "wb1": 4,
                 "wb2": 4, "B": 8, "C": 4, "x": 8, "z": 4, "pa": 4, "wo": 4}
    release = []
    seen = {}
    for name, _ in chunks:
        seen[name] = seen.get(name, 0) + 1
        if name == "ada":
            release.append(("ada", seen[name]))
        else:
            release.append(("gemm", place[(name, per_chunk[name] * seen[name] - 1)] + 1))

    units = [(name, m) for name in ("k", "q", "o", "mg1", "wb1", "B", "C", "x", "mg2", "wb2", "pa", "mg0", "wb0", "wo")
             for m in range(4 if name in ("B", "C") else KT)]
    unit_no = {key: u for u, key in enumerate(units)}

    def unit_end(u):
        name, m = units[u]
        return place[(name, 2 * m + 1 if name in ("k", "B", "x") else m)] + 1

    conv = []
    for m in range(8):
        conv += [("k", m, 0), ("k", m, 1)]
    conv += [("q", m, 0) for m in range(8)]
    for m in range(4):
        conv += [("B", m, 0), ("B", m, 1)]
    conv += [("C", m, 0) for m in range(4)]
    for m in range(8):
        conv += [("x", m, 0), ("x", m, 1)]
    conv_no = {t: n for n, t in enumerate(conv)}
    kind_no = []
    cnt = [0, 0]
    for s, m, cx in conv:
        kind_no.append(cnt[cx])
        cnt[cx] += 1

    def conv_before(n, slots):
        cx, no = conv[n][2], kind_no[n]
        if no < slots[cx]:
            return 0
        want = no - slots[cx]
        return next(i for i in range(len(conv)) if conv[i][2] == cx and kind_no[i] == want) + 1

    es = ExitStack()
    with es:
        def sb(name, shape):
            return es.enter_context(nc.sbuf_tensor(name, shape, f32))

        def sem(name):
            return es.enter_context(nc.semaphore(name))

        vec = sb("vec", [P, 3, P])
        csil = sb("csil", [P, KT, WIDE])
        ada = sb("ada", [P, 48, 2])
        modA = sb("modA", [P, 2, KT])
        modF = sb("modF", [P, KT])
        ident = sb("ident", [P, P])
        ones = sb("ones", [P, P])
        triu = sb("triu", [P, P])
        tril = sb("tril", [P, P])
        hide_past = sb("hide_past", [P, P])
        hide_next = sb("hide_next", [P, P])
        sel_last = sb("sel_last", [P, P])
        sel_first = sb("sel_first", [P, P])
        eps = sb("eps", [P, 1])
        gate_b = sb("gate_b", [P, 16])
        dt_b = sb("dt_b", [P, 32])
        a_log = sb("a_log", [P, 32])
        d_skip = sb("d_skip", [P, SH])
        ig = sb("ig", [P, NC_ALL, 8])
        lf = sb("lf", [P, 2 * NC_ALL, 8])
        ftot = sb("ftot", [P, NC_ALL, 8])
        fcum = sb("fcum", [P, NC_ALL, 8])
        bkey = sb("bkey", [P, NC_ALL, 8])
        em = sb("em", [P, NC_LAT, 8])
        dt = sb("dt", [P, 2, NC_ALL, SH])
        dta = sb("dta", [P, 2, NC_ALL, SH])
        acs = sb("acs", [P, 2, NC_ALL, SH])
        tot = sb("tot", [P, 2, NC_ALL, SH])
        e_in = sb("e_in", [P, 2, NC_ALL, SH])
        coef = sb("coef", [P, 2, NC_ALL, SH])
        den = sb("den", [P, 2])
        ms = sb("ms", [P, 16])
        inv_cnt = sb("inv_cnt", [P, 4, GRID_W])

        R0 = 18432

        def halves(name, at, *dims):
            at_pad = nc.sbuf_tensor(f"before_{name}", [P, at], f32) if at else ExitStack()
            with at_pad, nc.sbuf_tensor(name, [P, *dims], mybir.dt.float32r) as t:
                return t[tuple([slice(None)] * (1 + len(dims)))]

        w_high_all = halves("w_high", CH * NW, NHI, KT, P)
        w_high = [w_high_all[:, s] for s in range(NHI)]
        ring_low = [halves(f"ring_low{s}", CH * s, KT, 512) for s in range(NW)]
        br1_low = [t[:, j, :] for t in (halves("br1_low_a", R0 + 4096, KT // 2, T), halves("br1_low_b", R0 + 10240, KT // 2, T))
                   for j in range(KT // 2)]
        hT_low = halves("hT_low", 12288, KT, T)
        hTc_low = halves("hTc_low", 16384, KT, TC)
        merged_low = halves("merged_low", 44904, KT, T)
        h_high0 = halves("h_high0", R0 + 10240, KT, T)
        hc_high0 = halves("hc_high0", R0 + 14336, KT, TC)
        h_high1 = halves("h_high1", R0, KT, T)
        br1_high = halves("br1_high", R0 + 6144, KT, T)
        h_high3 = halves("h_high3", R0 + 13312, KT, T)
        hc_high3 = halves("hc_high3", R0 + 24424, KT, TC)
        h_high2 = halves("h_high2", R0 + 20096, KT, T)
        br2_high = halves("br2_high", R0 + 8192, KT, T)
        br2_low = halves("br2_low", R0, KT, T)
        br0_low = halves("br0_low", R0, KT, T)
        br0_high = halves("br0_high", R0 + 8192, KT, T)
        merged_high = halves("merged_high", R0 + 20096, KT, T)
        arena = sb("arena", [P, 49000])

        def tiles(*at):
            each = KT // len(at)
            return [arena[:, a + T * j:a + T * j + T] for a in at for j in range(each)]

        def area(at, *dims):
            n = 1
            for d in dims:
                n *= d
            ap = arena[:, at:at + n]
            if len(dims) == 2:
                ap = ap.rearrange("p (a b) -> p a b", a=dims[0])
            if len(dims) == 3:
                ap = ap.rearrange("p (a b c) -> p a b c", a=dims[0], b=dims[1])
            return ap

        ring = [area(CH * s, KT, 512) for s in range(NW)]
        hT = area(12288, KT, T)
        hTc = area(16384, KT, TC)
        merged = area(44904, KT, T)
        xin = area(R0, NC_ALL, D)
        xT = area(R0 + 6144, KT, T)
        xTc = area(R0 + 10240, KT, TC)
        sq = area(R0 + 12288, KT, T)
        sqc = area(R0 + 16384, KT, TC)
        rn = area(R0 + 18432, T + TC)
        vec_rows = area(R0 + 19200, 3, P)
        w_small = area(R0 + 24000, KT, WIDE)
        kT = area(R0, KT, T + TC)
        qT = area(R0 + 6144, KT, T)
        hsum = area(R0 + 6144, HEADS, NC_LAT, HD)
        vone = area(R0 + 10240, NC_ALL, HEADS * (HD + 1))
        scores = area(R0 + 16408, NC_ALL, T)
        attn = [area(R0 + 19480 + 3072 * s, NC_ALL, T) for s in range(2)]
        mrow = [area(R0 + 25624 + 1024 * s, 2, T) for s in range(2)]
        diag = [area(R0 + 27672 + 512 * s, NC_LAT, P) for s in range(2)]
        cin_m = area(R0 + 16408, NCIN, 515)
        cinc_m = area(R0 + 17953, NCINC, 259)
        acc_m = area(R0 + 18472, 3, T)
        gx = area(R0 + 20100, 240)
        gabs = area(R0 + 20340, 240)
        gexp = area(R0 + 20580, 240)
        gu = area(R0 + 20820, 240)
        gl = area(R0 + 21060, 240)
        gd_ = area(R0 + 21300, 240)
        expa = area(R0 + 21540, 32)
        brow = area(R0 + 21600, 2, T + TC)
        mx = area(R0 + 23200, 2, T + TC)
        hcm = area(R0 + 24800, KT, T)
        zero_src = area(47400, D)
        sig_o = area(R0 + 21624, KT, T)
        br1 = tiles(R0 + 4096, R0 + 10240)
        gate1 = area(R0 + 17408, KT, T)
        xtok = area(R0, NC_ALL, D)
        BT = area(R0 + 6144, SG_, T)
        Btok = area(R0 + 8192, NC_ALL, SG_ * SN)
        CT = area(R0 + 11264, SG_, T)
        ytok = area(R0 + 13312, NC_LAT, D)
        cin_s = area(R0 + 17408, NCIN, 515)
        cinc_s = area(R0 + 18953, NCINC, 259)
        acc_s = area(R0 + 19472, 3, T)
        xst = area(R0 + 21008, 3, T + TC)
        rowa = area(R0 + 23400, 2, T)
        decay = [area(R0 + 17408 + 4096 * s, 2, SH, P) for s in range(2)]
        state = area(R0 + 17408, 2, D)
        xw = area(R0 + 19456, 2, D)
        ytmp = area(R0 + 21504, 2, D)
        ztok = area(R0 + 17408, 2, 512)
        junk = area(R0 + 18500, D)
        br2 = area(R0, KT, T)
        gate2 = area(R0 + 4096, KT, T)
        pooled = area(R0 + 8192, KT, T)
        pw_sb = area(R0 + 24200, 2, 4, 256)
        PR = GRID_W + 16
        ppad = area(R0 + 12288, 2, GRID_H * PR)
        psum_a = area(R0 + 13568, GRID_H * PR)
        psum_b = area(R0 + 14208, GRID_H * PR)
        br0 = area(R0, KT, T)
        gate0 = area(R0 + 4096, KT, T)
        xl = area(R0 + 15960, KT, T)
        prod2 = area(R0 + 14900, 2, T)

        slot6 = [area(CH * s, CH) for s in range(6)]
        sq2 = area(24576, KT, T)
        rn2 = area(28672, T)
        h2T = area(29184, KT, T)
        h2tok = area(33280, NC_LAT, D)
        onehot = arena[:, 37376:37376 + NC_LAT * BS // 2].bitcast(bf16).rearrange("p (i s) -> p i s", i=NC_LAT)
        xg = area(37568, KT, BS)
        aT = area(38336, DE // P, BS)
        sg = area(38720, DE // P * BS)
        rowid = area(39104, BS)
        y_sb = area(39200, D)
        w_route = area(33280, KT, WIDE)
        b_route = area(38492, 36)
        parts = [arena[:, at:at + 2048].bitcast(bf16).rearrange("p (i n) -> p i n", i=NC_LAT)
                 for at in (24576, 26624, 40544)]
        eq = [area(34816 + 384 * j, NC_LAT, BS) for j in range(2)]
        xltok = area(44904, NC_LAT, D)
        mod_out = area(32768, D)
        g_last = area(33792, D)
        TMP = 42600
        logit = area(TMP, NC_LAT, 36)
        gsc = area(TMP + 144, NC_LAT, 4)
        ghot = area(TMP + 160, NC_LAT, 4)
        gmax = area(TMP + 176, NC_LAT)
        pgrp = area(TMP + 180, NC_LAT)
        lsel = area(TMP + 184, NC_LAT, 8)
        hot = [area(TMP + 216 + 32 * j, NC_LAT, 8) for j in range(2)]
        top = [area(TMP + 280 + 4 * j, NC_LAT) for j in range(2)]
        wtok = [area(TMP + 288 + 4 * j, NC_LAT) for j in range(2)]
        etmp = area(TMP + 296, NC_LAT)
        rtmp = area(TMP + 300, NC_LAT, 8)
        rmax = area(TMP + 332, NC_LAT)
        rev = area(TMP + 336, 8)
        strict = area(TMP + 344, P)
        lmul = area(TMP + 472, NC_LAT * 4, 8)
        member = [area(TMP + 600 + 128 * j, NC_LAT, NE) for j in range(2)]
        both = area(TMP + 856, NC_LAT, NE)
        row = area(TMP + 984, NC_LAT, NE)
        posm = area(TMP + 1112, NE, NC_LAT)
        thr = area(TMP + 1240, NE, SUBS - 1)
        nblk = area(TMP + 1464, NE)
        cumx = area(TMP + 1496, NE + 1)
        idxf = area(TMP + 1530, 8)
        ptmp = area(TMP + 1540, NC_LAT, NE)
        mtot = area(TMP + 1668, NC_LAT, NE)
        yg = [area(24576 + 1024 * j, D) for j in range(8)]
        table = es.enter_context(nc.sbuf_tensor("table", [1, NE + 1], mybir.dt.int32))
        idx = es.enter_context(nc.sbuf_tensor("idx", [P, 8], mybir.dt.uint32))

        bank = [es.enter_context(nc.psum_tensor(f"bank{i}", [P, 512], f32)) for i in range(8)]

        x_scr = nc.dram_tensor("x_scr", [P, KT * T], f32, kind="Internal").ap()
        m_scr = nc.dram_tensor("m_scr", [HEADS, 2, T], f32, kind="Internal").ap()
        a_scr = nc.dram_tensor("a_scr", [2, SH, T], f32, kind="Internal").ap()

        y_scr = nc.dram_tensor("y_scr", [MAXB, BS, D], f32, kind="Internal").ap()
        mod_scr = nc.dram_tensor("mod_scr", [D], f32, kind="Internal").ap()
        sq2_ok, stat2, root2, normed2, h2_ok, route_in, route_mm = (
            sem("sq2_ok"), sem("stat2"), sem("root2"), sem("normed2"), sem("h2_ok"), sem("route_in"), sem("route_mm"))
        gexp_pre, gexp_ok, topexp_pre, topexp_ok, member_ok, pos_mm, table_ok, iota_ok, idx_ok = (
            sem("gexp_pre"), sem("gexp_ok"), sem("topexp_pre"), sem("topexp_ok"), sem("member_ok"), sem("pos_mm"),
            sem("table_ok"), sem("iota_ok"), sem("idx_ok"))
        expert_in = [sem(f"expert_in{s}") for s in range(6)]
        split_lo, split_mid = sem("split_lo"), sem("split_mid")
        eq_ok, row_ok = sem("eq_ok"), sem("row_ok")
        ada2_read, split_ok, split_hi, blocks_done, route_pad = (
            sem("ada2_read"), sem("split_ok"), sem("split_hi"), sem("blocks_done"), sem("route_pad"))
        hot_ok, gather_mm, xg_ok, gu_mm, sg_ok, a_ok, down_mm, y_lo, y_hi, y_out = (
            sem("hot_ok"), sem("gather_mm"), sem("xg_ok"), sem("gu_mm"), sem("sg_ok"), sem("a_ok"), sem("down_mm"),
            sem("y_lo"), sem("y_hi"), sem("y_out"))
        fin_ok_pre = sem("fin_ok_pre")
        mod_out_s, mod_in_s, yg_in, fsq, froot, fin_ok = (
            sem("mod_out_s"), sem("mod_in_s"), [sem(f"yg_in{j}") for j in range(4)], sem("fsq"), sem("froot"), sem("fin_ok"))

        chunk_in = [sem(f"chunk_in{s}") for s in range(NW)]
        vec_in, x_in, ctxin_in, small_in = sem("vec_in"), sem("x_in"), sem("ctxin_in"), sem("small_in")
        y_zero = sem("y_zero")
        consts, filled = sem("consts"), sem("filled")
        gemm_done = sem("gemm_done")
        act_read = sem("act_read")
        dve_read = sem("dve_read")
        ada_done, vec_tr, vec_sb, csil_ok = sem("ada_done"), sem("vec_tr"), sem("vec_sb"), sem("csil_ok")
        squares, stat_done, norm_root, normed, modA_ok, h_ok = (
            sem("squares"), sem("stat_done"), sem("norm_root"), sem("normed"), sem("modA_ok"), sem("h_ok"))
        x_spill = sem("x_spill")
        pads = sem("pads")
        gates_mm, gates_read, gates_pre, gates_exp, gates_u, gates_ln, lf_ok, bkey_ok = (
            sem("gates_mm"), sem("gates_read"), sem("gates_pre"), sem("gates_exp"), sem("gates_u"),
            sem("gates_ln"), sem("lf_ok"), sem("bkey_ok"))
        cum_mm, cum_read, tot_mm, tot_read = sem("cum_mm"), sem("cum_read"), sem("tot_mm"), sem("tot_read")
        brow_tr, brow_ok, mx_ok, mback_tr, em_sum, em_ok, m_out, m_bc = (
            sem("brow_tr"), sem("brow_ok"), sem("mx_ok"), sem("mback_tr"), sem("em_sum"), sem("em_ok"),
            sem("m_out"), [sem("m_bc0"), sem("m_bc1")])
        ssd_pre, ssd_exp, coef_ok = sem("ssd_pre"), sem("ssd_exp"), sem("coef_ok")
        conv_done, silu_done = sem("conv_done"), sem("silu_done")
        wexp, wmul, av_done, av_read, diag_ok = (
            sem("wexp"), sem("wmul"), sem("av_done"), sem("av_read"), sem("diag_ok"))
        hsq, hroot, hnorm = sem("hsq"), sem("hroot"), sem("hnorm")
        arow_tr, arow_ok, arow_out = sem("arow_tr"), sem("arow_ok"), sem("arow_out")
        dec_in = [sem("dec_in0"), sem("dec_in1")]
        dmask, dsub, dexp, dmul, g_mm, intra_mm, y_ok = (
            sem("dmask"), sem("dsub"), sem("dexp"), sem("dmul"), sem("g_mm"), sem("intra_mm"), sem("y_ok"))
        xw_ok, cs_mm, st_ok, inter_mm, inter_read, inter_add = (
            sem("xw_ok"), sem("cs_mm"), sem("st_ok"), sem("inter_mm"), sem("inter_read"), sem("inter_add"))
        yz_ok, ysq, yroot, ynorm = sem("yz_ok"), sem("ysq"), sem("yroot"), sem("ynorm")
        pool_ok, pw_in, gate_ok, prod_ok, ada2_ok, xl_in, xl_ok = (
            sem("pool_ok"), sem("pw_in"), sem("gate_ok"), sem("prod_ok"), sem("ada2_ok"), sem("xl_in"), sem("xl_ok"))
        w_hi, w_lo, op_hi, op_lo, h_back = sem("w_hi"), sem("w_lo"), sem("op_hi"), sem("op_lo"), sem("h_back")
        h_low, ones_col, h_moved, h_first = sem("h_low"), sem("ones_col"), sem("h_moved"), sem("h_first")
        vlink, alink, plink = sem("vlink"), sem("alink"), sem("plink")
        out_done = sem("out_done")

        block = es.enter_context(nc.Block())

        def freed(eng, g):
            if g >= NB:
                e, n = read_no[g - NB]
                eng.wait_ge(act_read if e == "A" else dve_read, n)

        def arrived(eng, n):
            eng.wait_ge(chunk_in[n % NW], 16 * (n // NW + 1))

        def linker(eng, s):
            count = [0]

            def link(ins):
                count[0] += 1
                ins.then_inc(s, 1)
                eng.wait_ge(s, count[0])
            return link

        def colmajor(ap):
            return ap.rearrange("p (r w) -> p w r", r=GRID_H)

        def bk(g):
            return bank[g % NB]

        def raw_tile(u, of=ring):
            name, m = units[u]
            return of[(first_chunk[name] + m // 4) % NW][:, :, P * (m % 4):P * (m % 4) + P]

        VEC_ROWS = [[(b_ada[0], 48), (c[0], 8), (c_ctx, 8), (g_norm_mix[0], 8), (g_norm_ffn[0], 8),
                     (pool_scale[0], 8), (mlstm_norm_g[0], 8), (ssd_norm_g[0], 8), (g_final, 8)],
                    [(mlstm_conv_w[0].rearrange("j n -> (j n)"), 64), (mlstm_conv_b[0], 16)],
                    [(ssd_conv_w[0].rearrange("j n -> (j n)"), 64), (ssd_conv_b[0], 16)]]
        n_rows = [sum(n for _, n in part) for part in VEC_ROWS]
        n_vec = sum(len(part) for part in VEC_ROWS)
        V_BADA, V_C, V_GMIX, V_GFFN, V_PS, V_MG, V_SG, V_GF = 0, 48, 64, 72, 80, 88, 96, 104

        @block.sync
        def _(sp):
            for part, rows in enumerate(VEC_ROWS):
                at = 0
                for v, n in rows:
                    sp.dma_start(vec_rows[at:at + n, part, :], v.rearrange("(j p) -> j p", p=P)).then_inc(vec_in, 16)
                    at += n
            sp.dma_start(xin[:, NC_CTX:, :], x[0].rearrange("(t p) n -> p t n", p=P)).then_inc(x_in, 16)
            sp.dma_start(xin[:, 0:NC_CTX, :], ctx_in[0].rearrange("(t p) n -> p t n", p=P)).then_inc(ctxin_in, 16)
            for n, (name, src) in enumerate(chunks):
                if n >= NW:
                    kind, v = release[n - NW]
                    sp.wait_ge(ada_done if kind == "ada" else gemm_done, v)
                sp.dma_start(ring[n % NW], src).then_inc(chunk_in[n % NW], 16)
            if upto < 7:
                return

            def expert_loads(e, par):
                return [(3 * (1 - par) + j, src, kk) for j, (src, kk) in enumerate(
                    ((w_exp_gate[0][e], KT), (w_exp_up[0][e], KT), (w_exp_down[0][e], DE // P)))]

            sp.wait_ge(dve_read, read_no[place[("wb0", 7)]][1])
            for s, src, kk in expert_loads(0, 0):
                sp.dma_start(slot6[s].rearrange("p (k n) -> p k n", k=kk), src.rearrange("(k p) n -> p k n", p=P)
                             ).then_inc(expert_in[s], 16)
            sp.wait_ge(gemm_done, place[("wo", 7)] + 1)
            for s, src, kk in expert_loads(1, 1):
                sp.dma_start(slot6[s].rearrange("p (k n) -> p k n", k=kk), src.rearrange("(k p) n -> p k n", p=P)
                             ).then_inc(expert_in[s], 16)
            sp.wait_ge(table_ok, 1)
            with sp.Fori(1, NE // 2, 1) as ep:
                for par in range(2):
                    before = sp.value_load(table[0:1, bass.ds(2 * ep + (par - 1), 1)], min_val=0, max_val=MAXB)
                    for j, (s, src, kk) in enumerate(expert_loads(2 * ep + par, par)):
                        sp.wait_ge(down_mm if j == 2 else gu_mm, before)
                        sp.dma_start(slot6[s].rearrange("p (k n) -> p k n", k=kk), src.rearrange("(k p) n -> p k n", p=P)
                                     ).then_inc(expert_in[s], 16)

        @block.gpsimd
        def _(pool):
            link = linker(pool, plink)
            g = nc.gpsimd

            def low_weights(name, lo, hi):
                for m in range(lo, hi):
                    u = unit_no[(name, m)]
                    pool.wait_ge(w_hi, u + 1)
                    g.tensor_tensor(raw_tile(u, ring_low), raw_tile(u), w_high[u % NHI].bitcast(f32), ALU.subtract).then_inc(w_lo, 1)

            def low_operand(n, whole, low, high):
                for m in range(KT):
                    pool.wait_ge(op_hi, 8 * n + m + 1)
                    whole_m, low_m = (ap[m] if isinstance(ap, list) else ap[:, m, :] for ap in (whole, low))
                    g.tensor_tensor(low_m, whole_m, high[:, m, :].bitcast(f32), ALU.subtract).then_inc(op_lo, 1)
            link(g.memset(w_small, 0.0))
            g.memset(csil[:, :, :], 0.0).then_inc(filled, 1)
            g.memset(lf[:, :, :], 0.0).then_inc(filled, 1)
            pool.dma_start(w_small[:, :, 0:16],
                           w_in[0][:, COL_GA:COL_GA + 16].rearrange("(k p) n -> p k n", p=P)).then_inc(small_in, 16)
            pool.dma_start(w_small[:, :, 16:48],
                           w_in[0][:, COL_SDT:COL_SDT + 32].rearrange("(k p) n -> p k n", p=P)).then_inc(small_in, 16)
            pool.dma_start(gate_b[:, :], mlstm_gate_b[0].rearrange("a h -> (a h)").partition_broadcast(P)).then_inc(small_in, 16)
            pool.dma_start(dt_b[:, :], ssd_dt_bias[0].rearrange("a h -> (a h)").partition_broadcast(P)).then_inc(small_in, 16)
            pool.dma_start(a_log[:, :], ssd_a_log[0].rearrange("a h -> (a h)").partition_broadcast(P)).then_inc(small_in, 16)
            pool.dma_start(d_skip[:, :], ssd_d[0].partition_broadcast(P)).then_inc(small_in, 16)
            g.memset(ident[:, :], 0.0).then_inc(filled, 1)
            g.memset(ones[:, :], 1.0).then_inc(filled, 1)
            g.memset(hide_past[:, :], 0.0).then_inc(filled, 1)
            g.memset(hide_next[:, :], 0.0).then_inc(filled, 1)
            pool.wait_ge(filled, 6)

            def sel(dst, src, op, fill, base, step, mul):
                g.affine_select(out=dst[:, :], in_=src[:, :], compare_op=op, fill=fill, base=base,
                                pattern=[[step, P]], channel_multiplier=mul).then_inc(consts, 1)
            sel(ident, ident, ALU.not_equal, 1.0, 0, -1, 1)
            sel(triu, ones, ALU.is_ge, 0.0, 0, 1, -1)
            sel(tril, ones, ALU.is_ge, 0.0, 0, -1, 1)
            sel(hide_past, hide_past, ALU.is_ge, BIG, 0, 1, -1)
            sel(hide_next, hide_next, ALU.is_ge, BIG, 0, -1, 1)
            sel(sel_last, ones, ALU.is_equal, 0.0, -(P - 1), 0, 1)
            sel(sel_first, ones, ALU.is_equal, 0.0, 0, 0, 1)
            g.memset(eps[:, :], EPS).then_inc(consts, 1)
            link(g.memset(zero_src, 0.0))
            for j in range(NE, MAXB):
                pool.dma_start(y_scr[j], zero_src[0:BS, :]).then_inc(y_zero, 16)
            for gi, w in enumerate((2, 4, 8, 16)):
                link(g.memset(inv_cnt[:, gi, :], 1.0 / w))
                for t in list(range(w // 2)) + list(range(GRID_W - w // 2 + 1, GRID_W)):
                    lo, hi = max(t - w // 2, 0), min(t - w // 2 + w - 1, GRID_W - 1)
                    g.memset(inv_cnt[:, gi, t:t + 1], 1.0 / (hi - lo + 1))
            pool.wait_ge(y_zero, 16 * (MAXB - NE))
            pool.wait_ge(dve_read, 8)
            pool.dma_start(x_scr, area(R0 + 6144, KT * T)).then_inc(x_spill, 16)
            pool.wait_ge(x_spill, 16)
            pool.wait_ge(h_ok, 24)
            g.memset(cin_m[:, :, 0:2], 0.0).then_inc(pads, 1)
            g.memset(cin_m[:, :, 514:515], 0.0).then_inc(pads, 1)
            g.memset(cinc_m[:, :, 0:2], 0.0).then_inc(pads, 1)
            g.memset(cinc_m[:, :, 258:259], 0.0).then_inc(pads, 1)
            low_weights("k", 0, 8)
            low_weights("q", 0, 8)
            pool.wait_ge(h_back, 1)
            g.memset(vone.rearrange("p c (h e) -> p (c h) e", h=HEADS)[:, :, HD:HD + 1], 1.0).then_inc(ones_col, 1)
            pool.wait_ge(mx_ok, 1)
            pool.dma_start(m_scr, mx[0:HEADS, :, TC:]).then_inc(m_out, 16)
            pool.wait_ge(m_out, 16)
            if upto >= 2:
                pool.wait_ge(gemm_done, place[("v", 11)] + 1)
                for h in range(HEADS):
                    if h >= 2:
                        pool.wait_ge(wexp, 12 * (h - 1))
                        pool.wait_ge(diag_ok, 2 * (h - 1))
                    pool.dma_start(mrow[h % 2], m_scr[h].partition_broadcast(P)).then_inc(m_bc[h % 2], 16)
                    pool.wait_ge(m_bc[h % 2], 16 * (h // 2 + 1))
                    for d in range(2):
                        u = 2 * h + d
                        if u >= 2:
                            pool.wait_ge(wexp, 6 * (u - 1))
                        mask = (hide_past, hide_next)[d]
                        g.tensor_tensor(diag[d], mrow[h % 2][:, d, :].rearrange("p (i t) -> p i t", i=NC_LAT),
                                        mask[:, None, :].to_broadcast([P, NC_LAT, P]), ALU.add).then_inc(diag_ok, 1)
            if upto >= 3:
                low_operand(0, hT, hT_low, h_high1)
                low_weights("o", 0, 8)
                low_weights("mg1", 0, 4)
                low_operand(1, br1, br1_low, br1_high)
                low_weights("mg1", 4, 8)
                low_weights("wb1", 0, 8)
                low_weights("B", 0, 3)
            if upto >= 4:
                pool.wait_ge(dve_read, read_no[place[("wb1", 7)]][1])
                g.memset(cin_s[:, :, 0:2], 0.0).then_inc(pads, 1)
                g.memset(cin_s[:, :, 514:515], 0.0).then_inc(pads, 1)
                g.memset(cinc_s[:, :, 0:2], 0.0).then_inc(pads, 1)
                g.memset(cinc_s[:, :, 258:259], 0.0).then_inc(pads, 1)
                low_weights("B", 3, 4)
                low_weights("C", 0, 4)
                pool.wait_ge(arow_ok, 2)
                pool.dma_start(a_scr.rearrange("d h t -> h d t"), rowa[0:SH, :, :]).then_inc(arow_out, 16)
                pool.wait_ge(arow_out, 16)
                low_weights("x", 0, 8)
                for i in range(NC_LAT):
                    if i == 0:
                        pool.wait_ge(dve_read, read_no[place[("xTr", 15)]][1])
                    if i >= 2:
                        pool.wait_ge(intra_mm, i - 1)
                    pool.dma_start(decay[i % 2].rearrange("p d h t -> p (d h) t"),
                                   a_scr.rearrange("d h t -> (d h) t")[:, i * P:i * P + P].partition_broadcast(P)
                                   ).then_inc(dec_in[i % 2], 16)
                    pool.wait_ge(dec_in[i % 2], 16 * (i // 2 + 1))
                    for d in range(2):
                        mask = (hide_past, hide_next)[d]
                        g.tensor_tensor(decay[i % 2][:, d], decay[i % 2][:, d], mask[:, None, :].to_broadcast([P, SH, P]),
                                        ALU.subtract).then_inc(dmask, 1)
                pool.wait_ge(intra_mm, 4)
                for n in range(10):
                    d, step = n % 2, n // 2
                    cc = ([0, 1, 2, 3, 4], [1, 0, 5, 4, 3])[d][step]
                    if n >= 2:
                        pool.wait_ge(cs_mm, n - 1)
                    g.tensor_tensor(xw[:, d].rearrange("p (h e) -> p h e", h=SH),
                                    xtok[:, cc, :].rearrange("p (h e) -> p h e", h=SH),
                                    coef[:, d, cc, :, None].to_broadcast([P, SH, SP_]), ALU.mult).then_inc(xw_ok, 1)
            if upto >= 5:
                low_operand(2, hT, hT_low, h_high2)
                low_weights("mg2", 0, 4)
                low_operand(3, br2, br2_low, br2_high)
                low_weights("mg2", 4, 8)
                low_weights("wb2", 0, 8)
                low_weights("pa", 0, 4)
            if upto >= 6:
                pool.wait_ge(prod_ok, 8)
                g.memset(area(R0 + 12288, 2 * GRID_H * PR), 0.0).then_inc(pads, 1)
                for j in range(2):
                    pool.dma_start(pw_sb[:, j], pool_w[0][:, P * j:P * j + P, :].rearrange("g p n -> p g n")
                                   ).then_inc(pw_in, 16)
                pool.dma_start(xl, x_scr.rearrange("p (k t) -> p k t", k=KT)).then_inc(xl_in, 16)
                low_weights("pa", 4, 8)
                low_weights("mg0", 0, 4)
                low_operand(4, br0, br0_low, br0_high)
                low_weights("mg0", 4, 8)
                low_weights("wb0", 0, 8)
                low_operand(5, merged, merged_low, merged_high)
            if upto >= 7:
                pool.wait_ge(prod_ok, 16)
                g.memset(w_route, 0.0).then_inc(route_pad, 1)
                pool.wait_ge(route_pad, 1)
                pool.dma_start(w_route[:, :, 0:4], w_route_group[0].rearrange("(k p) n -> p k n", p=P)).then_inc(route_in, 16)
                pool.dma_start(w_route[:, :, 4:36], w_route_expert[0].rearrange("(k p) n -> p k n", p=P)).then_inc(route_in, 16)
                pool.dma_start(b_route[:, 0:4], b_route_group[0].partition_broadcast(P)).then_inc(route_in, 16)
                pool.dma_start(b_route[:, 4:36], b_route_expert[0].partition_broadcast(P)).then_inc(route_in, 16)
                low_weights("wo", 0, 8)
                pool.wait_ge(dve_read, read_no[place[("wo", 7)]][1])
                g.iota(rowid, pattern=[[1, BS]], base=0, channel_multiplier=0,
                       allow_small_or_imprecise_dtypes=True).then_inc(iota_ok, 1)
                pool.wait_ge(ada2_ok, 1)
                pool.dma_start(mod_scr.rearrange("(k p) -> p k", p=P), ada[:, 40:48, 0], allow_slow_non_contiguous=True).then_inc(mod_out_s, 16)
                pool.wait_ge(mod_out_s, 16)
                pool.wait_ge(split_ok, 8)
                pool.dma_start(mod_out, mod_scr.partition_broadcast(P)).then_inc(mod_in_s, 16)
                pool.dma_start(g_last, g_final.partition_broadcast(P)).then_inc(mod_in_s, 16)
                pool.wait_ge(blocks_done, 1)
                pool.wait_ge(idx_ok, 1)
                for i in range(NC_LAT):
                    for j in range(2):
                        g.indirect_dma_start(out=yg[2 * i + j], out_offset=None, in_=y_scr.rearrange("b s d -> (b s) d"),
                                             in_offset=bass.IndirectOffsetOnAxis(ap=idx[:, 2 * i + j:2 * i + j + 1], axis=0),
                                             bounds_check=MAXB * BS - 1).then_inc(yg_in[i], 16)
                for i in range(NC_LAT):
                    pool.wait_ge(fin_ok, i + 1)
                    pool.dma_start(out[0][P * i:P * i + P, :], yg[2 * i]).then_inc(out_done, 16)
                pool.wait_ge(out_done, 16 * NC_LAT)

        @block.tensor
        def _(pe):
            mm, tr = nc.tensor.matmul, nc.tensor.transpose

            def last_of(ins, s):
                ins.then_inc(s, 1)

            pe.wait_ge(consts, 8)
            pe.wait_ge(vec_in, 16 * n_vec)
            for part in range(3):
                ins = tr(bank[7][:, P * part:P * part + n_rows[part]], vec_rows[0:n_rows[part], part, :],
                         ident[0:n_rows[part], 0:n_rows[part]])
            last_of(ins, vec_tr)
            pe.wait_ge(x_in, 16)
            for m in range(KT):
                gi = place[("xT", m)]
                freed(pe, gi)
                for i in range(NC_LAT):
                    ins = tr(bk(gi)[:, P * i:P * i + P], xin[:, NC_CTX + i, P * m:P * m + P], ident[:, :])
                last_of(ins, gemm_done)
            pe.wait_ge(ctxin_in, 16)
            for m in range(KT):
                gi = place[("xTc", m)]
                freed(pe, gi)
                for i in range(NC_CTX):
                    ins = tr(bk(gi)[:, P * i:P * i + P], xin[:, i, P * m:P * m + P], ident[:, :])
                last_of(ins, gemm_done)
            pe.wait_ge(squares, 16)
            for m in range(KT):
                ins = mm(bank[5][:, :], ones[:, :], sq[:, m, :], start=m == 0, stop=m == KT - 1)
            last_of(ins, stat_done)
            for m in range(KT):
                ins = mm(bank[6][:, 0:TC], ones[:, :], sqc[:, m, :], start=m == 0, stop=m == KT - 1)
            last_of(ins, stat_done)
            def modulation(n, chunk):
                arrived(pe, chunk)
                for j in range(4):
                    for k in range(KT):
                        ins = mm(bank[4 + n % 4][:, WIDE * j:WIDE * j + WIDE], ring[chunk % NW][:, k, P * j:P * j + P],
                                 csil[:, k, :], start=k == 0, stop=k == KT - 1)
                last_of(ins, ada_done)

            pe.wait_ge(csil_ok, 1)
            pe.wait_ge(norm_root, 2)
            for n in range(4):
                modulation(n, n)
            pe.wait_ge(h_ok, 24)
            pe.wait_ge(small_in, 16 * 6)
            for cc in range(NC_ALL):
                for part, b in enumerate((5, 6)):
                    for k in range(KT):
                        if cc < NC_CTX:
                            tok = hTc[:, k, P * cc:P * cc + P]
                        elif part == 0:
                            tok = hcm[:, k, P * (cc - 2):P * (cc - 2) + P]
                        else:
                            tok = hT[:, k, P * (cc - 2):P * (cc - 2) + P]
                        ins = mm(bank[b][:, GST * cc:GST * cc + WIDE], tok, w_small[:, k, :],
                                 start=k == 0, stop=k == KT - 1)
            last_of(ins, gates_mm)

            def tile_w3(name, m, high, low, idx=None, n_tok=T, ready=None):
                u, gi = unit_no[(name, m)], place[(name, m if idx is None else idx)]
                pe.wait_ge(w_lo, u + 1)
                freed(pe, gi)
                w_h, w_l = w_high[u % NHI], raw_tile(u, ring_low)
                for k in range(KT):
                    if ready:
                        pe.wait_ge(h_low, ready + k + 1)
                    for j, (a, b) in enumerate(((w_h, high), (w_h, low), (w_l, high))):
                        b = b[k] if isinstance(b, list) else b[:, k, :]
                        ins = mm(bk(gi)[:, 0:n_tok], a[:, k, :], b,
                                 start=k + j == 0, stop=(k, j) == (KT - 1, 2))
                last_of(ins, gemm_done)

            pe.wait_ge(h_low, 2)
            for m in range(KT):
                tile_w3("k", m, h_high0, hT_low, 2 * m)
                tile_w3("k", m, hc_high0, hTc_low, 2 * m + 1, TC)
            pe.wait_ge(lf_ok, 2)
            for j, w in enumerate((triu, tril, ones)):
                ins = mm(bank[4][:, WIDE * j:WIDE * j + WIDE], w[:, :], lf[:, :, :].rearrange("p c h -> p (c h)"),
                         start=True, stop=True)
            for d in range(2):
                ins = mm(bank[7][:, 96 * d:96 * d + 96], (triu, tril)[d][:, :], dta[:, d].rearrange("p c h -> p (c h)"),
                         start=True, stop=True)
            last_of(ins, cum_mm)
            for m in range(KT):
                tile_w3("q", m, h_high0, hT_low)
                if m == 1:
                    pe.wait_ge(cum_read, 1)
                    for d in range(2):
                        ins = mm(bank[7][:, 192 + 96 * d:288 + 96 * d], (sel_last, sel_first)[d][:, :],
                                 acs[:, d].rearrange("p c h -> p (c h)"), start=True, stop=True)
                    last_of(ins, tot_mm)
                    pe.wait_ge(bkey_ok, 1)
                    for d in range(2):
                        for cc in range(NC_ALL):
                            to = (bank[4][0:HEADS, 256 * d + P * cc:256 * d + P * cc + P] if cc < NC_CTX else
                                  bank[5 + d][0:HEADS, P * (cc - 2):P * (cc - 2) + P])
                            if cc < NC_CTX:
                                to = bank[4][0:HEADS, P * (2 * d + cc):P * (2 * d + cc) + P]
                            ins = tr(to, bkey[:, cc, 4 * d:4 * d + 4], ident[:, :])
                    last_of(ins, brow_tr)
            for m in range(12):
                half, cc = m // NC_ALL, (m + NC_CTX) % NC_ALL
                n = first_chunk["v"] + half
                gi = place[("v", m)]
                arrived(pe, n)
                freed(pe, gi)
                if m == NC_LAT:
                    pe.wait_ge(h_back, 1)
                for k in range(KT):
                    tok = (hTc[:, k, P * cc:P * cc + P] if cc < NC_CTX else
                           hcm[:, k, P * (cc - 2):P * (cc - 2) + P])
                    ins = mm(bk(gi)[:, :], tok, ring[n % NW][:, k, :], start=k == 0, stop=k == KT - 1)
                last_of(ins, gemm_done)
                if m == 5:
                    pe.wait_ge(mx_ok, 1)
                    for i in range(NC_LAT):
                        for d in range(2):
                            ins = tr(bank[5][:, 8 * i + 4 * d:8 * i + 4 * d + 4],
                                     mx[0:HEADS, d, TC + P * i:TC + P * i + P], ident[0:HEADS, 0:HEADS])
                    last_of(ins, mback_tr)

            def score(h):
                for cc in range(NC_ALL):
                    gi = place[("S", NC_ALL * h + cc)]
                    freed(pe, gi)
                    if cc == 0:
                        pe.wait_ge(silu_done, 24 if h >= 0 else 0)
                    for j in range(2):
                        ins = mm(bk(gi)[:, :], kT[:, 2 * h + j, P * cc:P * cc + P], qT[:, 2 * h + j, :],
                                 start=j == 0, stop=j == 1)
                    last_of(ins, gemm_done)

            def weigh(h, d):
                u = 2 * h + d
                pe.wait_ge(wmul, 6 * (u + 1))
                for i in range(NC_LAT):
                    n = NC_LAT * u + i
                    keys = [0, 1] + (list(range(2, 2 + i + 1)) if d == 0 else list(range(2 + i, NC_ALL)))
                    if n >= 3:
                        pe.wait_ge(av_read, n - 2)
                    for j, cc in enumerate(keys):
                        ins = mm(bank[(4, 6, 7)[n % 3]][:, 0:HD + 1], attn[u % 2][:, cc, P * i:P * i + P],
                                 vone[:, cc, (HD + 1) * h:(HD + 1) * (h + 1)], start=j == 0, stop=j == len(keys) - 1)
                    last_of(ins, av_done)

            if upto >= 2:
                pe.wait_ge(act_read, read_no[place[("v", 11)]][1])
                pe.wait_ge(ones_col, 1)
                score(0)
                for h in range(HEADS):
                    weigh(h, 0)
                    if h + 1 < HEADS:
                        score(h + 1)
                    weigh(h, 1)

            if upto >= 3:
                pe.wait_ge(op_lo, 8)
                for m in range(KT):
                    tile_w3("o", m, h_high1, hT_low)
                for m in range(KT):
                    if m % 2 == 0:
                        pe.wait_ge(hnorm, m // 2 + 1)
                    gi = place[("hT", m)]
                    freed(pe, gi)
                    for i in range(NC_LAT):
                        ins = tr(bk(gi)[:, P * i:P * i + P], hsum[:, m // 2, i, P * (m % 2):P * (m % 2) + P], ident[:, :])
                    last_of(ins, gemm_done)
                for m in range(KT):
                    tile_w3("mg1", m, h_high1, hT_low)
                pe.wait_ge(op_lo, 16)
                for m in range(KT):
                    tile_w3("wb1", m, br1_high, br1_low)

            if upto >= 4:
                def token_major(name, m):
                    t0 = conv_no[(name, m, 0)]
                    pe.wait_ge(silu_done, t0 + 2)
                    for j in range(2):
                        gi = place[(name + "Tr", 2 * m + j)]
                        freed(pe, gi)
                        for i in range((NC_LAT, NC_CTX)[j]):
                            at = (TC + P * i) if j == 0 else P * i
                            ins = tr(bk(gi)[:, P * i:P * i + P], xst[:, m % 3, at:at + P], ident[:, :])
                        last_of(ins, gemm_done)

                pe.wait_ge(h_moved, 2)
                for m in range(4 + 2):
                    if m < 4:
                        tile_w3("B", m, h_high3, hT_low, 2 * m)
                        tile_w3("B", m, hc_high3, hTc_low, 2 * m + 1, TC)
                    if m >= 2:
                        token_major("B", m - 2)
                for m in range(4):
                    tile_w3("C", m, h_high3, hT_low)
                for d in range(2):
                    for i in range(NC_LAT):
                        ins = tr(bank[4 + d][0:SH, P * i:P * i + P], acs[:, d, NC_CTX + i, :], ident[:, :])
                last_of(ins, arow_tr)
                for m in range(8 + 2):
                    if m < 8:
                        tile_w3("x", m, h_high3, hT_low, 2 * m)
                        tile_w3("x", m, hc_high3, hTc_low, 2 * m + 1, TC)
                    if m >= 2:
                        token_major("x", m - 2)
                pe.wait_ge(dve_read, read_no[place[("xTr", 15)]][1])
                pe.wait_ge(silu_done, len(conv))
                pe.wait_ge(arow_ok, 2)
                for i in range(NC_LAT):
                    if i >= 2:
                        pe.wait_ge(dmul, i - 1)
                    for gq in range(SG_):
                        ins = mm(bank[4 + i % 2][:, P * gq:P * gq + P], BT[:, gq, P * i:P * i + P],
                                 CT[:, gq, P * i:P * i + P], start=True, stop=True)
                    last_of(ins, g_mm)
                    pe.wait_ge(dmul, i + 1)
                    if i >= 1:
                        pe.wait_ge(y_ok, i)
                    for h in reversed(range(SH)):
                        lo = 0 if h % 8 == 0 else WIDE - SP_
                        ins = mm(bank[6 + h // 8][:, SP_ * (h % 8) - lo:SP_ * (h % 8) + SP_], decay[i % 2][:, 0, h, :],
                                 xtok[:, NC_CTX + i, SP_ * h - lo:SP_ * h + SP_], start=True, stop=True)
                    last_of(ins, intra_mm)
                pe.wait_ge(y_ok, 4)
                n_inter = 0
                for n in range(10):
                    d, step = n % 2, n // 2
                    cc = ([0, 1, 2, 3, 4], [1, 0, 5, 4, 3])[d][step]
                    if step >= 2:
                        cq = (step - 2, 3 - (step - 2))[d]
                        pe.wait_ge(st_ok, n - 1)
                        if n_inter >= 1:
                            pe.wait_ge(inter_read, n_inter)
                        for gq in range(SG_):
                            ins = mm(bank[6 + gq // 2][:, 256 * (gq % 2):256 * (gq % 2) + 256], CT[:, gq, P * cq:P * cq + P],
                                     state[:, d, 256 * gq:256 * gq + 256], start=True, stop=True)
                        last_of(ins, inter_mm)
                        n_inter += 1
                    pe.wait_ge(xw_ok, n + 1)
                    if n >= 1:
                        pe.wait_ge(st_ok, n)
                    for gq in range(SG_):
                        ins = mm(bank[4 + gq // 2][:, 256 * (gq % 2):256 * (gq % 2) + 256], Btok[:, cc, SN * gq:SN * gq + SN],
                                 xw[:, d, 256 * gq:256 * gq + 256], start=True, stop=True)
                    last_of(ins, cs_mm)
                for d in range(2):
                    cq = (3, 0)[d]
                    pe.wait_ge(st_ok, 9 + d)
                    pe.wait_ge(inter_read, n_inter)
                    for gq in range(SG_):
                        ins = mm(bank[6 + gq // 2][:, 256 * (gq % 2):256 * (gq % 2) + 256], CT[:, gq, P * cq:P * cq + P],
                                 state[:, d, 256 * gq:256 * gq + 256], start=True, stop=True)
                    last_of(ins, inter_mm)
                    n_inter += 1

            if upto >= 5:
                for m in range(8):
                    i, half = m % 4, m // 4
                    n = first_chunk["z"] + half
                    gi = place[("z", m)]
                    pe.wait_ge(h_back, 2)
                    arrived(pe, n)
                    freed(pe, gi)
                    for k in range(KT):
                        ins = mm(bk(gi)[:, :], hT[:, k, P * i:P * i + P], ring[n % NW][:, k, :], start=k == 0, stop=k == KT - 1)
                    last_of(ins, gemm_done)
                pe.wait_ge(ynorm, 4)
                for m in range(KT):
                    gi = place[("yT", m)]
                    freed(pe, gi)
                    for i in range(NC_LAT):
                        ins = tr(bk(gi)[:, P * i:P * i + P], ytok[:, i, P * m:P * m + P], ident[:, :])
                    last_of(ins, gemm_done)
                pe.wait_ge(op_lo, 24)
                for m in range(KT):
                    tile_w3("mg2", m, h_high2, hT_low)
                pe.wait_ge(op_lo, 32)
                for m in range(KT):
                    tile_w3("wb2", m, br2_high, br2_low)

            if upto >= 6:
                for m in range(KT):
                    tile_w3("pa", m, h_high2, hT_low)
                pe.wait_ge(pw_in, 32)
                for m in range(KT):
                    gi = place[("pw", m)]
                    freed(pe, gi)
                    pe.wait_ge(pool_ok, 2 * (m // 2) + 2)
                    for j in range(2):
                        ins = mm(bk(gi)[:, :], pw_sb[:, j, m // 2, P * (m % 2):P * (m % 2) + P],
                                 pooled[:, 2 * (m // 2) + j, :], start=j == 0, stop=j == 1)
                    last_of(ins, gemm_done)
                for m in range(KT):
                    tile_w3("mg0", m, h_high2, hT_low)
                pe.wait_ge(op_lo, 40)
                for m in range(KT):
                    tile_w3("wb0", m, br0_high, br0_low)
                for n in range(8):
                    if n >= 4:
                        pe.wait_ge(ada2_read, n - 3)
                    modulation(n, ADA2 + n)
                pe.wait_ge(op_lo, 48)
                for m in range(KT):
                    tile_w3("wo", m, merged_high, merged_low)
            if upto >= 7:
                pe.wait_ge(dve_read, read_no[place[("wo", 7)]][1])
                for q in range(8):
                    i, half = q // 2, q % 2
                    gi = place[("xtok", q)]
                    freed(pe, gi)
                    for m in range(4):
                        ins = tr(bk(gi)[:, P * m:P * m + P], xl[:, 4 * half + m, P * i:P * i + P], ident[:, :])
                    last_of(ins, gemm_done)
                pe.wait_ge(sq2_ok, 8)
                for m in range(KT):
                    ins = mm(bank[5][:, :], ones[:, :], sq2[:, m, :], start=m == 0, stop=m == KT - 1)
                last_of(ins, stat2)
                pe.wait_ge(h2_ok, 8)
                pe.wait_ge(route_in, 64)
                for i in range(NC_LAT):
                    for k in range(KT):
                        ins = mm(bank[6][:, WIDE * i:WIDE * i + WIDE], h2T[:, k, P * i:P * i + P], w_route[:, k, :],
                                 start=k == 0, stop=k == KT - 1)
                last_of(ins, route_mm)
                for q in range(8):
                    i, half = q // 2, q % 2
                    gi = place[("htok", q)]
                    freed(pe, gi)
                    for m in range(4):
                        ins = tr(bk(gi)[:, P * m:P * m + P], h2T[:, 4 * half + m, P * i:P * i + P], ident[:, :])
                    last_of(ins, gemm_done)
                pe.wait_ge(member_ok, 1)
                for j, w in enumerate((strict, ones[:, :])):
                    ins = mm(bank[7][:, P * j:P * j + P], w, both.rearrange("p i e -> p (i e)"), start=True, stop=True)
                last_of(ins, pos_mm)
                pe.wait_ge(split_ok, 8)

                def gather(n):
                    pe.wait_ge(hot_ok, n + 1)
                    for m in range(KT):
                        for j, part in enumerate(parts):
                            for i in range(NC_LAT):
                                ins = mm(bank[(0, 5)[m // 4]][:, BS * (m % 4):BS * (m % 4) + BS],
                                         part[:, i, P * m:P * m + P], onehot[:, i, :],
                                         start=i + j == 0, stop=(i, j) == (NC_LAT - 1, 2))
                    last_of(ins, gather_mm)

                gather(0)
                pe.wait_ge(table_ok, 1)
                with pe.Fori(0, NE // 2, 1) as ep:
                    for par in range(2):
                        s0 = 3 * (1 - par)
                        wg, wu = (slot6[s0 + j].rearrange("p (k n) -> p k n", k=KT) for j in range(2))
                        wd = slot6[s0 + 2].rearrange("p (k n) -> p k n", k=DE // P)
                        first = pe.value_load(table[0:1, bass.ds(2 * ep + par, 1)], min_val=0, max_val=MAXB)
                        end = pe.value_load(table[0:1, bass.ds(2 * ep + (par + 1), 1)], min_val=1, max_val=MAXB)
                        with pe.Fori(first, end, 1) as blk:
                            pe.wait_ge(xg_ok, blk + 1)
                            pe.wait_ge(a_ok, blk)
                            for j, w in enumerate((wg, wu)):
                                pe.wait_ge(expert_in[s0 + j], 16 * ep + 16)
                                for f in range(DE // P):
                                    for k in range(KT):
                                        ins = mm(bank[1 + j][:, BS * f:BS * f + BS], w[:, k, P * f:P * f + P], xg[:, k, :],
                                                 start=k == 0, stop=k == KT - 1)
                            last_of(ins, gu_mm)
                            gather(blk + 1)
                            pe.wait_ge(expert_in[s0 + 2], 16 * ep + 16)
                            pe.wait_ge(y_lo, blk)
                            pe.wait_ge(y_hi, blk)
                            pe.wait_ge(a_ok, blk + 1)
                            for half in range(2):
                                for f in range(DE // P):
                                    ins = mm(bank[3 + half][0:BS, :], aT[:, f, :], wd[:, f, 512 * half:512 * half + 512],
                                             start=f == 0, stop=f == DE // P - 1)
                            last_of(ins, down_mm)

        @block.scalar
        def _(act):
            link = linker(act, alink)
            A = nc.scalar.activation

            def got(name, i):
                gi = place[(name, i)]
                act.wait_ge(gemm_done, gi + 1)
                return bk(gi)

            act.wait_ge(vec_sb, 1)
            act.wait_ge(filled, 6)
            A(csil[:, :, 0:2].rearrange("p k s -> p s k"), vec[:, 0, V_C:V_C + 16].rearrange("p (s k) -> p s k", s=2), ACT.Silu
              ).then_inc(csil_ok, 1)
            for m in range(KT):
                act.wait_ge(dve_read, m + 1)
                A(sq[:, m, :], xT[:, m, :], ACT.Square).then_inc(squares, 1)
            for m in range(KT):
                act.wait_ge(dve_read, 8 + m + 1)
                A(sqc[:, m, :], xTc[:, m, :], ACT.Square).then_inc(squares, 1)
            act.wait_ge(stat_done, 2)
            A(rn[:, TC:], bank[5][:, :], ACT.Sqrt, scale=1.0 / D, bias=eps[:, :]).then_inc(norm_root, 1)
            A(rn[:, 0:TC], bank[6][:, 0:TC], ACT.Sqrt, scale=1.0 / D, bias=eps[:, :]).then_inc(norm_root, 1)
            act.wait_ge(modA_ok, 1)
            act.wait_ge(normed, 2)
            for m in range(KT):
                A(hcm[:, m, :].rearrange("p (w r) -> p r w", r=GRID_H), hT[:, m, :].rearrange("p (r w) -> p r w", r=GRID_H),
                  ACT.Identity, scale=modA[:, 0, m:m + 1], bias=ada[:, m, 0:1]).then_inc(h_ok, 1)
                A(hT[:, m, :], hT[:, m, :], ACT.Identity, scale=modA[:, 0, m:m + 1], bias=ada[:, m, 0:1]).then_inc(h_ok, 1)
                A(hTc[:, m, :], hTc[:, m, :], ACT.Identity, scale=modA[:, 1, m:m + 1], bias=ada[:, m, 1:2]).then_inc(h_ok, 1)

            act.wait_ge(small_in, 16 * 6)
            link(A(expa, a_log[:, :], ACT.Exp))
            act.wait_ge(gates_pre, 1)
            link(A(gabs, gx, ACT.Abs))
            A(gexp, gabs, ACT.Exp, scale=-1.0).then_inc(gates_exp, 1)
            act.wait_ge(gates_u, 1)
            A(gl, gu, ACT.Ln).then_inc(gates_ln, 1)

            cin, cinc, acc = {}, {}, {}
            for s in ("k", "q"):
                cin[s], cinc[s], acc[s] = cin_m, cinc_m, acc_m
            for s in ("B", "C", "x"):
                cin[s], cinc[s], acc[s] = cin_s, cinc_s, acc_s

            def stage_in(n):
                s, m, cx = conv[n]
                src = got(s, 2 * m + cx if s in ("k", "B", "x") else m)
                before = conv_before(n, (NCIN, NCINC))
                if before:
                    act.wait_ge(conv_done, before)
                slot = kind_no[n] % (NCINC if cx else NCIN)
                if cx:
                    o, i_ = cinc[s][:, slot, 2:2 + TC], src[:, 0:TC]
                elif s in ("k", "q"):
                    o = cin[s][:, slot, 2:2 + T].rearrange("p (w r) -> p r w", r=GRID_H)
                    i_ = src[:, :].rearrange("p (r w) -> p r w", r=GRID_H)
                else:
                    o, i_ = cin[s][:, slot, 2:2 + T], src[:, :]
                A(o, i_, ACT.Copy).then_inc(act_read, 1)

            def finish_conv(n):
                s, m, cx = conv[n]
                act.wait_ge(conv_done, n + 1)
                w = TC if cx else T
                at = 0 if cx else TC
                if s == "k":
                    o = kT[:, m, at:at + w]
                elif s == "q":
                    o = qT[:, m, :]
                elif s == "C":
                    o = CT[:, m, :]
                else:
                    if m >= 3 or s == "x":
                        prev = {("B", 3): ("BTr", 1)}.get((s, m))
                        if s == "x":
                            prev = {0: ("BTr", 7), 1: ("BTr", 7), 2: ("BTr", 7)}.get(m, ("xTr", 2 * (m - 3) + 1))
                        act.wait_ge(gemm_done, place[prev] + 1)
                    o = xst[:, m % 3, at:at + w]
                if s == "B" and not cx:
                    A(BT[:, m, :], acc[s][:, n % 3, 0:w], ACT.Silu).then_inc(alink, 1)
                A(o, acc[s][:, n % 3, 0:w], ACT.Silu).then_inc(silu_done, 1)

            pads_seen = [5, 9]
            act.wait_ge(pads, 4)
            LAG = 2

            def conv_run(lo, hi):
                for n in range(lo, hi + LAG):
                    if n < hi:
                        stage_in(n)
                    if n >= lo + LAG:
                        finish_conv(n - LAG)

            conv_run(0, 24)
            for m in range(12):
                half, cc = m // NC_ALL, (m + NC_CTX) % NC_ALL
                src = got("v", m)
                if m == 0:
                    act.wait_ge(h_back, 1)
                A(vone[:, cc, :].rearrange("p (h e) -> p h e", h=HEADS)[:, 2 * half:2 * half + 2, 0:HD],
                  src[:, :].rearrange("p (h e) -> p h e", h=2), ACT.Copy).then_inc(act_read, 1)
            act.wait_ge(em_sum, 1)
            A(em[:, :, :], em[:, :, :], ACT.Exp, scale=-1.0).then_inc(em_ok, 1)
            act.wait_ge(ssd_pre, 1)
            A(e_in[:, :, :, :], acs[:, :, :, :], ACT.Exp).then_inc(ssd_exp, 1)
            A(coef[:, :, :, :], coef[:, :, :, :], ACT.Exp).then_inc(ssd_exp, 1)
            A(tot[:, :, :, :], tot[:, :, :, :], ACT.Exp).then_inc(ssd_exp, 1)

            def copy_scores(h):
                for cc in range(NC_ALL):
                    src = got("S", NC_ALL * h + cc)
                    if h >= 1 and cc == 0:
                        act.wait_ge(wmul, 12 * h)
                    A(scores[:, cc, :], src[:, :], ACT.Copy, scale=HD ** -0.5).then_inc(act_read, 1)

            def exps(h, d):
                u = 2 * h + d
                act.wait_ge(m_bc[h % 2], 16 * (h // 2 + 1))
                act.wait_ge(diag_ok, u + 1)
                if u >= 2:
                    act.wait_ge(av_done, NC_LAT * (u - 1))
                for cc in range(NC_ALL):
                    bias = bkey[:, cc, 4 * d + h:4 * d + h + 1]
                    if cc < NC_CTX:
                        A(attn[u % 2][:, cc, :], mrow[h % 2][:, d, :], ACT.Exp, scale=-1.0, bias=bias).then_inc(wexp, 1)
                        continue
                    j = cc - NC_CTX
                    lo, hi = ((j + 1) * P, T) if d == 0 else (0, j * P)
                    if hi > lo:
                        A(attn[u % 2][:, cc, lo:hi], mrow[h % 2][:, d, lo:hi], ACT.Exp, scale=-1.0, bias=bias)
                    A(attn[u % 2][:, cc, P * j:P * j + P], diag[d][:, j, :], ACT.Exp, scale=-1.0, bias=bias
                      ).then_inc(wexp, 1)

            if upto >= 2:
                copy_scores(0)
                exps(0, 0)
                exps(0, 1)
                for h in range(1, HEADS):
                    copy_scores(h)
                    exps(h, 0)
                    exps(h, 1)
            if upto >= 3:
                act.wait_ge(av_read, 32)
                for h in range(HEADS):
                    for i in range(NC_LAT):
                        A(gate1[:, 2 * h + i // 2, HD * (i % 2):HD * (i % 2) + HD], hsum[:, h, i, :], ACT.Square, accum_out=ms[:, 4 * h + i:4 * h + i + 1]
                          ).then_inc(hsq, 1)
                act.wait_ge(hsq, 16)
                A(ms[:, :], ms[:, :], ACT.Sqrt, scale=1.0 / HD, bias=eps[:, :]).then_inc(hroot, 1)
                for m in range(KT):
                    src = got("o", m)
                    A(sig_o[:, m, :], src[:, :], ACT.Sigmoid).then_inc(act_read, 1)

            def gates_of(b, dst, base):
                for m in range(KT):
                    src = got(f"mg{b}", m)
                    A(dst[:, m, :], src[:, :], ACT.Sigmoid).then_inc(act_read, 1)

            if upto >= 3:
                gates_of(1, gate1, 0)
            if upto >= 4:
                act.wait_ge(pads, 8)
                conv_run(24, 32)
                conv_run(32, len(conv))
                for i in range(NC_LAT):
                    for d in range(2):
                        act.wait_ge(dsub, 2 * i + d + 1)
                        A(decay[i % 2][:, d], decay[i % 2][:, d], ACT.Exp).then_inc(dexp, 1)
            if upto >= 5:
                act.wait_ge(inter_add, 8)
                for m in range(8):
                    i, half = m % 4, m // 4
                    src = got("z", m)
                    if m >= 2:
                        act.wait_ge(yz_ok, m - 1)
                    A(ztok[:, m % 2, :], src[:, :], ACT.Silu).then_inc(act_read, 1)
                for i in range(NC_LAT):
                    act.wait_ge(yz_ok, 5 + i)
                    if i:
                        act.wait_ge(ysq, i)
                    A(junk, ytok[:, i, :], ACT.Square, accum_out=ms[:, i:i + 1]).then_inc(ysq, 1)
                act.wait_ge(ysq, 4)
                A(ms[:, 0:NC_LAT], ms[:, 0:NC_LAT], ACT.Sqrt, scale=1.0 / D, bias=eps[:, :]).then_inc(yroot, 1)
                gates_of(2, gate2, 8)
            if upto >= 6:
                act.wait_ge(pads, 9)
                for m in range(KT):
                    src = got("pa", m)
                    if m >= 2:
                        act.wait_ge(pool_ok, m - 1)
                    A(ppad[:, m % 2, :].rearrange("p (r w) -> p r w", r=GRID_H)[:, :, 8:8 + GRID_W],
                      src[:, :].rearrange("p (r w) -> p r w", r=GRID_H), ACT.Copy).then_inc(act_read, 1)
                for m in range(KT):
                    src = got("pw", m)
                    A(br0[:, m, :], src[:, :], ACT.Copy, scale=vec[:, 0, V_PS + m:V_PS + m + 1]).then_inc(act_read, 1)
                gates_of(0, gate0, 16)
            if upto >= 7:
                for m in range(KT):
                    act.wait_ge(dve_read, read_no[place[("wo", m)]][1])
                    A(sq2[:, m, :], xl[:, m, :], ACT.Square).then_inc(sq2_ok, 1)
                act.wait_ge(stat2, 1)
                A(rn2, bank[5][:, :], ACT.Sqrt, scale=1.0 / D, bias=eps[:, :]).then_inc(root2, 1)
                act.wait_ge(normed2, 1)
                for m in range(KT):
                    A(h2T[:, m, :], h2T[:, m, :], ACT.Identity, scale=modF[:, m:m + 1], bias=ada[:, 24 + m, 0:1]
                      ).then_inc(h2_ok, 1)
                for q in range(8 + 2):
                    if q < 8:
                        i, half = q // 2, q % 2
                        at = slice(512 * half, 512 * half + 512)
                        src = got("htok", q)
                        A(h2tok[:, i, at], src[:, :], ACT.Copy).then_inc(act_read, 1)
                        act.wait_ge(act_read, read_no[place[("htok", q)]][1])
                        A(parts[0][:, i, at], h2tok[:, i, at], ACT.Copy).then_inc(split_hi, 1)
                    if q >= 2:
                        i, half = (q - 2) // 2, q % 2
                        at = slice(512 * half, 512 * half + 512)
                        act.wait_ge(split_lo, q - 1)
                        A(parts[1][:, i, at], h2tok[:, i, at], ACT.Copy).then_inc(split_mid, 1)
                act.wait_ge(gexp_pre, 1)
                A(gsc, gsc, ACT.Exp).then_inc(gexp_ok, 1)
                act.wait_ge(topexp_pre, 1)
                A(etmp, etmp, ACT.Exp).then_inc(topexp_ok, 1)
                act.wait_ge(table_ok, 1)
                n_blocks = act.value_load(table[0:1, NE:NE + 1], min_val=NE, max_val=MAXB)

                def take_gathered(n):
                    act.wait_ge(gather_mm, n + 1)
                    A(xg[:, 0:4, :].rearrange("p k s -> p (k s)"), bank[0][:, 0:4 * BS], ACT.Copy)
                    A(xg[:, 4:8, :].rearrange("p k s -> p (k s)"), bank[5][:, 0:4 * BS], ACT.Copy).then_inc(xg_ok, 1)

                take_gathered(0)
                with act.Fori(0, n_blocks, 1) as blk:
                    act.wait_ge(gu_mm, blk + 1)
                    A(sg, bank[1][:, 0:4 * BS], ACT.Silu).then_inc(sg_ok, 1)
                    take_gathered(blk + 1)
                    act.wait_ge(down_mm, blk + 1)
                    A(y_sb[0:BS, 0:512], bank[3][0:BS, :], ACT.Copy).then_inc(y_lo, 1)
                    act.wait_ge(y_lo, blk + 1)
                    act.wait_ge(y_hi, blk + 1)
                    act.dma_start(y_scr[blk], y_sb[0:BS, :]).then_inc(y_out, 16)
                    act.wait_ge(y_out, 16 * blk + 16)
                A(ms[:, 0:4], ms[:, 0:4], ACT.Copy).then_inc(blocks_done, 1)
                for i in range(NC_LAT):
                    act.wait_ge(fin_ok_pre, i + 1)
                    A(yg[2 * i + 1], yg[2 * i], ACT.Square, accum_out=ms[:, i:i + 1]).then_inc(fsq, 1)
                    act.wait_ge(fsq, i + 1)
                    A(ms[:, i:i + 1], ms[:, i:i + 1], ACT.Sqrt, scale=1.0 / D, bias=eps[:, :]).then_inc(froot, 1)

        @block.vector
        def _(dve):
            link = linker(dve, vlink)
            v = nc.vector

            def got(name, i):
                gi = place[(name, i)]
                dve.wait_ge(gemm_done, gi + 1)
                return bk(gi)

            def high_weights(name, m):
                u = unit_no[(name, m)]
                arrived(dve, first_chunk[name] + m // 4)
                if u >= NHI:
                    dve.wait_ge(gemm_done, unit_end(u - NHI))
                v.tensor_copy(w_high[u % NHI], raw_tile(u)).then_inc(w_hi, 1)

            def high_operand(high, whole, m):
                whole_m = whole[m] if isinstance(whole, list) else whole[:, m, :]
                v.tensor_copy(high[:, m, :], whole_m).then_inc(op_hi, 1)

            dve.wait_ge(vec_tr, 1)
            for part in range(3):
                ins = v.tensor_copy(vec[:, part, 0:n_rows[part]], bank[7][:, P * part:P * part + n_rows[part]])
            ins.then_inc(vec_sb, 1)
            for m in range(KT):
                v.tensor_copy(xT[:, m, :], got("xT", m)[:, :]).then_inc(dve_read, 1)
            for m in range(KT):
                v.tensor_copy(xTc[:, m, :], got("xTc", m)[:, 0:TC]).then_inc(dve_read, 1)
            dve.wait_ge(norm_root, 2)
            link(v.reciprocal(rn[:, :], rn[:, :]))
            v.tensor_tensor(hT, xT, rn[:, None, TC:].to_broadcast([P, KT, T]), ALU.mult).then_inc(normed, 1)
            v.tensor_tensor(hTc, xTc, rn[:, None, 0:TC].to_broadcast([P, KT, TC]), ALU.mult).then_inc(normed, 1)
            dve.wait_ge(ada_done, 4)
            def add_bias(n, at):
                return v.tensor_tensor(ada[:, at:at + 4, :],
                                       bank[4 + n % 4][:, 0:4 * WIDE].rearrange("p (j s) -> p j s", s=WIDE)[:, :, 0:2],
                                       vec[:, 0, V_BADA + at:V_BADA + at + 4, None].to_broadcast([P, 4, 2]), ALU.add)

            for n in range(4):
                ins = add_bias(n, 4 * n)
            link(ins)
            v.scalar_tensor_tensor(modA[:, :, :], ada[:, 8:16, :].rearrange("p k s -> p s k"), 1.0,
                                   vec[:, 0, None, V_GMIX:V_GMIX + 8].to_broadcast([P, 2, KT]), ALU.add, ALU.mult
                                   ).then_inc(modA_ok, 1)
            dve.wait_ge(h_ok, 24)
            v.tensor_copy(h_high0, hT).then_inc(h_first, 1)
            v.tensor_copy(hc_high0, hTc).then_inc(h_first, 1)
            for m in range(4):
                high_weights("k", m)
            dve.wait_ge(h_first, 2)
            dve.wait_ge(gates_mm, 1)
            v.tensor_tensor(hT_low, hT, h_high0.bitcast(f32), ALU.subtract).then_inc(h_low, 1)
            v.tensor_tensor(hTc_low, hTc, hc_high0.bitcast(f32), ALU.subtract).then_inc(h_low, 1)
            fpart = gx[:, 0:48].rearrange("p (c h) -> p c h", c=NC_ALL)
            dpart = gx[:, 48:240].rearrange("p (c h) -> p c h", c=NC_ALL)
            b5 = bank[5][:, 0:GST * NC_ALL].rearrange("p (c h) -> p c h", c=NC_ALL)
            b6 = bank[6][:, 0:GST * NC_ALL].rearrange("p (c h) -> p c h", c=NC_ALL)[:, :, 16:48]
            v.tensor_tensor(ig[:, :, :], b5[:, :, 0:8], gate_b[:, None, 0:8].to_broadcast([P, NC_ALL, 8]), ALU.add)
            v.tensor_tensor(fpart, b5[:, :, 8:16], gate_b[:, None, 8:16].to_broadcast([P, NC_ALL, 8]), ALU.add)
            v.tensor_tensor(dpart, b6, dt_b[:, None, :].to_broadcast([P, NC_ALL, 32]), ALU.add).then_inc(gates_pre, 1)
            dve.wait_ge(gates_exp, 1)
            v.tensor_scalar(gu, gexp, 1.0, None, ALU.add).then_inc(gates_u, 1)
            dve.wait_ge(gates_u, 1)
            link(v.tensor_scalar(gd_, gu, -1.0, None, ALU.add))
            link(v.tensor_tensor(gd_, gexp, gd_, ALU.subtract))
            dve.wait_ge(gates_ln, 1)
            link(v.reciprocal(gu, gu))
            link(v.tensor_tensor(gd_, gd_, gu, ALU.mult))
            link(v.tensor_tensor(gl, gl, gd_, ALU.add))
            v.scalar_tensor_tensor(lf[:, 0:NC_ALL, :].rearrange("p c h -> p (c h)"), gx[:, 0:48], 0.0, gl[:, 0:48],
                                   ALU.min, ALU.subtract).then_inc(lf_ok, 1)
            for d in range(2):
                ins = v.scalar_tensor_tensor(
                    dt[:, d], dpart[:, :, 16 * d:16 * d + 16], 0.0,
                    gl[:, 48:240].rearrange("p (c h) -> p c h", c=NC_ALL)[:, :, 16 * d:16 * d + 16], ALU.max, ALU.add)
            link(ins)
            for d in range(2):
                ins = v.scalar_tensor_tensor(dta[:, d], dt[:, d], -1.0,
                                             expa[:, None, 16 * d:16 * d + 16].to_broadcast([P, NC_ALL, SH]),
                                             ALU.mult, ALU.mult)
            ins.then_inc(lf_ok, 1)

            def conv_tile(n):
                s, m, cx = conv[n]
                first = s in ("k", "q")
                cin, cinc, acc = (cin_m, cinc_m, acc_m) if first else (cin_s, cinc_s, acc_s)
                part = 1 if first else 2
                base = {"k": 8, "q": 0, "x": 0, "B": 8, "C": 12}[s] + m
                g = place[(s, 2 * m + cx if s in ("k", "B", "x") else m)]
                dve.wait_ge(act_read, read_no[g][1])
                if n >= 3:
                    dve.wait_ge(silu_done, n - 2)
                w = TC if cx else T
                slot = kind_no[n] % (NCINC if cx else NCIN)
                src = (cinc if cx else cin)[:, slot, :]
                a = acc[:, n % 3, 0:w]

                def tap(j):
                    return vec[:, part, 16 * j + base:16 * j + base + 1]
                link(v.tensor_scalar(a, src[:, 0:w], tap(0), vec[:, part, 64 + base:65 + base], ALU.mult, ALU.add))
                for j in range(1, 4):
                    ins = v.scalar_tensor_tensor(a, src[:, j:j + w], tap(j), a, ALU.mult, ALU.add)
                    if j < 3:
                        link(ins)
                ins.then_inc(conv_done, 1)
                ahead = unit_no[(s, m)] + NHI
                if not cx and units[ahead][0] in ("k", "q", "C", "x"):
                    high_weights(*units[ahead])

            for n in range(16):
                conv_tile(n)
            dve.wait_ge(cum_mm, 1)
            v.tensor_copy(acs[:, :, :, :].rearrange("p d c h -> p (d c h)"), bank[7][:, 0:192]).then_inc(cum_read, 1)
            run = bank[4][:, 0:3 * WIDE].rearrange("p (j c h) -> p j c h", j=3, h=8)
            v.tensor_copy(ftot[:, :, :], run[:, 2, 0:NC_ALL, :])
            v.tensor_copy(fcum[:, :, 0:4], run[:, 0, 0:NC_ALL, 0:4])
            link(v.tensor_copy(fcum[:, :, 4:8], run[:, 1, 0:NC_ALL, 4:8]))
            orders = ([0, 1, 2, 3, 4, 5], [1, 0, 5, 4, 3, 2])
            for n in range(1, NC_ALL):
                for d, order in enumerate(orders):
                    cols_d = slice(4 * d, 4 * d + 4)
                    before, cc = ftot[:, order[n - 1], cols_d], order[n]
                    v.tensor_tensor(fcum[:, cc, cols_d], fcum[:, cc, cols_d], before, ALU.add)
                    ins = v.tensor_tensor(ftot[:, cc, cols_d], ftot[:, cc, cols_d], before, ALU.add)
                link(ins)
            v.tensor_tensor(bkey[:, :, :], ig[:, :, :], fcum[:, :, :], ALU.subtract).then_inc(bkey_ok, 1)
            for n in range(16, 20):
                conv_tile(n)
            dve.wait_ge(tot_mm, 1)
            link(v.tensor_copy(tot[:, :, :, :].rearrange("p d c h -> p (d c h)"), bank[7][:, 192:384]))
            v.tensor_tensor(coef[:, :, :, :], tot[:, :, :, :], acs[:, :, :, :], ALU.subtract).then_inc(ssd_pre, 1)
            dve.wait_ge(brow_tr, 1)
            v.tensor_copy(brow[0:HEADS, :, 0:TC], bank[4][0:HEADS, :].rearrange("p (d t) -> p d t", d=2))
            v.tensor_copy(brow[0:HEADS, 0, TC:], bank[5][0:HEADS, :])
            link(v.tensor_copy(brow[0:HEADS, 1, TC:], bank[6][0:HEADS, :]))
            scan = v.tensor_tensor_scan
            scan(mx[0:HEADS, 0, :], brow[0:HEADS, 0, :], brow[0:HEADS, 0, :], 0.0, ALU.max, ALU.max)
            link(scan(mx[0:HEADS, 1, 0:TC][:, ::-1], brow[0:HEADS, 1, 0:TC][:, ::-1], brow[0:HEADS, 1, 0:TC][:, ::-1],
                      0.0, ALU.max, ALU.max))
            scan(mx[0:HEADS, 1, TC:][:, ::-1], brow[0:HEADS, 1, TC:][:, ::-1], brow[0:HEADS, 1, TC:][:, ::-1],
                 mx[0:HEADS, 1, 0:1], ALU.max, ALU.max).then_inc(mx_ok, 1)
            for n in range(20, 23):
                conv_tile(n)
            dve.wait_ge(gemm_done, place[("q", 7)] + 1)
            dve.wait_ge(h_low, 2)
            link(v.tensor_tensor(hT, hT_low.bitcast(f32), h_high0.bitcast(f32), ALU.add))
            v.tensor_tensor(hTc, hTc_low.bitcast(f32), hc_high0.bitcast(f32), ALU.add).then_inc(h_back, 1)
            conv_tile(23)
            dve.wait_ge(mback_tr, 1)
            v.tensor_tensor(em[:, :, :], bank[5][:, 0:32].rearrange("p (i h) -> p i h", i=NC_LAT),
                            fcum[:, NC_CTX:, :], ALU.add).then_inc(em_sum, 1)
            dve.wait_ge(ssd_exp, 3)
            v.tensor_tensor(coef[:, :, :, :], coef[:, :, :, :], dt[:, :, :, :], ALU.mult).then_inc(coef_ok, 1)

            def weights(h, d):
                u = 2 * h + d
                for cc in range(NC_ALL):
                    j = cc - NC_CTX
                    dve.wait_ge(wexp, 6 * u + cc + 1)
                    dve.wait_ge(act_read, read_no[place[("S", NC_ALL * h + cc)]][1])
                    lo, hi = (0, T) if cc < NC_CTX else ((j * P, T) if d == 0 else (0, (j + 1) * P))
                    v.tensor_tensor(attn[u % 2][:, cc, lo:hi], attn[u % 2][:, cc, lo:hi], scores[:, cc, lo:hi],
                                    ALU.mult).then_inc(wmul, 1)

            def outputs(h, d):
                u = 2 * h + d
                for i in range(NC_LAT):
                    n = NC_LAT * u + i
                    b = bank[(4, 6, 7)[n % 3]]
                    dve.wait_ge(av_done, n + 1)
                    link(v.tensor_scalar(den[:, 0:1], b[:, HD:HD + 1], -1.0, em[:, i, 4 * d + h:4 * d + h + 1],
                                         ALU.mult, ALU.max))
                    link(v.tensor_tensor(den[:, 0:1], den[:, 0:1], b[:, HD:HD + 1], ALU.max))
                    link(v.reciprocal(den[:, 1:2], den[:, 0:1]))
                    if d == 0:
                        v.tensor_scalar(hsum[:, h, i, :], b[:, 0:HD], den[:, 1:2], None, ALU.mult).then_inc(av_read, 1)
                    else:
                        v.scalar_tensor_tensor(hsum[:, h, i, :], b[:, 0:HD], den[:, 1:2], hsum[:, h, i, :],
                                               ALU.mult, ALU.add).then_inc(av_read, 1)

            if upto >= 2:
                dve.wait_ge(em_ok, 1)
                for h in range(HEADS):
                    weights(h, 0)
                    if h >= 1:
                        outputs(h - 1, 1)
                    weights(h, 1)
                    if h == HEADS - 1:
                        dve.wait_ge(gemm_done, place[("S", 6 * HEADS - 1)] + 1)
                        for m in range(KT):
                            high_operand(h_high1, hT, m)
                        for m in range(4):
                            high_weights("o", m)
                    outputs(h, 0)
                outputs(HEADS - 1, 1)

            if upto >= 3:
                dve.wait_ge(hroot, 1)
                link(v.reciprocal(ms[:, :], ms[:, :]))
                for h in range(HEADS):
                    v.tensor_tensor(hsum[:, h], hsum[:, h], ms[:, 4 * h:4 * h + 4, None].to_broadcast([P, NC_LAT, HD]),
                                    ALU.mult).then_inc(hnorm, 1)
                for m in range(4, 8):
                    high_weights("o", m)
                for m in range(4):
                    high_weights("mg1", m)
                dve.wait_ge(act_read, read_no[place[("o", 7)]][1])
                for m in range(KT):
                    src = got("hT", m)
                    v.scalar_tensor_tensor(colmajor(br1[m]), src[:, :].rearrange("p (w r) -> p w r", r=GRID_H),
                                           vec[:, 0, V_MG + m:V_MG + m + 1], colmajor(sig_o[:, m, :]),
                                           ALU.mult, ALU.mult).then_inc(dve_read, 1)
                for m in range(KT):
                    dve.wait_ge(dve_read, read_no[place[("hT", m)]][1])
                    high_operand(br1_high, br1, m)
                for m in range(4, 8):
                    high_weights("mg1", m)
                for m in range(4):
                    high_weights("wb1", m)
                v.tensor_copy(h_high3, h_high1.bitcast(f32)).then_inc(h_moved, 1)
                link(v.tensor_copy(hc_high3, hTc))
                v.tensor_tensor(hTc_low, hTc, hc_high3.bitcast(f32), ALU.subtract).then_inc(h_moved, 1)

            def merge(b, gate, base, tmp, after=None):
                for m in range(KT):
                    if m < 4:
                        high_weights(f"wb{b}", 4 + m)
                    elif after:
                        high_weights(after, m - 4)
                    dve.wait_ge(act_read, read_no[place[(f"mg{b}", m)]][1])
                    src = got(f"wb{b}", m)
                    if base == 0:
                        v.tensor_tensor(merged[:, m, :], gate[:, m, :], src[:, :], ALU.mult).then_inc(dve_read, 1)
                    else:
                        v.tensor_tensor(tmp[:, m % 2, :], gate[:, m, :], src[:, :], ALU.mult).then_inc(dve_read, 1)
                        dve.wait_ge(dve_read, read_no[place[(f"wb{b}", m)]][1])
                        v.tensor_tensor(merged[:, m, :], merged[:, m, :], tmp[:, m % 2, :], ALU.add).then_inc(prod_ok, 1)
                        if b == 0:
                            dve.wait_ge(prod_ok, base + m - 7)
                            high_operand(merged_high, merged, m)

            if upto >= 3:
                merge(1, gate1, 0, None, after="B")
            if upto >= 4:
                def evac_token_major(name, m):
                    src = got(name + "Tr", 2 * m)
                    dst = Btok if name == "B" else xtok
                    v.tensor_copy(dst[:, NC_CTX:, P * m:P * m + P], src[:, :].rearrange("p (i t) -> p i t", i=NC_LAT)
                                  ).then_inc(dve_read, 1)
                    src = got(name + "Tr", 2 * m + 1)
                    v.tensor_copy(dst[:, 0:NC_CTX, P * m:P * m + P], src[:, 0:TC].rearrange("p (i t) -> p i t", i=NC_CTX)
                                  ).then_inc(dve_read, 1)

                for m in range(4 + 2):
                    if m < 4:
                        conv_tile(conv_no[("B", m, 0)])
                        conv_tile(conv_no[("B", m, 1)])
                    if m >= 2:
                        evac_token_major("B", m - 2)
                for m in range(4):
                    conv_tile(conv_no[("C", m, 0)])
                dve.wait_ge(arow_tr, 1)
                for d in range(2):
                    v.tensor_copy(rowa[0:SH, d, :], bank[4 + d][0:SH, :]).then_inc(arow_ok, 1)
                for m in range(8 + 2):
                    if m < 8:
                        conv_tile(conv_no[("x", m, 0)])
                        conv_tile(conv_no[("x", m, 1)])
                    if m >= 2:
                        evac_token_major("x", m - 2)
                dve.wait_ge(gemm_done, place[("x", 15)] + 1)
                v.tensor_tensor(hT, hT_low.bitcast(f32), h_high3.bitcast(f32), ALU.add).then_inc(h_back, 1)
                dve.wait_ge(h_back, 2)
                hx = lambda ap: ap.rearrange("p (h e) -> p h e", h=SH)
                for i in range(NC_LAT):
                    w = decay[i % 2]
                    cc = NC_CTX + i
                    for d in range(2):
                        dve.wait_ge(dmask, 2 * i + d + 1)
                        v.tensor_tensor(w[:, d], w[:, d], acs[:, d, cc, :, None].to_broadcast([P, SH, P]), ALU.subtract
                                        ).then_inc(dsub, 1)
                    for d in range(2):
                        dve.wait_ge(dexp, 2 * i + d + 1)
                        ins = v.tensor_tensor(w[:, d], w[:, d], dt[:, d, cc, :, None].to_broadcast([P, SH, P]), ALU.mult)
                    link(ins)
                    link(v.tensor_tensor(w[:, 0], w[:, 0], w[:, 1], ALU.add))
                    dve.wait_ge(g_mm, i + 1)
                    v.tensor_tensor(w[:, 0].rearrange("p (g h) t -> p g h t", g=SG_),
                                    w[:, 0].rearrange("p (g h) t -> p g h t", g=SG_),
                                    bank[4 + i % 2][:, :].rearrange("p (g t) -> p g t", g=SG_)[:, :, None, :]
                                    .to_broadcast([P, SG_, HPG, P]), ALU.mult).then_inc(dmul, 1)
                    link(v.tensor_tensor(hx(ytok[:, i, :]), hx(xtok[:, cc, :]),
                                         d_skip[:, :, None].to_broadcast([P, SH, SP_]), ALU.mult))
                    dve.wait_ge(intra_mm, i + 1)
                    v.tensor_tensor(ytok[:, i, 0:512], ytok[:, i, 0:512], bank[6][:, :], ALU.add)
                    v.tensor_tensor(ytok[:, i, 512:1024], ytok[:, i, 512:1024], bank[7][:, :], ALU.add).then_inc(y_ok, 1)
                dve.wait_ge(y_ok, 4)
                dve.wait_ge(coef_ok, 1)
                n_inter = 0

                def inter(d, cq):
                    cc = NC_CTX + cq
                    dve.wait_ge(inter_mm, n_inter + 1)
                    for b in range(2):
                        ins = v.tensor_tensor(ytmp[:, 0, 512 * b:512 * b + 512].rearrange("p (h e) -> p h e", h=8),
                                              bank[6 + b][:, :].rearrange("p (h e) -> p h e", h=8),
                                              e_in[:, d, cc, 8 * b:8 * b + 8, None].to_broadcast([P, 8, SP_]), ALU.mult)
                    ins.then_inc(inter_read, 1)
                    dve.wait_ge(inter_read, n_inter + 1)
                    v.tensor_tensor(ytok[:, cq, :], ytok[:, cq, :], ytmp[:, 0, :], ALU.add).then_inc(inter_add, 1)
                    dve.wait_ge(inter_add, n_inter + 1)

                for n in range(10):
                    d, step = n % 2, n // 2
                    cc = ([0, 1, 2, 3, 4], [1, 0, 5, 4, 3])[d][step]
                    if step >= 2:
                        inter(d, (step - 2, 3 - (step - 2))[d])
                        n_inter += 1
                    if step:
                        link(v.tensor_tensor(hx(state[:, d]), hx(state[:, d]), tot[:, d, cc, :, None].to_broadcast([P, SH, SP_]),
                                             ALU.mult))
                    dve.wait_ge(cs_mm, n + 1)
                    for b in range(2):
                        dst = state[:, d, 512 * b:512 * b + 512]
                        if step == 0:
                            ins = v.tensor_copy(dst, bank[4 + b][:, :])
                        else:
                            ins = v.tensor_tensor(dst, dst, bank[4 + b][:, :], ALU.add)
                    ins.then_inc(st_ok, 1)
                    dve.wait_ge(st_ok, n + 1)
                for d in range(2):
                    inter(d, (3, 0)[d])
                    n_inter += 1
            if upto >= 5:
                for m in range(8):
                    i, half = m % 4, m // 4
                    dve.wait_ge(act_read, read_no[place[("z", m)]][1])
                    v.tensor_tensor(ytok[:, i, 512 * half:512 * half + 512], ytok[:, i, 512 * half:512 * half + 512],
                                    ztok[:, m % 2, :], ALU.mult).then_inc(yz_ok, 1)
                dve.wait_ge(gemm_done, place[("z", 7)] + 1)
                for m in range(KT):
                    high_operand(h_high2, hT, m)
                for m in range(4):
                    high_weights("mg2", m)
                dve.wait_ge(yroot, 1)
                dve.wait_ge(yz_ok, 8)
                link(v.reciprocal(ms[:, 0:NC_LAT], ms[:, 0:NC_LAT]))
                for i in range(NC_LAT):
                    v.tensor_scalar(ytok[:, i, :], ytok[:, i, :], ms[:, i:i + 1], None, ALU.mult).then_inc(ynorm, 1)
                for m in range(KT):
                    src = got("yT", m)
                    v.tensor_scalar(br2[:, m, :], src[:, :], vec[:, 0, V_SG + m:V_SG + m + 1], None, ALU.mult
                                    ).then_inc(dve_read, 1)
                    dve.wait_ge(dve_read, read_no[place[("yT", m)]][1])
                    high_operand(br2_high, br2, m)
                for m in range(4, 8):
                    high_weights("mg2", m)
                for m in range(4):
                    high_weights("wb2", m)
                merge(2, gate2, 8, prod2, after="pa")
            if upto >= 6:
                for m in range(KT):
                    if m < 4:
                        high_weights("pa", 4 + m)
                    else:
                        high_weights("mg0", m - 4)
                    gi, w = m // 2, 2 << (m // 2)
                    dve.wait_ge(act_read, read_no[place[("pa", m)]][1])
                    rows = lambda ap: ap.rearrange("p (r w) -> p r w", r=GRID_H)
                    cur = rows(ppad[:, m % 2, :])
                    x0 = cur
                    bufs = [rows(psum_a), rows(psum_b)]
                    half, step = 1, 0
                    lo, hi = 1, PR
                    link(v.tensor_tensor(bufs[0][:, :, 1:PR], cur[:, :, 0:PR - 1], cur[:, :, 1:PR], ALU.add))
                    cur, n = bufs[0], 2
                    while n < w:
                        q = n // 2
                        lo, hi = lo + q, hi - q
                        nxt = bufs[(step + 1) % 2]
                        link(v.tensor_tensor(nxt[:, :, lo:hi], cur[:, :, lo - q:hi - q], cur[:, :, lo + q:hi + q], ALU.add))
                        cur, n, step = nxt, 2 * n, step + 1
                    o = rows(pooled[:, m, :])
                    link(v.tensor_tensor(o, cur[:, :, 8:8 + GRID_W],
                                         inv_cnt[:, gi, None, :].to_broadcast([P, GRID_H, GRID_W]), ALU.mult))
                    v.tensor_tensor(o, o, x0[:, :, 8:8 + GRID_W], ALU.subtract).then_inc(pool_ok, 1)
                for m in range(KT):
                    dve.wait_ge(act_read, read_no[place[("pw", m)]][1])
                    if m == 0:
                        dve.wait_ge(gemm_done, place[("pw", 7)] + 1)
                    high_operand(br0_high, br0, m)
                for m in range(4, 8):
                    high_weights("mg0", m)
                for m in range(4):
                    high_weights("wb0", m)
                merge(0, gate0, 16, prod2)
                for n in range(8):
                    dve.wait_ge(ada_done, 5 + n)
                    add_bias(n, 16 + 4 * n).then_inc(ada2_read, 1)
                dve.wait_ge(ada2_read, 8)
                v.scalar_tensor_tensor(modF[:, :], ada[:, 32:40, 0], 1.0, vec[:, 0, V_GFFN:V_GFFN + 8], ALU.add, ALU.mult
                                       ).then_inc(ada2_ok, 1)
                for m in range(4):
                    high_weights("wo", m)
                dve.wait_ge(xl_in, 16)
                for m in range(KT):
                    if m < 4:
                        high_weights("wo", 4 + m)
                    src = got("wo", m)
                    v.scalar_tensor_tensor(xl[:, m, :], src[:, :], ada[:, 16 + m, 0:1], xl[:, m, :], ALU.mult, ALU.add
                                           ).then_inc(dve_read, 1)
            if upto >= 7:
                for q in range(8):
                    i, half = q // 2, q % 2
                    src = got("xtok", q)
                    v.tensor_copy(xltok[:, i, 512 * half:512 * half + 512], src[:, :]).then_inc(dve_read, 1)
                dve.wait_ge(root2, 1)
                link(v.reciprocal(rn2, rn2))
                dve.wait_ge(dve_read, read_no[place[("wo", 7)]][1])
                v.tensor_tensor(h2T, xl, rn2[:, None, :].to_broadcast([P, KT, T]), ALU.mult).then_inc(normed2, 1)
                dve.wait_ge(iota_ok, 1)
                dve.wait_ge(normed2, 1)
                X = AX.X
                link(v.tensor_scalar(rev, rowid[:, 0:8], -1.0, 8.0, ALU.mult, ALU.add))
                link(v.tensor_tensor(strict, triu[:, :], ident[:, :], ALU.subtract))
                for q in range(8 + 2):
                    if q < 8:
                        i, half = q // 2, q % 2
                        at = slice(512 * half, 512 * half + 512)
                        dve.wait_ge(split_hi, q + 1)
                        v.tensor_tensor(h2tok[:, i, at], h2tok[:, i, at], parts[0][:, i, at], ALU.subtract).then_inc(split_lo, 1)
                    if q >= 2:
                        i, half = (q - 2) // 2, q % 2
                        at = slice(512 * half, 512 * half + 512)
                        dve.wait_ge(split_mid, q - 1)
                        v.tensor_tensor(parts[2][:, i, at], h2tok[:, i, at], parts[1][:, i, at], ALU.subtract).then_inc(split_ok, 1)
                dve.wait_ge(route_mm, 1)
                link(v.tensor_tensor(logit, bank[6][:, 0:NC_LAT * WIDE].rearrange("p (i n) -> p i n", i=NC_LAT)[:, :, 0:36],
                                     b_route[:, None, :].to_broadcast([P, NC_LAT, 36]), ALU.add))
                lg, le = logit[:, :, 0:4], logit[:, :, 4:36]

                def first_max(dst, best, src, n):
                    link(v.tensor_reduce(best, src, X, ALU.max))
                    sc = rtmp[:, :, 0:n]
                    link(v.tensor_tensor(sc, src, best[:, :, None].to_broadcast([P, NC_LAT, n]), ALU.is_equal))
                    link(v.tensor_tensor(sc, sc, rev[:, None, 0:n].to_broadcast([P, NC_LAT, n]), ALU.mult))
                    link(v.tensor_reduce(rmax, sc, X, ALU.max))
                    link(v.tensor_tensor(dst, sc, rmax[:, :, None].to_broadcast([P, NC_LAT, n]), ALU.is_equal))

                first_max(ghot, gmax, lg, 4)
                v.tensor_tensor(gsc, lg, gmax[:, :, None].to_broadcast([P, NC_LAT, 4]), ALU.subtract).then_inc(gexp_pre, 1)
                link(v.tensor_tensor(lmul, le.rearrange("p i (g x) -> p i g x", g=4),
                                     ghot[:, :, :, None].to_broadcast([P, NC_LAT, 4, 8]), ALU.mult)
                     if False else
                     v.tensor_tensor(lmul.rearrange("p (i g) x -> p i g x", i=NC_LAT), le.rearrange("p i (g x) -> p i g x", g=4),
                                     ghot[:, :, :, None].to_broadcast([P, NC_LAT, 4, 8]), ALU.mult))
                link(v.tensor_reduce(lsel, lmul.rearrange("p (i g) x -> p i x g", i=NC_LAT), X, ALU.add))
                first_max(hot[0], top[0], lsel, 8)
                link(v.scalar_tensor_tensor(lsel, hot[0], -BIG, lsel, ALU.mult, ALU.add))
                first_max(hot[1], top[1], lsel, 8)
                v.tensor_tensor(etmp, top[1], top[0], ALU.subtract).then_inc(topexp_pre, 1)
                dve.wait_ge(gexp_ok, 1)
                link(v.tensor_reduce(pgrp, gsc, X, ALU.add))
                dve.wait_ge(topexp_ok, 1)
                link(v.tensor_scalar(wtok[0], etmp, 1.0, None, ALU.add))
                link(v.tensor_tensor(wtok[0], wtok[0], pgrp, ALU.mult))
                link(v.reciprocal(wtok[0], wtok[0]))
                link(v.tensor_tensor(wtok[1], wtok[0], etmp, ALU.mult))
                for j in range(2):
                    ins = v.tensor_tensor(member[j].rearrange("p i (g x) -> p i g x", g=4),
                                          ghot[:, :, :, None].to_broadcast([P, NC_LAT, 4, 8]),
                                          hot[j][:, :, None, :].to_broadcast([P, NC_LAT, 4, 8]), ALU.mult)
                link(ins)
                v.tensor_tensor(both, member[0], member[1], ALU.add).then_inc(member_ok, 1)
                dve.wait_ge(pos_mm, 1)
                b7 = bank[7]
                nt = SUBS - 1
                v.tensor_copy(mtot, b7[:, P:2 * P].rearrange("p (i e) -> p i e", i=NC_LAT))
                link(v.tensor_copy(ptmp, b7[:, 0:P].rearrange("p (i e) -> p i e", i=NC_LAT)))
                for i in range(1, NC_LAT):
                    v.tensor_tensor(ptmp[:, i, :], ptmp[:, i, :], mtot[:, i - 1, :], ALU.add)
                    link(v.tensor_tensor(mtot[:, i, :], mtot[:, i, :], mtot[:, i - 1, :], ALU.add))
                link(v.tensor_scalar(thr[:, 0, :], rowid[:, 1:1 + nt], float(BS), None, ALU.mult))
                link(v.tensor_copy(thr[:, 1:, :], thr[:, 0:1, :].to_broadcast([P, NE - 1, nt])))
                link(v.tensor_tensor(thr, mtot[:, NC_LAT - 1, :, None].to_broadcast([P, NE, nt]), thr, ALU.is_gt))
                link(v.tensor_reduce(nblk, thr, X, ALU.add))
                link(v.tensor_scalar(nblk, nblk, 1.0, None, ALU.add))
                link(v.memset(cumx[:, 0:1], 0.0))
                link(v.tensor_tensor_scan(cumx[:, 1:], ones[:, 0:NE], nblk, 0.0, ALU.mult, ALU.add))
                v.tensor_copy(table[:, :], cumx[0:1, :]).then_inc(table_ok, 1)
                link(v.scalar_tensor_tensor(row, cumx[:, None, 0:NE].to_broadcast([P, NC_LAT, NE]), float(BS), ptmp,
                                            ALU.mult, ALU.add))
                for j in range(2):
                    link(v.tensor_tensor(member[j], member[j], row, ALU.mult))
                    link(v.tensor_reduce(idxf[:, j::2], member[j], X, ALU.add))
                v.tensor_copy(idx[:, :], idxf).then_inc(idx_ok, 1)
                n_blocks = dve.value_load(table[0:1, NE:NE + 1], min_val=NE, max_val=MAXB)

                def fill_onehot(n):
                    for j in range(2):
                        ins = v.tensor_tensor(eq[j], rowid[:, None, :].to_broadcast([P, NC_LAT, BS]),
                                              idxf[:, j::2, None].to_broadcast([P, NC_LAT, BS]), ALU.is_equal)
                    ins.then_inc(eq_ok, 1)
                    dve.wait_ge(eq_ok, n + 1)
                    v.tensor_tensor(onehot, eq[0], eq[1], ALU.add).then_inc(hot_ok, 1)
                    v.tensor_scalar(rowid, rowid, float(BS), None, ALU.add).then_inc(row_ok, 1)

                fill_onehot(0)
                with dve.Fori(0, n_blocks, 1) as blk:
                    dve.wait_ge(gather_mm, blk + 1)
                    dve.wait_ge(row_ok, blk + 1)
                    dve.wait_ge(hot_ok, blk + 1)
                    fill_onehot(blk + 1)
                    dve.wait_ge(sg_ok, blk + 1)
                    v.tensor_tensor(aT.rearrange("p f s -> p (f s)"), sg, bank[2][:, 0:4 * BS], ALU.mult
                                    ).then_inc(a_ok, 1)
                    dve.wait_ge(down_mm, blk + 1)
                    dve.wait_ge(y_out, blk * 16)
                    v.tensor_copy(y_sb[0:BS, 512:1024], bank[4][0:BS, :]).then_inc(y_hi, 1)
                dve.wait_ge(mod_in_s, 32)
                for i in range(NC_LAT):
                    dve.wait_ge(yg_in[i], 32)
                    a, b = yg[2 * i], yg[2 * i + 1]
                    link(v.tensor_scalar(a, a, wtok[0][:, i:i + 1], None, ALU.mult))
                    link(v.scalar_tensor_tensor(a, b, wtok[1][:, i:i + 1], a, ALU.mult, ALU.add))
                    link(v.tensor_tensor(a, a, mod_out, ALU.mult))
                    v.tensor_tensor(a, a, xltok[:, i, :], ALU.add).then_inc(fin_ok_pre, 1)
                for i in range(NC_LAT):
                    dve.wait_ge(froot, i + 1)
                    dve.wait_ge(fin_ok_pre, i + 1)
                    link(v.reciprocal(ms[:, i:i + 1], ms[:, i:i + 1]))
                    v.scalar_tensor_tensor(yg[2 * i], yg[2 * i], ms[:, i:i + 1], g_last, ALU.mult, ALU.mult
                                           ).then_inc(fin_ok, 1)


_INS = ['x', 'c', 'ctx', 'c_ctx', 'w_ada', 'b_ada', 'g_norm_mix', 'g_norm_ffn', 'w_in', 'pool_w', 'pool_scale',
        'mlstm_conv_w', 'mlstm_conv_b', 'mlstm_gate_b', 'mlstm_norm_g', 'ssd_conv_w', 'ssd_conv_b',
        'ssd_dt_bias', 'ssd_a_log', 'ssd_d', 'ssd_norm_g', 'w_branch', 'w_out', 'w_route_group', 'b_route_group',
        'w_route_expert', 'b_route_expert', 'w_exp_gate', 'w_exp_up', 'w_exp_down', 'g_final']

_OUTS = [((1, T, D), 'float32')]


def kernel(**inputs):
    import numpy as _np
    import concourse.bacc as _bacc
    from concourse import mybir as _mybir
    from concourse.bass_utils import run_bass_kernel_spmd as _run

    nc = _bacc.Bacc("TRN2", target_bir_lowering=False, num_devices=1)
    arrays, args = {}, []
    for name in _INS:
        a = _np.ascontiguousarray(inputs[name])
        arrays[f"in_{name}_dram"] = a
        args.append(nc.dram_tensor(f"in_{name}_dram", a.shape, _mybir.dt.from_np(a.dtype), kind="ExternalInput").ap())
    for i, (shape, dtype) in enumerate(_OUTS):
        dt = _mybir.dt.from_np(_np.dtype(dtype))
        args.append(nc.dram_tensor(f"out_{i}_dram", shape, dt, kind="ExternalOutput").ap())
    build(nc, *args)
    r = _run(nc, [arrays], core_ids=[0])
    got = tuple(r.results[0][f"out_{i}_dram"] for i in range(len(_OUTS)))
    return got[0]
```

```python
import concourse.bass as bass
from concourse import mybir
from contextlib import ExitStack

D = 1024
T = 512
TC = 256
P = 128
KT = D // P
GRID_W = 64
GRID_H = T // GRID_W
NC_CTX = TC // P
NC_LAT = T // P
NC_ALL = NC_CTX + NC_LAT
HEADS = 4
HD = D // HEADS
SH = 16
SP_ = D // SH
SG_ = 4
SN = 128
HPG = SH // SG_
NE = 32
DE = 512
EPS = 1e-6
BIG = 1e30

COL_POOL, COL_Q, COL_K, COL_V, COL_O, COL_GA = 0, 1024, 2048, 3072, 4096, 5120
COL_SX = COL_GA + 16
COL_SZ = COL_SX + D
COL_SB = COL_SZ + D
COL_SC = COL_SB + SG_ * SN
COL_SDT = COL_SC + SG_ * SN
COL_MG = COL_SDT + 2 * SH

CH = 4096
NW = 2
NHI = 4
NCIN = 3
NCINC = 2
BS = 96
SUBS = -(-T // BS)
MAXB = 2 * T // BS + NE
SLICES = 12
NSL = 4
WIDE = 96
GST = 80
ADA_BANK = (4, 5, 6, 7, 0, 0, 4, 7)
Z_AT = ((0, 1, 2, 3), (4, 5), (6,), (7,))
Q_EXP = 5
Q_POOL = 6
NB = 4


def build(nc, x, c, ctx_in, c_ctx, w_ada, b_ada, g_norm_mix, g_norm_ffn, w_in, pool_w, pool_scale,
          mlstm_conv_w, mlstm_conv_b, mlstm_gate_b, mlstm_norm_g, ssd_conv_w, ssd_conv_b,
          ssd_dt_bias, ssd_a_log, ssd_d, ssd_norm_g, w_branch, w_out, w_route_group, b_route_group,
          w_route_expert, b_route_expert, w_exp_gate, w_exp_up, w_exp_down, g_final, out):
    f32 = mybir.dt.float32
    bf16 = mybir.dt.bfloat16
    ALU = mybir.AluOpType
    ACT = mybir.ActivationFunctionType
    AX = mybir.AxisListType

    def cols(w, c0):
        return w[0][:, c0:c0 + 512].rearrange("(k p) n -> p k n", p=P)

    chunks = [("ada", cols(w_ada, 512 * n)) for n in range(4)]
    for name, c0, n in (("k", COL_K, 2), ("q", COL_Q, 2), ("v", COL_V, 2), ("o", COL_O, 2)):
        chunks += [(name, cols(w_in, c0 + 512 * i)) for i in range(n)]

    def branch_chunks(b):
        got = [(f"mg{b}", cols(w_in, COL_MG + D * b + 512 * i)) for i in range(2)]
        return got + [(f"wb{b}", w_branch[0, b][:, 512 * i:512 * i + 512].rearrange("(k p) n -> p k n", p=P))
                      for i in range(2)]

    chunks += branch_chunks(1)
    for name, c0, n in (("B", COL_SB, 1), ("C", COL_SC, 1), ("x", COL_SX, 2), ("z", COL_SZ, 2)):
        chunks += [(name, cols(w_in, c0 + 512 * i)) for i in range(n)]
    chunks += branch_chunks(2)
    chunks += [("pa", cols(w_in, COL_POOL + 512 * i)) for i in range(2)]
    chunks += branch_chunks(0)
    chunks += [("wo", cols(w_out, 512 * i)) for i in range(2)]
    chunks += [("ada", cols(w_ada, 512 * n)) for n in range(10, 12)]
    first_chunk = {}
    for n, (name, _) in enumerate(chunks):
        first_chunk.setdefault(name, n)

    PIECES = (1,) * 8 + (1,) * 4 + (2,) * 4 + (1,) * 4
    N_PIECE = sum(PIECES)
    piece_at = [sum(PIECES[:t]) for t in range(len(PIECES) + 1)]

    stages = [("xT", 8, "V"), ("xTc", 8, "V"), ("k", 16, "A"), ("q", 8, "A"), ("v", 12, "A"),
              ("S", 24, "A"), ("o", 8, "A"), ("hT", 8, "V"), ("mg1", 8, "A"), ("wb1", 8, "V"),
              ("B", 8, "A"), ("BTr", 8, "V"), ("C", 4, "A"), ("x", 16, "A"), ("xTr", 16, "V"),
              ("z", 8, "A"), ("yT", 8, "V"), ("mg2", 8, "A"), ("wb2", 8, "V"),
              ("pa", 8, "A"), ("pw", 8, "A"), ("mg0", 8, "A"), ("wb0", 8, "V"), ("wo", 8, "V"),
              ("xtok", 8, "V"), ("htok", 8, "A")]
    items = []
    for name, n, e in stages:
        if name in ("BTr", "xTr", "mg2"):
            continue
        if name == "yT":
            items += [("mg2", i, "A") for i in range(4)] + [("yT", i, "V") for i in range(8)]
            items += [("mg2", i, "A") for i in range(4, 8)]
            continue
        if name in ("B", "x"):
            tr = "BTr" if name == "B" else "xTr"
            m_of = n // 2
            for m in range(m_of + 2):
                if m < m_of:
                    items += [(name, 2 * m, e), (name, 2 * m + 1, e)]
                if m >= 2:
                    items += [(tr, 2 * (m - 2), "V"), (tr, 2 * (m - 2) + 1, "V")]
        else:
            items += [(name, i, e) for i in range(n)]
    place = {(name, i): g for g, (name, i, e) in enumerate(items)}
    reads = {"A": 0, "V": 0}
    read_no = []
    for name, i, e in items:
        reads[e] += 1
        read_no.append((e, reads[e]))

    per_chunk = {"k": 8, "q": 4, "v": 6, "o": 4, "mg0": 4, "mg1": 4, "mg2": 4, "wb0": 4, "wb1": 4,
                 "wb2": 4, "B": 8, "C": 4, "x": 8, "z": 4, "pa": 4, "wo": 4}
    release = []
    seen = {}
    for name, _ in chunks:
        seen[name] = seen.get(name, 0) + 1
        if name == "ada":
            release.append(("ada", seen[name]))
        else:
            release.append(("gemm", place[(name, per_chunk[name] * seen[name] - 1)] + 1))

    units = [(name, m) for name in ("k", "q", "o", "mg1", "wb1", "B", "C", "x", "mg2", "wb2", "pa", "mg0", "wb0", "wo")
             for m in range(4 if name in ("B", "C") else KT)]
    unit_no = {key: u for u, key in enumerate(units)}

    def unit_end(u):
        name, m = units[u]
        return place[(name, 2 * m + 1 if name in ("k", "B", "x") else m)] + 1

    conv = []
    for m in range(8):
        conv += [("k", m, 0), ("k", m, 1)]
    conv += [("q", m, 0) for m in range(8)]
    for m in range(4):
        conv += [("B", m, 0), ("B", m, 1)]
    conv += [("C", m, 0) for m in range(4)]
    for m in range(8):
        conv += [("x", m, 0), ("x", m, 1)]
    conv_no = {t: n for n, t in enumerate(conv)}
    kind_no = []
    cnt = [0, 0]
    for s, m, cx in conv:
        kind_no.append(cnt[cx])
        cnt[cx] += 1

    def conv_before(n, slots):
        cx, no = conv[n][2], kind_no[n]
        if no < slots[cx]:
            return 0
        want = no - slots[cx]
        return next(i for i in range(len(conv)) if conv[i][2] == cx and kind_no[i] == want) + 1

    es = ExitStack()
    with es:
        def sb(name, shape):
            return es.enter_context(nc.sbuf_tensor(name, shape, f32))

        def sem(name):
            return es.enter_context(nc.semaphore(name))

        vec = sb("vec", [P, 3, P])
        csil = sb("csil", [P, KT, WIDE])
        ada = sb("ada", [P, 48, 2])
        modA = sb("modA", [P, 2, KT])
        modF = sb("modF", [P, KT])
        ident = sb("ident", [P, P])
        ones = sb("ones", [P, P])
        triu = sb("triu", [P, P])
        tril = sb("tril", [P, P])
        hide_past = sb("hide_past", [P, P])
        hide_next = sb("hide_next", [P, P])
        sel_last = sb("sel_last", [P, P])
        sel_first = sb("sel_first", [P, P])
        eps = sb("eps", [P, 1])
        gate_b = sb("gate_b", [P, 16])
        dt_b = sb("dt_b", [P, 32])
        a_log = sb("a_log", [P, 32])
        d_skip = sb("d_skip", [P, SH])
        ig = sb("ig", [P, NC_ALL, 8])
        lf = sb("lf", [P, 2 * NC_ALL, 8])
        ftot = sb("ftot", [P, NC_ALL, 8])
        fcum = sb("fcum", [P, NC_ALL, 8])
        bkey = sb("bkey", [P, NC_ALL, 8])
        em = sb("em", [P, NC_LAT, 8])
        dt = sb("dt", [P, 2, NC_ALL, SH])
        dta = sb("dta", [P, 2, NC_ALL, SH])
        acs = sb("acs", [P, 2, NC_ALL, SH])
        tot = sb("tot", [P, 2, NC_ALL, SH])
        e_in = sb("e_in", [P, 2, NC_ALL, SH])
        coef = sb("coef", [P, 2, NC_ALL, SH])
        den = sb("den", [P, 2])
        ms = sb("ms", [P, 16])
        inv_cnt = sb("inv_cnt", [P, 4, GRID_W])

        R0 = 18432

        def halves(name, at, *dims):
            at_pad = nc.sbuf_tensor(f"before_{name}", [P, at], f32) if at else ExitStack()
            with at_pad, nc.sbuf_tensor(name, [P, *dims], mybir.dt.float32r) as t:
                return t[tuple([slice(None)] * (1 + len(dims)))]

        slice_high = [halves(f"slice_high{j}", 28672 + 1024 * j, 2, 512) for j in range(NSL)]
        slice_low = [halves(f"slice_low{j}", 32768 + 1024 * j, 2, 512) for j in range(NSL)]
        xg_high = halves("xg_high", 36864, KT, BS)
        xg_low = halves("xg_low", 37632, KT, BS)
        aT_high = halves("aT_high", 38400, DE // P, BS)
        aT_low = halves("aT_low", 38784, DE // P, BS)
        w_high_all = halves("w_high", CH * NW, NHI, KT, P)
        w_high = [w_high_all[:, s] for s in range(NHI)]
        ring_low = [halves(f"ring_low{s}", CH * s, KT, 512) for s in range(NW)]
        br1_low = [t[:, j, :] for t in (halves("br1_low_a", R0 + 4096, KT // 2, T), halves("br1_low_b", R0 + 10240, KT // 2, T))
                   for j in range(KT // 2)]
        hT_low = halves("hT_low", 12288, KT, T)
        hTc_low = halves("hTc_low", 16384, KT, TC)
        merged_low = halves("merged_low", 44904, KT, T)
        h_high0 = halves("h_high0", R0 + 10240, KT, T)
        hc_high0 = halves("hc_high0", R0 + 14336, KT, TC)
        h_high1 = halves("h_high1", R0, KT, T)
        br1_high = halves("br1_high", R0 + 6144, KT, T)
        h_high3 = halves("h_high3", R0 + 13312, KT, T)
        hc_high3 = halves("hc_high3", R0 + 24424, KT, TC)
        h_high2 = [t[:, j, :] for t in (halves("h_high2_a", 16384, KT // 2, T), halves("h_high2_b", R0 + 22528, KT // 2, T))
                   for j in range(KT // 2)]
        br2_high = halves("br2_high", R0 + 8192, KT, T)
        br2_low = halves("br2_low", R0, KT, T)
        br0_low = halves("br0_low", R0, KT, T)
        br0_high = halves("br0_high", R0 + 8192, KT, T)
        merged_high = halves("merged_high", R0 + 20096, KT, T)
        arena = sb("arena", [P, 49000])

        def tiles(*at):
            each = KT // len(at)
            return [arena[:, a + T * j:a + T * j + T] for a in at for j in range(each)]

        def area(at, *dims):
            n = 1
            for d in dims:
                n *= d
            ap = arena[:, at:at + n]
            if len(dims) == 2:
                ap = ap.rearrange("p (a b) -> p a b", a=dims[0])
            if len(dims) == 3:
                ap = ap.rearrange("p (a b c) -> p a b c", a=dims[0], b=dims[1])
            return ap

        ring = [area(CH * s, KT, 512) for s in range(NW)]
        hT = area(12288, KT, T)
        hTc = area(16384, KT, TC)
        merged = area(44904, KT, T)
        xin = area(R0, NC_ALL, D)
        xT = area(R0 + 6144, KT, T)
        xTc = area(R0 + 10240, KT, TC)
        sq = area(R0 + 12288, KT, T)
        sqc = area(R0 + 16384, KT, TC)
        rn = area(R0 + 18432, T + TC)
        vec_rows = area(R0 + 19200, 3, P)
        w_small = area(R0 + 24000, KT, WIDE)
        kT = area(R0, KT, T + TC)
        qT = area(R0 + 6144, KT, T)
        hsum = area(R0 + 6144, HEADS, NC_LAT, HD)
        vone = area(R0 + 10240, NC_ALL, HEADS * (HD + 1))
        scores = area(R0 + 16408, NC_ALL, T)
        attn = [area(R0 + 19480 + 3072 * s, NC_ALL, T) for s in range(2)]
        mrow = [area(R0 + 25624 + 1024 * s, 2, T) for s in range(2)]
        diag = [area(R0 + 27672 + 512 * s, NC_LAT, P) for s in range(2)]
        cin_m = area(R0 + 16408, NCIN, 515)
        cinc_m = area(R0 + 17953, NCINC, 259)
        acc_m = area(R0 + 18472, 3, T)
        gx = area(R0 + 20100, 240)
        gabs = area(R0 + 20340, 240)
        gexp = area(R0 + 20580, 240)
        gu = area(R0 + 20820, 240)
        gl = area(R0 + 21060, 240)
        gd_ = area(R0 + 21300, 240)
        expa = area(R0 + 21540, 32)
        brow = area(R0 + 21600, 2, T + TC)
        mx = area(R0 + 23200, 2, T + TC)
        hcm = area(R0 + 24800, KT, T)
        zero_src = area(47400, D)
        sig_o = area(R0 + 21624, KT, T)
        br1 = tiles(R0 + 4096, R0 + 10240)
        gate1 = area(R0 + 17408, KT, T)
        xtok = area(R0, NC_ALL, D)
        BT = area(R0 + 6144, SG_, T)
        Btok = area(R0 + 8192, NC_ALL, SG_ * SN)
        CT = area(R0 + 11264, SG_, T)
        ytok = area(R0 + 13312, NC_LAT, D)
        cin_s = area(R0 + 17408, NCIN, 515)
        cinc_s = area(R0 + 18953, NCINC, 259)
        acc_s = area(R0 + 19472, 3, T)
        xst = area(R0 + 21008, 3, T + TC)
        rowa = area(R0 + 23400, 2, T)
        decay = [area(R0 + 17408 + 4096 * s, 2, SH, P) for s in range(2)]
        state = area(R0 + 17408, 2, D)
        xw = area(R0 + 19456, 2, D)
        ytmp = area(R0 + 21504, 2, D)
        zbuf = area(CH * NW, NC_LAT, D)
        neg_acs = area(R0 + 25600, 2, NC_ALL, SH)
        junk = area(R0 + 18500, D)
        br2 = area(R0, KT, T)
        gate2 = area(R0 + 4096, KT, T)
        pooled = area(R0 + 8192, KT, T)
        pw_sb = area(R0 + 20480, 2, 4, 256)
        PR = GRID_W + 16
        ppad = area(R0 + 12288, 2, GRID_H * PR)
        psum_a = area(R0 + 13568, GRID_H * PR)
        psum_b = area(R0 + 14208, GRID_H * PR)
        br0 = area(R0, KT, T)
        gate0 = area(R0 + 4096, KT, T)
        xl = area(R0 + 15960, KT, T)
        prod2 = area(R0 + 14900, 2, T)

        slot6 = [area(CH * s, CH) for s in range(6)]
        sq2 = area(24576, KT, T)
        rn2 = area(28672, T)
        h2T = area(29184, KT, T)
        h2tok = area(33280, NC_LAT, D)
        onehot = arena[:, 39168:39168 + NC_LAT * BS // 2].bitcast(bf16).rearrange("p (i s) -> p i s", i=NC_LAT)
        act_tok = area(44152, DE)
        rowid = area(39360, BS)
        y_sb = area(39456, D)
        piece_in = [area(at, KT, P) for at in (R0 + 15960, R0 + 16984, R0 + 18008)]
        piece_sum = area(R0 + 25600, 2, P)
        w_route = area(33280, KT, WIDE)
        b_route = area(38492, 36)
        parts = [arena[:, at:at + 2048].bitcast(bf16).rearrange("p (i n) -> p i n", i=NC_LAT)
                 for at in (24576, 26624, 40544)]
        eq = [area(43200 + 384 * j, NC_LAT, BS) for j in range(2)]
        xltok = area(44904, NC_LAT, D)
        mod_out = area(32768, D)
        g_last = area(33792, D)
        TMP = 42600
        logit = area(TMP, NC_LAT, 36)
        gsc = area(TMP + 144, NC_LAT, 4)
        ghot = area(TMP + 160, NC_LAT, 4)
        gmax = area(TMP + 176, NC_LAT)
        pgrp = area(TMP + 180, NC_LAT)
        lsel = area(TMP + 184, NC_LAT, 8)
        hot = [area(TMP + 216 + 32 * j, NC_LAT, 8) for j in range(2)]
        top = [area(TMP + 280 + 4 * j, NC_LAT) for j in range(2)]
        wtok = [area(TMP + 288 + 4 * j, NC_LAT) for j in range(2)]
        etmp = area(TMP + 296, NC_LAT)
        rtmp = area(TMP + 300, NC_LAT, 8)
        rmax = area(TMP + 332, NC_LAT)
        rev = area(TMP + 336, 8)
        strict = area(TMP + 344, P)
        lmul = area(TMP + 472, NC_LAT * 4, 8)
        member = [area(TMP + 600 + 128 * j, NC_LAT, NE) for j in range(2)]
        both = area(TMP + 856, NC_LAT, NE)
        row = area(TMP + 984, NC_LAT, NE)
        thr = area(TMP + 1240, NE, SUBS - 1)
        nblk = area(TMP + 1464, NE)
        cumx = area(TMP + 1496, NE + 1)
        idxf = area(TMP + 1530, 8)
        ptmp = area(TMP + 1540, NC_LAT, NE)
        mtot = area(TMP + 1668, NC_LAT, NE)
        yg = [area(24576 + 1024 * j, D) for j in range(8)]
        table = es.enter_context(nc.sbuf_tensor("table", [1, NE + 1], mybir.dt.int32))
        idx = es.enter_context(nc.sbuf_tensor("idx", [P, 8], mybir.dt.uint32))

        bank = [es.enter_context(nc.psum_tensor(f"bank{i}", [P, 512], f32)) for i in range(8)]

        x_scr = nc.dram_tensor("x_scr", [P, KT * T], f32, kind="Internal").ap()
        m_scr = nc.dram_tensor("m_scr", [HEADS, 2, T], f32, kind="Internal").ap()
        a_scr = nc.dram_tensor("a_scr", [2, SH, T], f32, kind="Internal").ap()

        y_scr = nc.dram_tensor("y_scr", [MAXB + 1, BS, D], f32, kind="Internal").ap()
        mod_scr = nc.dram_tensor("mod_scr", [D], f32, kind="Internal").ap()
        sq2_ok, stat2, root2, normed2, h2_ok, route_in, route_mm = (
            sem("sq2_ok"), sem("stat2"), sem("root2"), sem("normed2"), sem("h2_ok"), sem("route_in"), sem("route_mm"))
        gexp_pre, gexp_ok, topexp_pre, topexp_ok, member_ok, pos_mm, table_ok, iota_ok, idx_ok = (
            sem("gexp_pre"), sem("gexp_ok"), sem("topexp_pre"), sem("topexp_ok"), sem("member_ok"), sem("pos_mm"),
            sem("table_ok"), sem("iota_ok"), sem("idx_ok"))
        expert_in = [sem(f"expert_in{s}") for s in range(6)]
        split_lo, split_mid = sem("split_lo"), sem("split_mid")
        eq_ok, row_ok = sem("eq_ok"), sem("row_ok")
        ada2_read, split_ok, split_hi, blocks_done = (
            sem("ada2_read"), sem("split_ok"), sem("split_hi"), sem("blocks_done"))
        slice_hi, slice_lo, slice_mm, xg_hi, xg_lo, a_tr, a_hi = (
            sem("slice_hi"), sem("slice_lo"), sem("slice_mm"), sem("xg_hi"), sem("xg_lo"), sem("a_tr"), sem("a_hi"))
        hot_ok, gather_mm, sg_ok, a_ok, a_lo, y_lo, y_hi, y_out = (
            sem("hot_ok"), sem("gather_mm"), sem("sg_ok"), sem("a_ok"), sem("a_lo"),
            sem("y_lo"), sem("y_hi"), sem("y_out"))
        fin_ok_pre = sem("fin_ok_pre")
        mod_out_s, mod_in_s, yg_in, froot, fin_ok = (
            sem("mod_out_s"), sem("mod_in_s"), [sem(f"yg_in{j}") for j in range(4)], sem("froot"), sem("fin_ok"))

        chunk_in = [sem(f"chunk_in{s}") for s in range(NW)]
        vec_in, x_in, ctxin_in, small_in = sem("vec_in"), sem("x_in"), sem("ctxin_in"), sem("small_in")
        y_zero = sem("y_zero")
        consts, filled = sem("consts"), sem("filled")
        gemm_done = sem("gemm_done")
        act_read = sem("act_read")
        dve_read = sem("dve_read")
        ada_done, vec_tr, vec_sb, csil_ok = sem("ada_done"), sem("vec_tr"), sem("vec_sb"), sem("csil_ok")
        squares, stat_done, norm_root, normed, modA_ok, h_ok = (
            sem("squares"), sem("stat_done"), sem("norm_root"), sem("normed"), sem("modA_ok"), sem("h_ok"))
        x_spill = sem("x_spill")
        pads = sem("pads")
        gates_mm, gates_pre, gates_exp, gates_u, gates_ln, lf_ok, bkey_ok = (
            sem("gates_mm"), sem("gates_pre"), sem("gates_exp"), sem("gates_u"),
            sem("gates_ln"), sem("lf_ok"), sem("bkey_ok"))
        cum_mm, cum_read, tot_mm = sem("cum_mm"), sem("cum_read"), sem("tot_mm")
        brow_tr, mx_ok, mback_tr, em_sum, em_ok, m_out, m_bc = (
            sem("brow_tr"), sem("mx_ok"), sem("mback_tr"), sem("em_sum"), sem("em_ok"),
            sem("m_out"), [sem("m_bc0"), sem("m_bc1")])
        ssd_pre, ssd_exp, coef_ok = sem("ssd_pre"), sem("ssd_exp"), sem("coef_ok")
        conv_done, silu_done = sem("conv_done"), sem("silu_done")
        wexp, wmul, av_done, av_read, diag_ok = (
            sem("wexp"), sem("wmul"), sem("av_done"), sem("av_read"), sem("diag_ok"))
        hroot, hnorm = sem("hroot"), sem("hnorm")
        arow_tr, arow_ok, arow_out = sem("arow_tr"), sem("arow_ok"), sem("arow_out")
        dec_in = [sem("dec_in0"), sem("dec_in1")]
        dmask, neg_ok, dexp, dmul, g_mm, intra_mm, y_ok = (
            sem("dmask"), sem("neg_ok"), sem("dexp"), sem("dmul"), sem("g_mm"), sem("intra_mm"), sem("y_ok"))
        xw_ok, cs_mm, st_ok, inter_mm, inter_read, inter_add = (
            sem("xw_ok"), sem("cs_mm"), sem("st_ok"), sem("inter_mm"), sem("inter_read"), sem("inter_add"))
        yz_ok, yroot, ynorm = sem("yz_ok"), sem("yroot"), sem("ynorm")
        pool_ok, pw_in, prod_ok, xl_in = (
            sem("pool_ok"), sem("pw_in"), sem("prod_ok"), sem("xl_in"))
        w_hi, w_lo, op_hi, op_lo, h_back = sem("w_hi"), sem("w_lo"), sem("op_hi"), sem("op_lo"), sem("h_back")
        hcm_ok, piece_mm, piece_ok = sem("hcm_ok"), sem("piece_mm"), sem("piece_ok")
        piece_ld = [sem(f"piece_ld{j}") for j in range(3)]
        h_low, ones_col, h_moved = sem("h_low"), sem("ones_col"), sem("h_moved")
        vlink, alink, plink = sem("vlink"), sem("alink"), sem("plink")
        out_done = sem("out_done")

        block = es.enter_context(nc.Block())

        def freed(eng, g):
            if g >= NB:
                e, n = read_no[g - NB]
                eng.wait_ge(act_read if e == "A" else dve_read, n)

        def arrived(eng, n):
            eng.wait_ge(chunk_in[n % NW], 16 * (n // NW + 1))

        def linker(eng, s):
            count = [0]

            def link(ins):
                count[0] += 1
                ins.then_inc(s, 1)
                eng.wait_ge(s, count[0])
            return link

        def colmajor(ap):
            return ap.rearrange("p (r w) -> p w r", r=GRID_H)

        def bk(g):
            return bank[g % NB]

        def raw_tile(u, of=ring):
            name, m = units[u]
            return of[(first_chunk[name] + m // 4) % NW][:, :, P * (m % 4):P * (m % 4) + P]

        VEC_ROWS = [[(b_ada[0], 48), (c[0], 8), (c_ctx, 8), (g_norm_mix[0], 8), (g_norm_ffn[0], 8),
                     (pool_scale[0], 8), (mlstm_norm_g[0], 8), (ssd_norm_g[0], 8), (g_final, 8)],
                    [(mlstm_conv_w[0].rearrange("j n -> (j n)"), 64), (mlstm_conv_b[0], 16)],
                    [(ssd_conv_w[0].rearrange("j n -> (j n)"), 64), (ssd_conv_b[0], 16)]]
        n_rows = [sum(n for _, n in part) for part in VEC_ROWS]
        n_vec = sum(len(part) for part in VEC_ROWS)
        V_BADA, V_C, V_GMIX, V_GFFN, V_PS, V_MG, V_SG, V_GF = 0, 48, 64, 72, 80, 88, 96, 104

        @block.sync
        def _(sp):
            for part, rows in enumerate(VEC_ROWS):
                at = 0
                for v, n in rows:
                    sp.dma_start(vec_rows[at:at + n, part, :], v.rearrange("(j p) -> j p", p=P)).then_inc(vec_in, 16)
                    at += n
            sp.dma_start(xin[:, NC_CTX:, :], x[0].rearrange("(t p) n -> p t n", p=P)).then_inc(x_in, 16)
            sp.dma_start(xin[:, 0:NC_CTX, :], ctx_in[0].rearrange("(t p) n -> p t n", p=P)).then_inc(ctxin_in, 16)
            for n, (name, src) in enumerate(chunks):
                if n >= NW:
                    kind, v = release[n - NW]
                    sp.wait_ge(ada_done if kind == "ada" else gemm_done, v)
                sp.dma_start(ring[n % NW], src).then_inc(chunk_in[n % NW], 16)

            def expert_loads(e, par):
                return [(3 * (1 - par) + j, src, kk) for j, (src, kk) in enumerate(
                    ((w_exp_gate[0][e], KT), (w_exp_up[0][e], KT), (w_exp_down[0][e], DE // P)))]

            sp.wait_ge(dve_read, read_no[place[("wb0", 7)]][1])
            for s, src, kk in expert_loads(0, 0):
                sp.dma_start(slot6[s].rearrange("p (k n) -> p k n", k=kk), src.rearrange("(k p) n -> p k n", p=P)
                             ).then_inc(expert_in[s], 16)
            sp.wait_ge(gemm_done, place[("wo", 7)] + 1)
            sp.wait_ge(ada_done, 6)
            for s, src, kk in expert_loads(1, 1):
                sp.dma_start(slot6[s].rearrange("p (k n) -> p k n", k=kk), src.rearrange("(k p) n -> p k n", p=P)
                             ).then_inc(expert_in[s], 16)
            sp.wait_ge(table_ok, 1)
            with sp.Fori(1, NE // 2, 1) as ep:
                for par in range(2):
                    before = sp.value_load(table[0:1, bass.ds(2 * ep + (par - 1), 1)], min_val=1, max_val=MAXB)
                    for j, (s, src, kk) in enumerate(expert_loads(2 * ep + par, par)):
                        if j == 2:
                            sp.wait_ge(xg_lo, before * 2 + 2)
                        else:
                            sp.wait_ge(gather_mm, before * 2 + 1)
                        sp.dma_start(slot6[s].rearrange("p (k n) -> p k n", k=kk), src.rearrange("(k p) n -> p k n", p=P)
                                     ).then_inc(expert_in[s], 16)

        @block.gpsimd
        def _(pool):
            link = linker(pool, plink)
            g = nc.gpsimd

            def low_weights(name, lo, hi):
                for m in range(lo, hi):
                    u = unit_no[(name, m)]
                    pool.wait_ge(w_hi, u + 1)
                    g.tensor_tensor(raw_tile(u, ring_low), raw_tile(u), w_high[u % NHI].bitcast(f32), ALU.subtract).then_inc(w_lo, 1)

            def low_operand(n, whole, low, high, lo=0, hi=KT):
                for m in range(lo, hi):
                    pool.wait_ge(op_hi, 8 * n + m + 1)
                    whole_m, low_m, high_m = (ap[m] if isinstance(ap, list) else ap[:, m, :] for ap in (whole, low, high))
                    g.tensor_tensor(low_m, whole_m, high_m.bitcast(f32), ALU.subtract).then_inc(op_lo, 1)
            link(g.memset(w_small, 0.0))
            g.memset(csil[:, :, :], 0.0).then_inc(filled, 1)
            g.memset(lf[:, :, :], 0.0).then_inc(filled, 1)
            pool.dma_start(w_small[:, :, 0:16],
                           w_in[0][:, COL_GA:COL_GA + 16].rearrange("(k p) n -> p k n", p=P)).then_inc(small_in, 16)
            pool.dma_start(w_small[:, :, 16:48],
                           w_in[0][:, COL_SDT:COL_SDT + 32].rearrange("(k p) n -> p k n", p=P)).then_inc(small_in, 16)
            pool.dma_start(gate_b[:, :], mlstm_gate_b[0].rearrange("a h -> (a h)").partition_broadcast(P)).then_inc(small_in, 16)
            pool.dma_start(dt_b[:, :], ssd_dt_bias[0].rearrange("a h -> (a h)").partition_broadcast(P)).then_inc(small_in, 16)
            pool.dma_start(a_log[:, :], ssd_a_log[0].rearrange("a h -> (a h)").partition_broadcast(P)).then_inc(small_in, 16)
            pool.dma_start(d_skip[:, :], ssd_d[0].partition_broadcast(P)).then_inc(small_in, 16)
            g.memset(ident[:, :], 0.0).then_inc(filled, 1)
            g.memset(ones[:, :], 1.0).then_inc(filled, 1)
            g.memset(hide_past[:, :], 0.0).then_inc(filled, 1)
            g.memset(hide_next[:, :], 0.0).then_inc(filled, 1)
            pool.wait_ge(filled, 6)

            def sel(dst, src, op, fill, base, step, mul):
                g.affine_select(out=dst[:, :], in_=src[:, :], compare_op=op, fill=fill, base=base,
                                pattern=[[step, P]], channel_multiplier=mul).then_inc(consts, 1)
            sel(ident, ident, ALU.not_equal, 1.0, 0, -1, 1)
            sel(triu, ones, ALU.is_ge, 0.0, 0, 1, -1)
            sel(tril, ones, ALU.is_ge, 0.0, 0, -1, 1)
            sel(hide_past, hide_past, ALU.is_ge, BIG, 0, 1, -1)
            sel(hide_next, hide_next, ALU.is_ge, BIG, 0, -1, 1)
            sel(sel_last, ones, ALU.is_equal, 0.0, -(P - 1), 0, 1)
            sel(sel_first, ones, ALU.is_equal, 0.0, 0, 0, 1)
            g.memset(eps[:, :], EPS).then_inc(consts, 1)
            link(g.memset(zero_src, 0.0))
            for j in range(NE + 1, MAXB + 1):
                pool.dma_start(y_scr[j], zero_src[0:BS, :]).then_inc(y_zero, 16)
            for gi, w in enumerate((2, 4, 8, 16)):
                link(g.memset(inv_cnt[:, gi, :], 1.0 / w))
                for t in list(range(w // 2)) + list(range(GRID_W - w // 2 + 1, GRID_W)):
                    lo, hi = max(t - w // 2, 0), min(t - w // 2 + w - 1, GRID_W - 1)
                    g.memset(inv_cnt[:, gi, t:t + 1], 1.0 / (hi - lo + 1))
            pool.wait_ge(y_zero, 16 * (MAXB - NE))
            pool.wait_ge(dve_read, 8)
            pool.dma_start(x_scr, area(R0 + 6144, KT * T)).then_inc(x_spill, 16)
            pool.wait_ge(x_spill, 16)
            pool.wait_ge(h_ok, 16)
            pool.wait_ge(hcm_ok, 8)
            g.memset(cin_m[:, :, 0:2], 0.0).then_inc(pads, 1)
            g.memset(cin_m[:, :, 514:515], 0.0).then_inc(pads, 1)
            g.memset(cinc_m[:, :, 0:2], 0.0).then_inc(pads, 1)
            g.memset(cinc_m[:, :, 258:259], 0.0).then_inc(pads, 1)
            low_weights("k", 0, 8)
            low_weights("q", 0, 8)
            pool.wait_ge(h_back, 1)
            g.memset(vone.rearrange("p c (h e) -> p (c h) e", h=HEADS)[:, :, HD:HD + 1], 1.0).then_inc(ones_col, 1)
            pool.wait_ge(mx_ok, 1)
            pool.dma_start(m_scr, mx[0:HEADS, :, TC:]).then_inc(m_out, 16)
            pool.wait_ge(m_out, 16)
            pool.wait_ge(gemm_done, place[("v", 11)] + 1)
            for h in range(HEADS):
                if h >= 2:
                    pool.wait_ge(wexp, 12 * (h - 1))
                    pool.wait_ge(diag_ok, 2 * (h - 1))
                pool.dma_start(mrow[h % 2], m_scr[h].partition_broadcast(P)).then_inc(m_bc[h % 2], 16)
                pool.wait_ge(m_bc[h % 2], 16 * (h // 2 + 1))
                for d in range(2):
                    u = 2 * h + d
                    if u >= 2:
                        pool.wait_ge(wexp, 6 * (u - 1))
                    mask = (hide_past, hide_next)[d]
                    g.tensor_tensor(diag[d], mrow[h % 2][:, d, :].rearrange("p (i t) -> p i t", i=NC_LAT),
                                    mask[:, None, :].to_broadcast([P, NC_LAT, P]), ALU.add).then_inc(diag_ok, 1)
            low_operand(0, hT, hT_low, h_high1)
            low_weights("o", 0, 8)
            low_weights("mg1", 0, 4)
            low_operand(1, br1, br1_low, br1_high)
            low_weights("mg1", 4, 8)
            low_weights("wb1", 0, 8)
            low_weights("B", 0, 3)
            pool.wait_ge(dve_read, read_no[place[("wb1", 7)]][1])
            g.memset(cin_s[:, :, 0:2], 0.0).then_inc(pads, 1)
            g.memset(cin_s[:, :, 514:515], 0.0).then_inc(pads, 1)
            g.memset(cinc_s[:, :, 0:2], 0.0).then_inc(pads, 1)
            g.memset(cinc_s[:, :, 258:259], 0.0).then_inc(pads, 1)
            low_weights("B", 3, 4)
            low_weights("C", 0, 4)
            low_weights("x", 0, 4)
            pool.wait_ge(arow_ok, 2)
            pool.dma_start(a_scr.rearrange("d h t -> h d t"), rowa[0:SH, :, :]).then_inc(arow_out, 16)
            pool.wait_ge(arow_out, 16)
            low_weights("x", 4, 8)
            for i in range(NC_LAT):
                if i == 0:
                    pool.wait_ge(dve_read, read_no[place[("xTr", 15)]][1])
                if i >= 2:
                    pool.wait_ge(intra_mm, i - 1)
                pool.dma_start(decay[i % 2].rearrange("p d h t -> p (d h) t"),
                               a_scr.rearrange("d h t -> (d h) t")[:, i * P:i * P + P].partition_broadcast(P)
                               ).then_inc(dec_in[i % 2], 16)
                pool.wait_ge(dec_in[i % 2], 16 * (i // 2 + 1))
                for d in range(2):
                    mask = (hide_past, hide_next)[d]
                    g.tensor_tensor(decay[i % 2][:, d], decay[i % 2][:, d], mask[:, None, :].to_broadcast([P, SH, P]),
                                    ALU.subtract).then_inc(dmask, 1)
            pool.wait_ge(intra_mm, 4)
            for n in range(10):
                d, step = n % 2, n // 2
                cc = ([0, 1, 2, 3, 4], [1, 0, 5, 4, 3])[d][step]
                if n >= 2:
                    pool.wait_ge(cs_mm, n - 1)
                g.tensor_tensor(xw[:, d].rearrange("p (h e) -> p h e", h=SH),
                                xtok[:, cc, :].rearrange("p (h e) -> p h e", h=SH),
                                coef[:, d, cc, :, None].to_broadcast([P, SH, SP_]), ALU.mult).then_inc(xw_ok, 1)
            low_operand(2, hT, hT_low, h_high2)
            low_weights("mg2", 0, 8)
            low_operand(3, br2, br2_low, br2_high)
            low_weights("wb2", 0, 8)
            low_weights("pa", 0, 4)
            pool.wait_ge(prod_ok, 8)
            g.memset(area(R0 + 12288, 2 * GRID_H * PR), 0.0).then_inc(pads, 1)
            for j in range(2):
                pool.dma_start(pw_sb[:, j], pool_w[0][:, P * j:P * j + P, :].rearrange("g p n -> p g n")
                               ).then_inc(pw_in, 16)
            low_weights("pa", 4, 8)
            low_weights("mg0", 0, 4)
            low_operand(4, br0, br0_low, br0_high)
            low_weights("mg0", 4, 8)
            low_weights("wb0", 0, 8)
            low_operand(5, merged, merged_low, merged_high, 0, 5)
            low_weights("wo", 0, 1)
            low_operand(5, merged, merged_low, merged_high, 5, 7)
            low_weights("wo", 1, 2)
            low_operand(5, merged, merged_low, merged_high, 7, 8)
            low_weights("wo", 2, 3)
            pool.wait_ge(piece_ok, N_PIECE)
            pool.dma_start(xl, x_scr.rearrange("p (k t) -> p k t", k=KT)).then_inc(xl_in, 16)
            pool.wait_ge(prod_ok, 16)
            link(g.memset(w_route, 0.0))
            pool.dma_start(w_route[:, :, 0:4], w_route_group[0].rearrange("(k p) n -> p k n", p=P)).then_inc(route_in, 16)
            pool.dma_start(w_route[:, :, 4:36], w_route_expert[0].rearrange("(k p) n -> p k n", p=P)).then_inc(route_in, 16)
            pool.dma_start(b_route[:, 0:4], b_route_group[0].partition_broadcast(P)).then_inc(route_in, 16)
            pool.dma_start(b_route[:, 4:36], b_route_expert[0].partition_broadcast(P)).then_inc(route_in, 16)
            low_weights("wo", 3, 8)
            pool.wait_ge(dve_read, read_no[place[("wo", 7)]][1])
            g.iota(rowid, pattern=[[1, BS]], base=0, channel_multiplier=0,
                   allow_small_or_imprecise_dtypes=True).then_inc(iota_ok, 1)
            pool.wait_ge(ada2_read, 3)
            pool.dma_start(mod_scr.rearrange("(k p) -> p k", p=P), ada[:, 40:48, 0], allow_slow_non_contiguous=True).then_inc(mod_out_s, 16)
            for q in range(8 + Q_POOL):
                if q < 8:
                    i, at = q // 2, slice(512 * (q % 2), 512 * (q % 2) + 512)
                    pool.wait_ge(split_hi, q + 1)
                    g.tensor_tensor(h2tok[:, i, at], h2tok[:, i, at], parts[0][:, i, at], ALU.subtract).then_inc(split_lo, 1)
                else:
                    i, at = (q - 8) // 2, slice(512 * (q % 2), 512 * (q % 2) + 512)
                    pool.wait_ge(split_mid, q - 7)
                    g.tensor_tensor(parts[2][:, i, at], h2tok[:, i, at], parts[1][:, i, at], ALU.subtract).then_inc(split_ok, 1)
            pool.wait_ge(mod_out_s, 16)
            pool.wait_ge(blocks_done, 1)
            pool.wait_ge(idx_ok, 1)
            pool.dma_start(mod_out, mod_scr.partition_broadcast(P)).then_inc(mod_in_s, 16)
            pool.dma_start(g_last, g_final.partition_broadcast(P)).then_inc(mod_in_s, 16)
            for i in range(NC_LAT):
                for j in range(2):
                    g.indirect_dma_start(out=yg[2 * i + j], out_offset=None, in_=y_scr.rearrange("b s d -> (b s) d"),
                                         in_offset=bass.IndirectOffsetOnAxis(ap=idx[:, 2 * i + j:2 * i + j + 1], axis=0),
                                         bounds_check=(MAXB + 1) * BS - 1).then_inc(yg_in[i], 16)
            for i in range(NC_LAT):
                pool.wait_ge(fin_ok, i + 1)
                pool.dma_start(out[0][P * i:P * i + P, :], yg[2 * i]).then_inc(out_done, 16)
            pool.wait_ge(out_done, 16 * NC_LAT)

        @block.tensor
        def _(pe):
            mm, tr = nc.tensor.matmul, nc.tensor.transpose

            def last_of(ins, s):
                ins.then_inc(s, 1)

            pe.wait_ge(consts, 8)
            pe.wait_ge(vec_in, 16 * n_vec)
            for part in range(3):
                ins = tr(bank[7][:, P * part:P * part + n_rows[part]], vec_rows[0:n_rows[part], part, :],
                         ident[0:n_rows[part], 0:n_rows[part]])
            last_of(ins, vec_tr)
            pe.wait_ge(x_in, 16)
            for m in range(KT):
                gi = place[("xT", m)]
                freed(pe, gi)
                for i in range(NC_LAT):
                    ins = tr(bk(gi)[:, P * i:P * i + P], xin[:, NC_CTX + i, P * m:P * m + P], ident[:, :])
                last_of(ins, gemm_done)
            pe.wait_ge(ctxin_in, 16)
            for m in range(KT):
                gi = place[("xTc", m)]
                freed(pe, gi)
                for i in range(NC_CTX):
                    ins = tr(bk(gi)[:, P * i:P * i + P], xin[:, i, P * m:P * m + P], ident[:, :])
                last_of(ins, gemm_done)
            pe.wait_ge(squares, 16)
            for m in range(KT):
                ins = mm(bank[5][:, :], ones[:, :], sq[:, m, :], start=m == 0, stop=m == KT - 1)
            last_of(ins, stat_done)
            for m in range(KT):
                ins = mm(bank[6][:, 0:TC], ones[:, :], sqc[:, m, :], start=m == 0, stop=m == KT - 1)
            last_of(ins, stat_done)
            def modulation(n, chunk):
                arrived(pe, chunk)
                for j in range(4):
                    for k in range(KT):
                        ins = mm(bank[ADA_BANK[n]][:, WIDE * j:WIDE * j + WIDE], ring[chunk % NW][:, k, P * j:P * j + P],
                                 csil[:, k, :], start=k == 0, stop=k == KT - 1)
                last_of(ins, ada_done)

            pe.wait_ge(csil_ok, 1)
            pe.wait_ge(norm_root, 2)
            for n in range(4):
                modulation(n, n)
            pe.wait_ge(h_ok, 16)
            pe.wait_ge(small_in, 16 * 6)
            for cc in range(NC_ALL):
                if cc == NC_CTX:
                    pe.wait_ge(hcm_ok, 8)
                for part, b in enumerate((5, 6)):
                    for k in range(KT):
                        if cc < NC_CTX:
                            tok = hTc[:, k, P * cc:P * cc + P]
                        elif part == 0:
                            tok = hcm[:, k, P * (cc - 2):P * (cc - 2) + P]
                        else:
                            tok = hT[:, k, P * (cc - 2):P * (cc - 2) + P]
                        ins = mm(bank[b][:, GST * cc:GST * cc + WIDE], tok, w_small[:, k, :],
                                 start=k == 0, stop=k == KT - 1)
            last_of(ins, gates_mm)

            def tile_w3(name, m, high, low, idx=None, n_tok=T, ready=None):
                u, gi = unit_no[(name, m)], place[(name, m if idx is None else idx)]
                pe.wait_ge(w_lo, u + 1)
                freed(pe, gi)
                w_h, w_l = w_high[u % NHI], raw_tile(u, ring_low)
                for k in range(KT):
                    if ready is not None:
                        pe.wait_ge(h_low, ready + k + 1)
                    for j, (a, b) in enumerate(((w_h, high), (w_h, low), (w_l, high))):
                        b = b[k] if isinstance(b, list) else b[:, k, :]
                        ins = mm(bk(gi)[:, 0:n_tok], a[:, k, :], b,
                                 start=k + j == 0, stop=(k, j) == (KT - 1, 2))
                last_of(ins, gemm_done)

            for m in range(KT):
                tile_w3("k", m, h_high0, hT_low, 2 * m, ready=0 if m == 0 else None)
                tile_w3("k", m, hc_high0, hTc_low, 2 * m + 1, TC, ready=KT if m == 0 else None)
            pe.wait_ge(lf_ok, 2)
            for j, w in enumerate((triu, tril, ones)):
                ins = mm(bank[4][:, WIDE * j:WIDE * j + WIDE], w[:, :], lf[:, :, :].rearrange("p c h -> p (c h)"),
                         start=True, stop=True)
            for d in range(2):
                ins = mm(bank[7][:, 96 * d:96 * d + 96], (triu, tril)[d][:, :], dta[:, d].rearrange("p c h -> p (c h)"),
                         start=True, stop=True)
            last_of(ins, cum_mm)
            for m in range(KT):
                tile_w3("q", m, h_high0, hT_low)
                if m == 1:
                    pe.wait_ge(cum_read, 1)
                    for d in range(2):
                        ins = mm(bank[7][:, 192 + 96 * d:288 + 96 * d], (sel_last, sel_first)[d][:, :],
                                 acs[:, d].rearrange("p c h -> p (c h)"), start=True, stop=True)
                    last_of(ins, tot_mm)
                    pe.wait_ge(bkey_ok, 1)
                    for d in range(2):
                        for cc in range(NC_ALL):
                            to = (bank[4][0:HEADS, P * (2 * d + cc):P * (2 * d + cc) + P] if cc < NC_CTX else
                                  bank[5 + d][0:HEADS, P * (cc - 2):P * (cc - 2) + P])
                            ins = tr(to, bkey[:, cc, 4 * d:4 * d + 4], ident[:, :])
                    last_of(ins, brow_tr)
            for m in range(12):
                half, cc = m // NC_ALL, (m + NC_CTX) % NC_ALL
                n = first_chunk["v"] + half
                gi = place[("v", m)]
                arrived(pe, n)
                freed(pe, gi)
                if m == NC_LAT:
                    pe.wait_ge(h_back, 1)
                for k in range(KT):
                    tok = (hTc[:, k, P * cc:P * cc + P] if cc < NC_CTX else
                           hcm[:, k, P * (cc - 2):P * (cc - 2) + P])
                    ins = mm(bk(gi)[:, :], tok, ring[n % NW][:, k, :], start=k == 0, stop=k == KT - 1)
                last_of(ins, gemm_done)
                if m == 5:
                    pe.wait_ge(mx_ok, 1)
                    for i in range(NC_LAT):
                        for d in range(2):
                            ins = tr(bank[5][:, 8 * i + 4 * d:8 * i + 4 * d + 4],
                                     mx[0:HEADS, d, TC + P * i:TC + P * i + P], ident[0:HEADS, 0:HEADS])
                    last_of(ins, mback_tr)

            def score(h):
                for cc in range(NC_ALL):
                    gi = place[("S", NC_ALL * h + cc)]
                    freed(pe, gi)
                    if cc == 0:
                        pe.wait_ge(silu_done, 24)
                    for j in range(2):
                        ins = mm(bk(gi)[:, :], kT[:, 2 * h + j, P * cc:P * cc + P], qT[:, 2 * h + j, :],
                                 start=j == 0, stop=j == 1)
                    last_of(ins, gemm_done)

            def weigh(h, d):
                u = 2 * h + d
                pe.wait_ge(wmul, 6 * (u + 1))
                for i in range(NC_LAT):
                    n = NC_LAT * u + i
                    keys = [0, 1] + (list(range(2, 2 + i + 1)) if d == 0 else list(range(2 + i, NC_ALL)))
                    if n >= 3:
                        pe.wait_ge(av_read, n - 2)
                    for j, cc in enumerate(keys):
                        ins = mm(bank[(4, 6, 7)[n % 3]][:, 0:HD + 1], attn[u % 2][:, cc, P * i:P * i + P],
                                 vone[:, cc, (HD + 1) * h:(HD + 1) * (h + 1)], start=j == 0, stop=j == len(keys) - 1)
                    last_of(ins, av_done)

            pe.wait_ge(act_read, read_no[place[("v", 11)]][1])
            pe.wait_ge(ones_col, 1)
            score(0)
            for h in range(HEADS):
                weigh(h, 0)
                if h + 1 < HEADS:
                    score(h + 1)
                weigh(h, 1)

            pe.wait_ge(op_lo, 8)
            for m in range(KT):
                tile_w3("o", m, h_high1, hT_low)
            for m in range(KT):
                if m % 2 == 0:
                    pe.wait_ge(hnorm, m // 2 + 1)
                gi = place[("hT", m)]
                freed(pe, gi)
                for i in range(NC_LAT):
                    ins = tr(bk(gi)[:, P * i:P * i + P], hsum[:, m // 2, i, P * (m % 2):P * (m % 2) + P], ident[:, :])
                last_of(ins, gemm_done)
            for m in range(KT):
                tile_w3("mg1", m, h_high1, hT_low)
            pe.wait_ge(op_lo, 16)
            for m in range(KT):
                tile_w3("wb1", m, br1_high, br1_low)

            def token_major(name, m):
                t0 = conv_no[(name, m, 0)]
                pe.wait_ge(silu_done, t0 + 2)
                for j in range(2):
                    gi = place[(name + "Tr", 2 * m + j)]
                    freed(pe, gi)
                    for i in range((NC_LAT, NC_CTX)[j]):
                        at = (TC + P * i) if j == 0 else P * i
                        ins = tr(bk(gi)[:, P * i:P * i + P], xst[:, m % 3, at:at + P], ident[:, :])
                    last_of(ins, gemm_done)

            pe.wait_ge(h_moved, 2)
            for m in range(4 + 2):
                if m < 4:
                    tile_w3("B", m, h_high3, hT_low, 2 * m)
                    tile_w3("B", m, hc_high3, hTc_low, 2 * m + 1, TC)
                if m >= 2:
                    token_major("B", m - 2)
            for m in range(4):
                tile_w3("C", m, h_high3, hT_low)
            for d in range(2):
                for i in range(NC_LAT):
                    ins = tr(bank[4 + d][0:SH, P * i:P * i + P], acs[:, d, NC_CTX + i, :], ident[:, :])
            last_of(ins, arow_tr)
            for m in range(8 + 2):
                if m < 8:
                    tile_w3("x", m, h_high3, hT_low, 2 * m)
                    tile_w3("x", m, hc_high3, hTc_low, 2 * m + 1, TC)
                if m >= 2:
                    token_major("x", m - 2)
            def gate_z(m):
                i, half = m % NC_LAT, m // NC_LAT
                n = first_chunk["z"] + half
                gi = place[("z", m)]
                pe.wait_ge(h_back, 2)
                arrived(pe, n)
                freed(pe, gi)
                for k in range(KT):
                    ins = mm(bk(gi)[:, :], hT[:, k, P * i:P * i + P], ring[n % NW][:, k, :], start=k == 0, stop=k == KT - 1)
                last_of(ins, gemm_done)

            pe.wait_ge(dve_read, read_no[place[("xTr", 15)]][1])
            pe.wait_ge(silu_done, len(conv))
            pe.wait_ge(arow_ok, 2)
            for i in range(NC_LAT):
                if i >= 2:
                    pe.wait_ge(dmul, i - 1)
                for gq in range(SG_):
                    ins = mm(bank[4 + i % 2][:, P * gq:P * gq + P], BT[:, gq, P * i:P * i + P],
                             CT[:, gq, P * i:P * i + P], start=True, stop=True)
                last_of(ins, g_mm)
                for m in Z_AT[i]:
                    gate_z(m)
                pe.wait_ge(dmul, i + 1)
                if i >= 1:
                    pe.wait_ge(y_ok, i)
                for h in reversed(range(SH)):
                    lo = 0 if h % 8 == 0 else WIDE - SP_
                    ins = mm(bank[6 + h // 8][:, SP_ * (h % 8) - lo:SP_ * (h % 8) + SP_], decay[i % 2][:, 0, h, :],
                             xtok[:, NC_CTX + i, SP_ * h - lo:SP_ * h + SP_], start=True, stop=True)
                last_of(ins, intra_mm)
            pe.wait_ge(y_ok, 4)
            n_inter = 0
            for n in range(10):
                d, step = n % 2, n // 2
                cc = ([0, 1, 2, 3, 4], [1, 0, 5, 4, 3])[d][step]
                if step >= 2:
                    cq = (step - 2, 3 - (step - 2))[d]
                    pe.wait_ge(st_ok, n - 1)
                    if n_inter >= 1:
                        pe.wait_ge(inter_read, n_inter)
                    for gq in range(SG_):
                        ins = mm(bank[6 + gq // 2][:, 256 * (gq % 2):256 * (gq % 2) + 256], CT[:, gq, P * cq:P * cq + P],
                                 state[:, d, 256 * gq:256 * gq + 256], start=True, stop=True)
                    last_of(ins, inter_mm)
                    n_inter += 1
                pe.wait_ge(xw_ok, n + 1)
                if n >= 1:
                    pe.wait_ge(st_ok, n)
                for gq in range(SG_):
                    ins = mm(bank[4 + gq // 2][:, 256 * (gq % 2):256 * (gq % 2) + 256], Btok[:, cc, SN * gq:SN * gq + SN],
                             xw[:, d, 256 * gq:256 * gq + 256], start=True, stop=True)
                last_of(ins, cs_mm)
            for d in range(2):
                cq = (3, 0)[d]
                pe.wait_ge(st_ok, 9 + d)
                pe.wait_ge(inter_read, n_inter)
                for gq in range(SG_):
                    ins = mm(bank[6 + gq // 2][:, 256 * (gq % 2):256 * (gq % 2) + 256], CT[:, gq, P * cq:P * cq + P],
                             state[:, d, 256 * gq:256 * gq + 256], start=True, stop=True)
                last_of(ins, inter_mm)
                n_inter += 1

            pe.wait_ge(op_lo, 24)
            for m in range(4):
                tile_w3("mg2", m, h_high2, hT_low)
            pe.wait_ge(ynorm, 4)
            for m in range(KT):
                gi = place[("yT", m)]
                freed(pe, gi)
                for i in range(NC_LAT):
                    ins = tr(bk(gi)[:, P * i:P * i + P], ytok[:, i, P * m:P * m + P], ident[:, :])
                last_of(ins, gemm_done)
            for m in range(4, KT):
                tile_w3("mg2", m, h_high2, hT_low)
            pe.wait_ge(op_lo, 32)
            def sum_pieces(t):
                if 0 <= t < len(PIECES):
                    for q in range(piece_at[t], piece_at[t + 1]):
                        pe.wait_ge(piece_ok, q + 1)
                        mm(bank[4][:, q:q + WIDE], piece_sum[:, q % 2, :], ones[:, 0:WIDE], start=True, stop=True
                           ).then_inc(piece_mm, 1)

            for m in range(KT):
                tile_w3("wb2", m, br2_high, br2_low)
                sum_pieces(m - 2)

            for m in range(KT):
                tile_w3("pa", m, h_high2, hT_low)
                if m < 2:
                    sum_pieces(KT + m - 2)
            pe.wait_ge(pw_in, 32)
            for m in range(KT):
                gi = place[("pw", m)]
                freed(pe, gi)
                pe.wait_ge(pool_ok, 2 * (m // 2) + 2)
                for j in range(2):
                    ins = mm(bk(gi)[:, :], pw_sb[:, j, m // 2, P * (m % 2):P * (m % 2) + P],
                             pooled[:, 2 * (m // 2) + j, :], start=j == 0, stop=j == 1)
                last_of(ins, gemm_done)
            for m in range(KT):
                tile_w3("mg0", m, h_high2, hT_low)
                if m >= 2:
                    sum_pieces(KT + m - 2)
            pe.wait_ge(op_lo, 40)
            for m in range(KT):
                tile_w3("wb0", m, br0_high, br0_low)
                sum_pieces(2 * KT + m - 2)
            pe.wait_ge(op_lo, 48)
            for m in range(KT):
                tile_w3("wo", m, merged_high, merged_low)
            pe.wait_ge(dve_read, read_no[place[("wo", 7)]][1])
            for q in range(8):
                i, half = q // 2, q % 2
                gi = place[("xtok", q)]
                freed(pe, gi)
                for m in range(4):
                    ins = tr(bk(gi)[:, P * m:P * m + P], xl[:, 4 * half + m, P * i:P * i + P], ident[:, :])
                last_of(ins, gemm_done)
            pe.wait_ge(sq2_ok, 8)
            for m in range(KT):
                ins = mm(bank[5][:, :], ones[:, :], sq2[:, m, :], start=m == 0, stop=m == KT - 1)
            last_of(ins, stat2)
            pe.wait_ge(ada2_read, 1)
            for n in range(6, 8):
                modulation(n, first_chunk["wo"] + 2 + n - 6)
            pe.wait_ge(h2_ok, 8)
            pe.wait_ge(route_in, 64)
            for i in range(NC_LAT):
                for k in range(KT):
                    ins = mm(bank[6][:, WIDE * i:WIDE * i + WIDE], h2T[:, k, P * i:P * i + P], w_route[:, k, :],
                             start=k == 0, stop=k == KT - 1)
            last_of(ins, route_mm)
            for q in range(8):
                i, half = q // 2, q % 2
                gi = place[("htok", q)]
                freed(pe, gi)
                for m in range(4):
                    ins = tr(bk(gi)[:, P * m:P * m + P], h2T[:, 4 * half + m, P * i:P * i + P], ident[:, :])
                last_of(ins, gemm_done)
            pe.wait_ge(member_ok, 1)
            for j, w in enumerate((strict, ones[:, :])):
                ins = mm(bank[7][:, P * j:P * j + P], w, both.rearrange("p i e -> p (i e)"), start=True, stop=True)
            last_of(ins, pos_mm)
            pe.wait_ge(split_ok, 8)

            def gather(n, half, ms):
                for m in ms:
                    for j, part in enumerate(parts):
                        for i in range(NC_LAT):
                            ins = mm(bank[(0, 5)[half]][:, BS * (m % 4):BS * (m % 4) + BS],
                                     part[:, i, P * m:P * m + P], onehot[:, i, :],
                                     start=i + j == 0, stop=(i, j) == (NC_LAT - 1, 2))
                return ins

            pe.wait_ge(hot_ok, 1)
            for half in range(2):
                gather(0, half, range(4 * half, 4 * half + 4)).then_inc(gather_mm, 1)
            for m in range(NSL):
                tr(bank[6][:, 0:P], ident[:, :], ident[:, :]).then_inc(slice_mm, 1)
            pe.wait_ge(table_ok, 1)
            n_blocks = pe.value_load(table[0:1, NE:NE + 1], min_val=NE, max_val=MAXB)
            with pe.Fori(0, n_blocks, 1) as blk:
                for u in range(8):
                    k0 = 2 * (u % 4)
                    if u == 0:
                        pe.wait_ge(xg_lo, blk * 2 + 1)
                    if u == 2:
                        pe.wait_ge(xg_lo, blk * 2 + 2)
                    pe.wait_ge(slice_lo, blk * SLICES + (u + 1))
                    w_h, w_l = slice_high[u % NSL], slice_low[u % NSL]
                    for k in range(2):
                        for j, (a, b) in enumerate(((xg_high, w_h), (xg_high, w_l), (xg_low, w_h))):
                            ins = mm(bank[1 + u // 4][0:BS, :], a[:, k0 + k, :], b[:, k, :],
                                     start=k0 + k + j == 0, stop=(k0 + k, j) == (KT - 1, 2))
                    last_of(ins, slice_mm)
                pe.wait_ge(hot_ok, blk + 2)
                last_of(gather(blk + 1, 0, range(4)), gather_mm)
                pe.wait_ge(a_ok, blk + 1)
                for f in range(DE // P):
                    ins = tr(bank[6][:, BS * f:BS * f + BS], act_tok[0:BS, P * f:P * f + P], ident[0:BS, 0:BS])
                last_of(ins, a_tr)
                last_of(gather(blk + 1, 1, range(4, 8)), gather_mm)
                pe.wait_ge(a_lo, blk + 1)
                pe.wait_ge(y_lo, blk + 1)
                pe.wait_ge(y_hi, blk + 1)
                for u in range(8, SLICES):
                    f = u - 8
                    pe.wait_ge(slice_lo, blk * SLICES + (u + 1))
                    w_h, w_l = slice_high[u % NSL], slice_low[u % NSL]
                    for j, (a, b) in enumerate(((aT_high, w_h), (aT_high, w_l), (aT_low, w_h))):
                        for half in range(2):
                            ins = mm(bank[3 + half][0:BS, :], a[:, f, :], b[:, half, :],
                                     start=f + j == 0, stop=(f, j) == (DE // P - 1, 2))
                    last_of(ins, slice_mm)

        @block.scalar
        def _(act):
            link = linker(act, alink)
            A = nc.scalar.activation

            def got(name, i):
                gi = place[(name, i)]
                act.wait_ge(gemm_done, gi + 1)
                return bk(gi)

            act.wait_ge(vec_sb, 1)
            act.wait_ge(filled, 6)
            A(csil[:, :, 0:2].rearrange("p k s -> p s k"), vec[:, 0, V_C:V_C + 16].rearrange("p (s k) -> p s k", s=2), ACT.Silu
              ).then_inc(csil_ok, 1)
            for m in range(KT):
                act.wait_ge(dve_read, m + 1)
                A(sq[:, m, :], xT[:, m, :], ACT.Square).then_inc(squares, 1)
            for m in range(KT):
                act.wait_ge(dve_read, 8 + m + 1)
                A(sqc[:, m, :], xTc[:, m, :], ACT.Square).then_inc(squares, 1)
            act.wait_ge(stat_done, 2)
            A(rn[:, TC:], bank[5][:, :], ACT.Sqrt, scale=1.0 / D, bias=eps[:, :]).then_inc(norm_root, 1)
            A(rn[:, 0:TC], bank[6][:, 0:TC], ACT.Sqrt, scale=1.0 / D, bias=eps[:, :]).then_inc(norm_root, 1)
            for m in range(KT):
                act.wait_ge(h_ok, m + 1)
                A(hcm[:, m, :].rearrange("p (w r) -> p r w", r=GRID_H), hT[:, m, :].rearrange("p (r w) -> p r w", r=GRID_H),
                  ACT.Copy).then_inc(hcm_ok, 1)

            act.wait_ge(small_in, 16 * 6)
            link(A(expa, a_log[:, :], ACT.Exp))
            act.wait_ge(gates_pre, 1)
            link(A(gabs, gx, ACT.Abs))
            A(gexp, gabs, ACT.Exp, scale=-1.0).then_inc(gates_exp, 1)
            act.wait_ge(gates_u, 1)
            A(gl, gu, ACT.Ln).then_inc(gates_ln, 1)

            cin, cinc, acc = {}, {}, {}
            for s in ("k", "q"):
                cin[s], cinc[s], acc[s] = cin_m, cinc_m, acc_m
            for s in ("B", "C", "x"):
                cin[s], cinc[s], acc[s] = cin_s, cinc_s, acc_s

            def stage_in(n):
                s, m, cx = conv[n]
                src = got(s, 2 * m + cx if s in ("k", "B", "x") else m)
                before = conv_before(n, (NCIN, NCINC))
                if before:
                    act.wait_ge(conv_done, before)
                slot = kind_no[n] % (NCINC if cx else NCIN)
                if cx:
                    o, i_ = cinc[s][:, slot, 2:2 + TC], src[:, 0:TC]
                elif s in ("k", "q"):
                    o = cin[s][:, slot, 2:2 + T].rearrange("p (w r) -> p r w", r=GRID_H)
                    i_ = src[:, :].rearrange("p (r w) -> p r w", r=GRID_H)
                else:
                    o, i_ = cin[s][:, slot, 2:2 + T], src[:, :]
                A(o, i_, ACT.Copy).then_inc(act_read, 1)

            def finish_conv(n):
                s, m, cx = conv[n]
                act.wait_ge(conv_done, n + 1)
                w = TC if cx else T
                at = 0 if cx else TC
                if s == "k":
                    o = kT[:, m, at:at + w]
                elif s == "q":
                    o = qT[:, m, :]
                elif s == "C":
                    o = CT[:, m, :]
                else:
                    if m >= 3 or s == "x":
                        prev = {("B", 3): ("BTr", 1)}.get((s, m))
                        if s == "x":
                            prev = {0: ("BTr", 7), 1: ("BTr", 7), 2: ("BTr", 7)}.get(m, ("xTr", 2 * (m - 3) + 1))
                        act.wait_ge(gemm_done, place[prev] + 1)
                    o = xst[:, m % 3, at:at + w]
                if s == "B" and not cx:
                    A(BT[:, m, :], acc[s][:, n % 3, 0:w], ACT.Silu)
                A(o, acc[s][:, n % 3, 0:w], ACT.Silu).then_inc(silu_done, 1)

            act.wait_ge(pads, 4)
            LAG = 2

            def conv_run(lo, hi):
                for n in range(lo, hi + LAG):
                    if n < hi:
                        stage_in(n)
                    if n >= lo + LAG:
                        finish_conv(n - LAG)

            conv_run(0, 24)
            for m in range(12):
                half, cc = m // NC_ALL, (m + NC_CTX) % NC_ALL
                src = got("v", m)
                if m == 0:
                    act.wait_ge(h_back, 1)
                A(vone[:, cc, :].rearrange("p (h e) -> p h e", h=HEADS)[:, 2 * half:2 * half + 2, 0:HD],
                  src[:, :].rearrange("p (h e) -> p h e", h=2), ACT.Copy).then_inc(act_read, 1)
            act.wait_ge(em_sum, 1)
            A(em[:, :, :], em[:, :, :], ACT.Exp, scale=-1.0).then_inc(em_ok, 1)
            act.wait_ge(ssd_pre, 1)
            A(e_in[:, :, :, :], acs[:, :, :, :], ACT.Exp).then_inc(ssd_exp, 1)
            A(coef[:, :, :, :], coef[:, :, :, :], ACT.Exp).then_inc(ssd_exp, 1)
            A(tot[:, :, :, :], tot[:, :, :, :], ACT.Exp).then_inc(ssd_exp, 1)

            def copy_scores(h):
                for cc in range(NC_ALL):
                    src = got("S", NC_ALL * h + cc)
                    if h >= 1 and cc == 0:
                        act.wait_ge(wmul, 12 * h)
                    A(scores[:, cc, :], src[:, :], ACT.Copy, scale=HD ** -0.5).then_inc(act_read, 1)

            def exps(h, d):
                u = 2 * h + d
                act.wait_ge(m_bc[h % 2], 16 * (h // 2 + 1))
                act.wait_ge(diag_ok, u + 1)
                if u >= 2:
                    act.wait_ge(av_done, NC_LAT * (u - 1))
                for cc in range(NC_ALL):
                    bias = bkey[:, cc, 4 * d + h:4 * d + h + 1]
                    if cc < NC_CTX:
                        A(attn[u % 2][:, cc, :], mrow[h % 2][:, d, :], ACT.Exp, scale=-1.0, bias=bias).then_inc(wexp, 1)
                        continue
                    j = cc - NC_CTX
                    lo, hi = ((j + 1) * P, T) if d == 0 else (0, j * P)
                    if hi > lo:
                        A(attn[u % 2][:, cc, lo:hi], mrow[h % 2][:, d, lo:hi], ACT.Exp, scale=-1.0, bias=bias)
                    A(attn[u % 2][:, cc, P * j:P * j + P], diag[d][:, j, :], ACT.Exp, scale=-1.0, bias=bias
                      ).then_inc(wexp, 1)

            copy_scores(0)
            exps(0, 0)
            exps(0, 1)
            for h in range(1, HEADS):
                copy_scores(h)
                exps(h, 0)
                exps(h, 1)
            act.wait_ge(av_read, 32)
            for h in range(HEADS):
                for i in range(NC_LAT):
                    ins = A(gate1[:, 2 * h + i // 2, HD * (i % 2):HD * (i % 2) + HD], hsum[:, h, i, :], ACT.Square,
                            accum_out=ms[:, 4 * h + i:4 * h + i + 1])
            link(ins)
            A(ms[:, :], ms[:, :], ACT.Sqrt, scale=1.0 / HD, bias=eps[:, :]).then_inc(hroot, 1)
            for m in range(KT):
                src = got("o", m)
                A(sig_o[:, m, :], src[:, :], ACT.Sigmoid).then_inc(act_read, 1)

            def gates_of(b, dst):
                for m in range(KT):
                    src = got(f"mg{b}", m)
                    A(dst[:, m, :], src[:, :], ACT.Sigmoid).then_inc(act_read, 1)

            gates_of(1, gate1)
            act.wait_ge(pads, 8)
            conv_run(24, 32)
            conv_run(32, len(conv))

            def silu_z(m):
                src = got("z", m)
                if m == 0:
                    act.wait_ge(gemm_done, place[("x", 15)] + 1)
                A(zbuf[:, m % NC_LAT, 512 * (m // NC_LAT):512 * (m // NC_LAT) + 512], src[:, :], ACT.Silu).then_inc(act_read, 1)

            act.wait_ge(neg_ok, 1)
            for i in range(NC_LAT):
                for d in range(2):
                    act.wait_ge(dmask, 2 * i + d + 1)
                    for h in range(SH):
                        ins = A(decay[i % 2][:, d, h, :], decay[i % 2][:, d, h, :], ACT.Exp,
                                bias=neg_acs[:, d, NC_CTX + i, h:h + 1])
                    ins.then_inc(dexp, 1)
                for m in Z_AT[i]:
                    silu_z(m)
            for i in range(NC_LAT):
                act.wait_ge(yz_ok, 1 + i)
                link(A(junk, ytok[:, i, :], ACT.Square, accum_out=ms[:, i:i + 1]))
            A(ms[:, 0:NC_LAT], ms[:, 0:NC_LAT], ACT.Sqrt, scale=1.0 / D, bias=eps[:, :]).then_inc(yroot, 1)
            gates_of(2, gate2)
            def load_pieces(lo, hi):
                for q in range(lo, min(hi, N_PIECE)):
                    if q >= 3:
                        act.wait_ge(piece_ok, q - 2)
                    act.dma_start(piece_in[q % 3], w_ada[0][:, 2048 + P * q:2048 + P * q + P]
                                  .rearrange("(k p) n -> p k n", p=P)).then_inc(piece_ld[q % 3], 16)

            act.wait_ge(gemm_done, place[("yT", 7)] + 1)
            load_pieces(0, 3)
            for t in range(KT):
                load_pieces(3 + piece_at[t], 3 + piece_at[t + 1])
            act.wait_ge(pads, 9)
            for m in range(KT):
                src = got("pa", m)
                if m >= 2:
                    act.wait_ge(pool_ok, m - 1)
                A(ppad[:, m % 2, :].rearrange("p (r w) -> p r w", r=GRID_H)[:, :, 8:8 + GRID_W],
                  src[:, :].rearrange("p (r w) -> p r w", r=GRID_H), ACT.Copy).then_inc(act_read, 1)
            for m in range(KT):
                src = got("pw", m)
                A(br0[:, m, :], src[:, :], ACT.Copy, scale=vec[:, 0, V_PS + m:V_PS + m + 1]).then_inc(act_read, 1)
            for m in range(KT):
                src = got("mg0", m)
                A(gate0[:, m, :], src[:, :], ACT.Sigmoid).then_inc(act_read, 1)
                if m >= 1:
                    load_pieces(3 + piece_at[KT + m - 1], 3 + piece_at[KT + m])
            load_pieces(3 + piece_at[2 * KT - 1], N_PIECE)
            for m in range(KT):
                act.wait_ge(dve_read, read_no[place[("wo", m)]][1])
                A(sq2[:, m, :], xl[:, m, :], ACT.Square).then_inc(sq2_ok, 1)
            act.wait_ge(stat2, 1)
            A(rn2, bank[5][:, :], ACT.Sqrt, scale=1.0 / D, bias=eps[:, :]).then_inc(root2, 1)
            act.wait_ge(normed2, 1)
            for m in range(KT):
                A(h2T[:, m, :], h2T[:, m, :], ACT.Identity, scale=modF[:, m:m + 1], bias=ada[:, 24 + m, 0:1]
                  ).then_inc(h2_ok, 1)
            for q in range(8 + 2):
                if q == Q_EXP:
                    act.wait_ge(gexp_pre, 1)
                    A(gsc, gsc, ACT.Exp).then_inc(gexp_ok, 1)
                if q == Q_EXP + 1:
                    act.wait_ge(topexp_pre, 1)
                    A(etmp, etmp, ACT.Exp).then_inc(topexp_ok, 1)
                if q < 8:
                    i, half = q // 2, q % 2
                    at = slice(512 * half, 512 * half + 512)
                    src = got("htok", q)
                    A(h2tok[:, i, at], src[:, :], ACT.Copy).then_inc(act_read, 1)
                    act.wait_ge(act_read, read_no[place[("htok", q)]][1])
                    A(parts[0][:, i, at], h2tok[:, i, at], ACT.Copy).then_inc(split_hi, 1)
                if q >= 2:
                    i, half = (q - 2) // 2, q % 2
                    at = slice(512 * half, 512 * half + 512)
                    act.wait_ge(split_lo, q - 1)
                    A(parts[1][:, i, at], h2tok[:, i, at], ACT.Copy).then_inc(split_mid, 1)
            act.wait_ge(table_ok, 1)

            def take_gathered(n, half):
                act.wait_ge(gather_mm, n * 2 + (half + 1))
                A(xg_high[:, 4 * half:4 * half + 4, :].rearrange("p k s -> p (k s)"), bank[(0, 5)[half]][:, 0:4 * BS],
                  ACT.Copy).then_inc(xg_hi, 1)

            def first_rows(n):
                act.wait_ge(slice_mm, n * SLICES + NSL)
                A(y_sb[0:BS, 0:512], bank[3][0:BS, :], ACT.Copy).then_inc(y_lo, 1)

            def store_rows(n):
                act.wait_ge(y_lo, n + 1)
                act.wait_ge(y_hi, n + 1)
                act.dma_start(y_scr[n], y_sb[0:BS, :]).then_inc(y_out, 16)

            for half in range(2):
                take_gathered(0, half)
            with act.Fori(0, NE // 2, 1) as ep:
                for par in range(2):
                    s0 = 3 * (1 - par)
                    first = act.value_load(table[0:1, bass.ds(2 * ep + par, 1)], min_val=0, max_val=MAXB)
                    end = act.value_load(table[0:1, bass.ds(2 * ep + (par + 1), 1)], min_val=1, max_val=MAXB)
                    with act.Fori(first, end, 1) as blk:
                        for u in range(SLICES):
                            if u % 4 == 0:
                                act.wait_ge(expert_in[s0 + u // 4], ep * 16 + 16)
                            act.wait_ge(slice_mm, blk * SLICES + (u + 1))
                            A(slice_high[u % NSL].rearrange("p k n -> p (k n)"),
                              slot6[s0 + u // 4][:, 1024 * (u % 4):1024 * (u % 4) + 1024], ACT.Copy).then_inc(slice_hi, 1)
                            if u == NSL - 1:
                                first_rows(blk)
                            if u == 5:
                                store_rows(blk)
                            if u == 10:
                                act.wait_ge(slice_mm, blk * SLICES + (8 + NSL))
                                A(act_tok[0:BS, :], bank[1][0:BS, :], ACT.Silu).then_inc(sg_ok, 1)
                            if u == 11:
                                for half in range(2):
                                    take_gathered(blk + 1, half)
                        act.wait_ge(y_out, blk * 16 + 16)
            n_blocks = act.value_load(table[0:1, NE:NE + 1], min_val=NE, max_val=MAXB)
            first_rows(n_blocks)
            store_rows(n_blocks)
            act.wait_ge(y_out, n_blocks * 16 + 16)
            A(ms[:, 0:4], ms[:, 0:4], ACT.Copy).then_inc(blocks_done, 1)
            for i in range(NC_LAT):
                act.wait_ge(fin_ok_pre, i + 1)
                link(A(yg[2 * i + 1], yg[2 * i], ACT.Square, accum_out=ms[:, i:i + 1]))
                A(ms[:, i:i + 1], ms[:, i:i + 1], ACT.Sqrt, scale=1.0 / D, bias=eps[:, :]).then_inc(froot, 1)

        @block.vector
        def _(dve):
            link = linker(dve, vlink)
            v = nc.vector

            def got(name, i):
                gi = place[(name, i)]
                dve.wait_ge(gemm_done, gi + 1)
                return bk(gi)

            def high_weights(name, m):
                u = unit_no[(name, m)]
                arrived(dve, first_chunk[name] + m // 4)
                if u >= NHI:
                    dve.wait_ge(gemm_done, unit_end(u - NHI))
                v.tensor_copy(w_high[u % NHI], raw_tile(u)).then_inc(w_hi, 1)

            def high_operand(high, whole, m):
                whole_m, high_m = (ap[m] if isinstance(ap, list) else ap[:, m, :] for ap in (whole, high))
                v.tensor_copy(high_m, whole_m).then_inc(op_hi, 1)

            dve.wait_ge(vec_tr, 1)
            for part in range(3):
                ins = v.tensor_copy(vec[:, part, 0:n_rows[part]], bank[7][:, P * part:P * part + n_rows[part]])
            ins.then_inc(vec_sb, 1)
            for m in range(KT):
                v.tensor_copy(xT[:, m, :], got("xT", m)[:, :]).then_inc(dve_read, 1)
            for m in range(KT):
                v.tensor_copy(xTc[:, m, :], got("xTc", m)[:, 0:TC]).then_inc(dve_read, 1)
            dve.wait_ge(norm_root, 2)
            link(v.reciprocal(rn[:, :], rn[:, :]))
            v.tensor_tensor(hT, xT, rn[:, None, TC:].to_broadcast([P, KT, T]), ALU.mult).then_inc(normed, 1)
            v.tensor_tensor(hTc, xTc, rn[:, None, 0:TC].to_broadcast([P, KT, TC]), ALU.mult).then_inc(normed, 1)
            dve.wait_ge(ada_done, 4)
            def add_bias(n, at):
                return v.tensor_tensor(ada[:, at:at + 4, :],
                                       bank[ADA_BANK[n]][:, 0:4 * WIDE].rearrange("p (j s) -> p j s", s=WIDE)[:, :, 0:2],
                                       vec[:, 0, V_BADA + at:V_BADA + at + 4, None].to_broadcast([P, 4, 2]), ALU.add)

            for n in range(4):
                ins = add_bias(n, 4 * n)
            link(ins)
            v.scalar_tensor_tensor(modA[:, :, :], ada[:, 8:16, :].rearrange("p k s -> p s k"), 1.0,
                                   vec[:, 0, None, V_GMIX:V_GMIX + 8].to_broadcast([P, 2, KT]), ALU.add, ALU.mult
                                   ).then_inc(modA_ok, 1)
            dve.wait_ge(modA_ok, 1)
            dve.wait_ge(normed, 2)
            for s_, h_ in enumerate((hT, hTc)):
                for m in range(KT):
                    v.tensor_scalar(h_[:, m, :], h_[:, m, :], modA[:, s_, m:m + 1], ada[:, m, s_:s_ + 1], ALU.mult, ALU.add
                                    ).then_inc(h_ok, 1)
            dve.wait_ge(h_ok, 16)
            v.tensor_copy(h_high0, hT)
            link(v.tensor_copy(hc_high0, hTc))
            for m in range(4):
                high_weights("k", m)
            dve.wait_ge(gates_mm, 1)
            for low, whole, high in ((hT_low, hT, h_high0), (hTc_low, hTc, hc_high0)):
                for m in range(KT):
                    v.tensor_tensor(low[:, m, :], whole[:, m, :], high[:, m, :].bitcast(f32), ALU.subtract).then_inc(h_low, 1)
            fpart = gx[:, 0:48].rearrange("p (c h) -> p c h", c=NC_ALL)
            dpart = gx[:, 48:240].rearrange("p (c h) -> p c h", c=NC_ALL)
            b5 = bank[5][:, 0:GST * NC_ALL].rearrange("p (c h) -> p c h", c=NC_ALL)
            b6 = bank[6][:, 0:GST * NC_ALL].rearrange("p (c h) -> p c h", c=NC_ALL)[:, :, 16:48]
            v.tensor_tensor(ig[:, :, :], b5[:, :, 0:8], gate_b[:, None, 0:8].to_broadcast([P, NC_ALL, 8]), ALU.add)
            v.tensor_tensor(fpart, b5[:, :, 8:16], gate_b[:, None, 8:16].to_broadcast([P, NC_ALL, 8]), ALU.add)
            v.tensor_tensor(dpart, b6, dt_b[:, None, :].to_broadcast([P, NC_ALL, 32]), ALU.add).then_inc(gates_pre, 1)
            dve.wait_ge(gates_exp, 1)
            v.tensor_scalar(gu, gexp, 1.0, None, ALU.add).then_inc(gates_u, 1)
            dve.wait_ge(gates_u, 1)
            link(v.tensor_scalar(gd_, gu, -1.0, None, ALU.add))
            link(v.tensor_tensor(gd_, gexp, gd_, ALU.subtract))
            dve.wait_ge(gates_ln, 1)
            link(v.reciprocal(gu, gu))
            link(v.tensor_tensor(gd_, gd_, gu, ALU.mult))
            link(v.tensor_tensor(gl, gl, gd_, ALU.add))
            v.scalar_tensor_tensor(lf[:, 0:NC_ALL, :].rearrange("p c h -> p (c h)"), gx[:, 0:48], 0.0, gl[:, 0:48],
                                   ALU.min, ALU.subtract).then_inc(lf_ok, 1)
            for d in range(2):
                ins = v.scalar_tensor_tensor(
                    dt[:, d], dpart[:, :, 16 * d:16 * d + 16], 0.0,
                    gl[:, 48:240].rearrange("p (c h) -> p c h", c=NC_ALL)[:, :, 16 * d:16 * d + 16], ALU.max, ALU.add)
            link(ins)
            for d in range(2):
                ins = v.scalar_tensor_tensor(dta[:, d], dt[:, d], -1.0,
                                             expa[:, None, 16 * d:16 * d + 16].to_broadcast([P, NC_ALL, SH]),
                                             ALU.mult, ALU.mult)
            ins.then_inc(lf_ok, 1)

            def conv_tile(n):
                s, m, cx = conv[n]
                first = s in ("k", "q")
                cin, cinc, acc = (cin_m, cinc_m, acc_m) if first else (cin_s, cinc_s, acc_s)
                part = 1 if first else 2
                base = {"k": 8, "q": 0, "x": 0, "B": 8, "C": 12}[s] + m
                g = place[(s, 2 * m + cx if s in ("k", "B", "x") else m)]
                dve.wait_ge(act_read, read_no[g][1])
                if n >= 3:
                    dve.wait_ge(silu_done, n - 2)
                w = TC if cx else T
                slot = kind_no[n] % (NCINC if cx else NCIN)
                src = (cinc if cx else cin)[:, slot, :]
                a = acc[:, n % 3, 0:w]

                def tap(j):
                    return vec[:, part, 16 * j + base:16 * j + base + 1]
                link(v.tensor_scalar(a, src[:, 0:w], tap(0), vec[:, part, 64 + base:65 + base], ALU.mult, ALU.add))
                for j in range(1, 4):
                    ins = v.scalar_tensor_tensor(a, src[:, j:j + w], tap(j), a, ALU.mult, ALU.add)
                    if j < 3:
                        link(ins)
                ins.then_inc(conv_done, 1)
                ahead = unit_no[(s, m)] + NHI
                if not cx and units[ahead][0] in ("k", "q", "C", "x"):
                    high_weights(*units[ahead])

            for n in range(16):
                conv_tile(n)
            dve.wait_ge(cum_mm, 1)
            v.tensor_copy(acs[:, :, :, :].rearrange("p d c h -> p (d c h)"), bank[7][:, 0:192]).then_inc(cum_read, 1)
            run = bank[4][:, 0:3 * WIDE].rearrange("p (j c h) -> p j c h", j=3, h=8)
            v.tensor_copy(ftot[:, :, :], run[:, 2, 0:NC_ALL, :])
            v.tensor_copy(fcum[:, :, 0:4], run[:, 0, 0:NC_ALL, 0:4])
            link(v.tensor_copy(fcum[:, :, 4:8], run[:, 1, 0:NC_ALL, 4:8]))
            orders = ([0, 1, 2, 3, 4, 5], [1, 0, 5, 4, 3, 2])
            for n in range(1, NC_ALL):
                for d, order in enumerate(orders):
                    cols_d = slice(4 * d, 4 * d + 4)
                    before, cc = ftot[:, order[n - 1], cols_d], order[n]
                    v.tensor_tensor(fcum[:, cc, cols_d], fcum[:, cc, cols_d], before, ALU.add)
                    ins = v.tensor_tensor(ftot[:, cc, cols_d], ftot[:, cc, cols_d], before, ALU.add)
                link(ins)
            v.tensor_tensor(bkey[:, :, :], ig[:, :, :], fcum[:, :, :], ALU.subtract).then_inc(bkey_ok, 1)
            for n in range(16, 20):
                conv_tile(n)
            dve.wait_ge(tot_mm, 1)
            link(v.tensor_copy(tot[:, :, :, :].rearrange("p d c h -> p (d c h)"), bank[7][:, 192:384]))
            v.tensor_tensor(coef[:, :, :, :], tot[:, :, :, :], acs[:, :, :, :], ALU.subtract).then_inc(ssd_pre, 1)
            dve.wait_ge(brow_tr, 1)
            v.tensor_copy(brow[0:HEADS, :, 0:TC], bank[4][0:HEADS, :].rearrange("p (d t) -> p d t", d=2))
            v.tensor_copy(brow[0:HEADS, 0, TC:], bank[5][0:HEADS, :])
            link(v.tensor_copy(brow[0:HEADS, 1, TC:], bank[6][0:HEADS, :]))
            scan = v.tensor_tensor_scan
            scan(mx[0:HEADS, 0, :], brow[0:HEADS, 0, :], brow[0:HEADS, 0, :], 0.0, ALU.max, ALU.max)
            link(scan(mx[0:HEADS, 1, 0:TC][:, ::-1], brow[0:HEADS, 1, 0:TC][:, ::-1], brow[0:HEADS, 1, 0:TC][:, ::-1],
                      0.0, ALU.max, ALU.max))
            scan(mx[0:HEADS, 1, TC:][:, ::-1], brow[0:HEADS, 1, TC:][:, ::-1], brow[0:HEADS, 1, TC:][:, ::-1],
                 mx[0:HEADS, 1, 0:1], ALU.max, ALU.max).then_inc(mx_ok, 1)
            for n in range(20, 23):
                conv_tile(n)
            dve.wait_ge(gemm_done, place[("q", 7)] + 1)
            dve.wait_ge(h_low, 16)
            link(v.tensor_tensor(hT, hT_low.bitcast(f32), h_high0.bitcast(f32), ALU.add))
            v.tensor_tensor(hTc, hTc_low.bitcast(f32), hc_high0.bitcast(f32), ALU.add).then_inc(h_back, 1)
            conv_tile(23)
            dve.wait_ge(mback_tr, 1)
            v.tensor_tensor(em[:, :, :], bank[5][:, 0:32].rearrange("p (i h) -> p i h", i=NC_LAT),
                            fcum[:, NC_CTX:, :], ALU.add).then_inc(em_sum, 1)
            dve.wait_ge(ssd_exp, 3)
            v.tensor_tensor(coef[:, :, :, :], coef[:, :, :, :], dt[:, :, :, :], ALU.mult).then_inc(coef_ok, 1)

            def weights(h, d):
                u = 2 * h + d
                for cc in range(NC_ALL):
                    j = cc - NC_CTX
                    dve.wait_ge(wexp, 6 * u + cc + 1)
                    dve.wait_ge(act_read, read_no[place[("S", NC_ALL * h + cc)]][1])
                    lo, hi = (0, T) if cc < NC_CTX else ((j * P, T) if d == 0 else (0, (j + 1) * P))
                    v.tensor_tensor(attn[u % 2][:, cc, lo:hi], attn[u % 2][:, cc, lo:hi], scores[:, cc, lo:hi],
                                    ALU.mult).then_inc(wmul, 1)

            def outputs(h, d):
                u = 2 * h + d
                for i in range(NC_LAT):
                    n = NC_LAT * u + i
                    b = bank[(4, 6, 7)[n % 3]]
                    dve.wait_ge(av_done, n + 1)
                    link(v.tensor_scalar(den[:, 0:1], b[:, HD:HD + 1], -1.0, em[:, i, 4 * d + h:4 * d + h + 1],
                                         ALU.mult, ALU.max))
                    link(v.tensor_tensor(den[:, 0:1], den[:, 0:1], b[:, HD:HD + 1], ALU.max))
                    link(v.reciprocal(den[:, 1:2], den[:, 0:1]))
                    if d == 0:
                        v.tensor_scalar(hsum[:, h, i, :], b[:, 0:HD], den[:, 1:2], None, ALU.mult).then_inc(av_read, 1)
                    else:
                        v.scalar_tensor_tensor(hsum[:, h, i, :], b[:, 0:HD], den[:, 1:2], hsum[:, h, i, :],
                                               ALU.mult, ALU.add).then_inc(av_read, 1)

            dve.wait_ge(em_ok, 1)
            for h in range(HEADS):
                weights(h, 0)
                if h >= 1:
                    outputs(h - 1, 1)
                weights(h, 1)
                if h == HEADS - 1:
                    dve.wait_ge(gemm_done, place[("S", 6 * HEADS - 1)] + 1)
                    for m in range(KT):
                        high_operand(h_high1, hT, m)
                    for m in range(4):
                        high_weights("o", m)
                outputs(h, 0)
            outputs(HEADS - 1, 1)

            dve.wait_ge(hroot, 1)
            link(v.reciprocal(ms[:, :], ms[:, :]))
            for h in range(HEADS):
                v.tensor_tensor(hsum[:, h], hsum[:, h], ms[:, 4 * h:4 * h + 4, None].to_broadcast([P, NC_LAT, HD]),
                                ALU.mult).then_inc(hnorm, 1)
            for m in range(4, 8):
                high_weights("o", m)
            for m in range(4):
                high_weights("mg1", m)
            dve.wait_ge(act_read, read_no[place[("o", 7)]][1])
            for m in range(KT):
                src = got("hT", m)
                v.scalar_tensor_tensor(colmajor(br1[m]), src[:, :].rearrange("p (w r) -> p w r", r=GRID_H),
                                       vec[:, 0, V_MG + m:V_MG + m + 1], colmajor(sig_o[:, m, :]),
                                       ALU.mult, ALU.mult).then_inc(dve_read, 1)
            for m in range(KT):
                dve.wait_ge(dve_read, read_no[place[("hT", m)]][1])
                high_operand(br1_high, br1, m)
            for m in range(4, 8):
                high_weights("mg1", m)
            for m in range(4):
                high_weights("wb1", m)
            v.tensor_copy(h_high3, h_high1.bitcast(f32)).then_inc(h_moved, 1)
            link(v.tensor_copy(hc_high3, hTc))
            v.tensor_tensor(hTc_low, hTc, hc_high3.bitcast(f32), ALU.subtract).then_inc(h_moved, 1)

            def merge(b, gate, base, tmp, after=None, pieces=None):
                for m in range(KT):
                    if m < 4:
                        high_weights(f"wb{b}", 4 + m)
                    elif after:
                        high_weights(after, m - 4)
                    dve.wait_ge(act_read, read_no[place[(f"mg{b}", m)]][1])
                    src = got(f"wb{b}", m)
                    if base == 0:
                        v.tensor_tensor(merged[:, m, :], gate[:, m, :], src[:, :], ALU.mult).then_inc(dve_read, 1)
                    else:
                        v.tensor_tensor(tmp[:, m % 2, :], gate[:, m, :], src[:, :], ALU.mult).then_inc(dve_read, 1)
                        dve.wait_ge(dve_read, read_no[place[(f"wb{b}", m)]][1])
                        v.tensor_tensor(merged[:, m, :], merged[:, m, :], tmp[:, m % 2, :], ALU.add).then_inc(prod_ok, 1)
                        if b == 0:
                            dve.wait_ge(prod_ok, base + m - 7)
                            high_operand(merged_high, merged, m)
                    if pieces is not None:
                        use_pieces(pieces + m)

            merge(1, gate1, 0, None, after="B")
            def evac_token_major(name, m):
                src = got(name + "Tr", 2 * m)
                dst = Btok if name == "B" else xtok
                v.tensor_copy(dst[:, NC_CTX:, P * m:P * m + P], src[:, :].rearrange("p (i t) -> p i t", i=NC_LAT)
                              ).then_inc(dve_read, 1)
                src = got(name + "Tr", 2 * m + 1)
                v.tensor_copy(dst[:, 0:NC_CTX, P * m:P * m + P], src[:, 0:TC].rearrange("p (i t) -> p i t", i=NC_CTX)
                              ).then_inc(dve_read, 1)

            for m in range(4 + 2):
                if m < 4:
                    conv_tile(conv_no[("B", m, 0)])
                    conv_tile(conv_no[("B", m, 1)])
                if m >= 2:
                    evac_token_major("B", m - 2)
            for m in range(4):
                conv_tile(conv_no[("C", m, 0)])
            dve.wait_ge(arow_tr, 1)
            for d in range(2):
                v.tensor_copy(rowa[0:SH, d, :], bank[4 + d][0:SH, :]).then_inc(arow_ok, 1)
            for m in range(8 + 2):
                if m < 8:
                    conv_tile(conv_no[("x", m, 0)])
                    conv_tile(conv_no[("x", m, 1)])
                if m >= 2:
                    evac_token_major("x", m - 2)
            v.tensor_scalar(neg_acs, acs[:, :, :, :], -1.0, None, ALU.mult).then_inc(neg_ok, 1)
            dve.wait_ge(gemm_done, place[("x", 15)] + 1)
            v.tensor_tensor(hT, hT_low.bitcast(f32), h_high3.bitcast(f32), ALU.add).then_inc(h_back, 1)
            dve.wait_ge(h_back, 2)
            hx = lambda ap: ap.rearrange("p (h e) -> p h e", h=SH)
            for i in range(NC_LAT):
                w = decay[i % 2]
                cc = NC_CTX + i
                for d in range(2):
                    dve.wait_ge(dexp, 2 * i + d + 1)
                    ins = v.tensor_tensor(w[:, d], w[:, d], dt[:, d, cc, :, None].to_broadcast([P, SH, P]), ALU.mult)
                link(ins)
                link(v.tensor_tensor(w[:, 0], w[:, 0], w[:, 1], ALU.add))
                dve.wait_ge(g_mm, i + 1)
                v.tensor_tensor(w[:, 0].rearrange("p (g h) t -> p g h t", g=SG_),
                                w[:, 0].rearrange("p (g h) t -> p g h t", g=SG_),
                                bank[4 + i % 2][:, :].rearrange("p (g t) -> p g t", g=SG_)[:, :, None, :]
                                .to_broadcast([P, SG_, HPG, P]), ALU.mult).then_inc(dmul, 1)
                link(v.tensor_tensor(hx(ytok[:, i, :]), hx(xtok[:, cc, :]),
                                     d_skip[:, :, None].to_broadcast([P, SH, SP_]), ALU.mult))
                dve.wait_ge(intra_mm, i + 1)
                v.tensor_tensor(ytok[:, i, 0:512], ytok[:, i, 0:512], bank[6][:, :], ALU.add)
                v.tensor_tensor(ytok[:, i, 512:1024], ytok[:, i, 512:1024], bank[7][:, :], ALU.add).then_inc(y_ok, 1)
            dve.wait_ge(y_ok, 4)
            dve.wait_ge(coef_ok, 1)
            n_inter = 0

            def inter(d, cq):
                cc = NC_CTX + cq
                dve.wait_ge(inter_mm, n_inter + 1)
                for b in range(2):
                    ins = v.tensor_tensor(ytmp[:, 0, 512 * b:512 * b + 512].rearrange("p (h e) -> p h e", h=8),
                                          bank[6 + b][:, :].rearrange("p (h e) -> p h e", h=8),
                                          e_in[:, d, cc, 8 * b:8 * b + 8, None].to_broadcast([P, 8, SP_]), ALU.mult)
                ins.then_inc(inter_read, 1)
                dve.wait_ge(inter_read, n_inter + 1)
                v.tensor_tensor(ytok[:, cq, :], ytok[:, cq, :], ytmp[:, 0, :], ALU.add).then_inc(inter_add, 1)
                dve.wait_ge(inter_add, n_inter + 1)

            for n in range(10):
                d, step = n % 2, n // 2
                if n == 6:
                    dve.wait_ge(gemm_done, place[("z", 7)] + 1)
                    for m in range(KT):
                        high_operand(h_high2, hT, m)
                cc = ([0, 1, 2, 3, 4], [1, 0, 5, 4, 3])[d][step]
                if step >= 2:
                    inter(d, (step - 2, 3 - (step - 2))[d])
                    n_inter += 1
                if step:
                    link(v.tensor_tensor(hx(state[:, d]), hx(state[:, d]), tot[:, d, cc, :, None].to_broadcast([P, SH, SP_]),
                                         ALU.mult))
                dve.wait_ge(cs_mm, n + 1)
                for b in range(2):
                    dst = state[:, d, 512 * b:512 * b + 512]
                    if step == 0:
                        ins = v.tensor_copy(dst, bank[4 + b][:, :])
                    else:
                        ins = v.tensor_tensor(dst, dst, bank[4 + b][:, :], ALU.add)
                ins.then_inc(st_ok, 1)
                dve.wait_ge(st_ok, n + 1)
            for d in range(2):
                inter(d, (3, 0)[d])
                n_inter += 1
            dve.wait_ge(act_read, read_no[place[("z", 7)]][1])
            for i in range(NC_LAT):
                v.tensor_tensor(ytok[:, i, :], ytok[:, i, :], zbuf[:, i, :], ALU.mult).then_inc(yz_ok, 1)
                dve.wait_ge(yz_ok, i + 1)
                high_weights("mg2", i)
            dve.wait_ge(yroot, 1)
            link(v.reciprocal(ms[:, 0:NC_LAT], ms[:, 0:NC_LAT]))
            for i in range(NC_LAT):
                v.tensor_scalar(ytok[:, i, :], ytok[:, i, :], ms[:, i:i + 1], None, ALU.mult).then_inc(ynorm, 1)
            for m in range(4, 8):
                high_weights("mg2", m)
            for m in range(KT):
                src = got("yT", m)
                v.tensor_scalar(br2[:, m, :], src[:, :], vec[:, 0, V_SG + m:V_SG + m + 1], None, ALU.mult
                                ).then_inc(dve_read, 1)
                dve.wait_ge(dve_read, read_no[place[("yT", m)]][1])
                high_operand(br2_high, br2, m)
            for m in range(4):
                high_weights("wb2", m)
            def use_pieces(t):
                if t < len(PIECES):
                    for q in range(piece_at[t], piece_at[t + 1]):
                        dve.wait_ge(piece_ld[q % 3], 16 * (q // 3 + 1))
                        if q >= 2:
                            dve.wait_ge(piece_mm, q - 1)
                        o, w = piece_sum[:, q % 2, :], piece_in[q % 3]
                        link(v.tensor_scalar(o, w[:, 0, :], csil[:, 0, 0:1], None, ALU.mult))
                        for k in range(1, KT):
                            ins = v.scalar_tensor_tensor(o, w[:, k, :], csil[:, k, 0:1], o, ALU.mult, ALU.add)
                            if k < KT - 1:
                                link(ins)
                        ins.then_inc(piece_ok, 1)

            merge(2, gate2, 8, prod2, after="pa", pieces=0)
            for m in range(KT):
                if m < 4:
                    high_weights("pa", 4 + m)
                else:
                    high_weights("mg0", m - 4)
                gi, w = m // 2, 2 << (m // 2)
                dve.wait_ge(act_read, read_no[place[("pa", m)]][1])
                rows = lambda ap: ap.rearrange("p (r w) -> p r w", r=GRID_H)
                cur = rows(ppad[:, m % 2, :])
                x0 = cur
                bufs = [rows(psum_a), rows(psum_b)]
                half, step = 1, 0
                lo, hi = 1, PR
                link(v.tensor_tensor(bufs[0][:, :, 1:PR], cur[:, :, 0:PR - 1], cur[:, :, 1:PR], ALU.add))
                cur, n = bufs[0], 2
                while n < w:
                    q = n // 2
                    lo, hi = lo + q, hi - q
                    nxt = bufs[(step + 1) % 2]
                    link(v.tensor_tensor(nxt[:, :, lo:hi], cur[:, :, lo - q:hi - q], cur[:, :, lo + q:hi + q], ALU.add))
                    cur, n, step = nxt, 2 * n, step + 1
                o = rows(pooled[:, m, :])
                link(v.tensor_tensor(o, cur[:, :, 8:8 + GRID_W],
                                     inv_cnt[:, gi, None, :].to_broadcast([P, GRID_H, GRID_W]), ALU.mult))
                v.tensor_tensor(o, o, x0[:, :, 8:8 + GRID_W], ALU.subtract).then_inc(pool_ok, 1)
            for m in range(KT):
                dve.wait_ge(act_read, read_no[place[("pw", m)]][1])
                if m == 0:
                    dve.wait_ge(gemm_done, place[("pw", 7)] + 1)
                high_operand(br0_high, br0, m)
            for m in range(4, 8):
                high_weights("mg0", m)
                use_pieces(KT + m - 4)
            for m in range(4):
                high_weights("wb0", m)
                use_pieces(KT + 4 + m)
            merge(0, gate0, 16, prod2, pieces=2 * KT, after="wo")
            dve.wait_ge(piece_mm, N_PIECE)
            v.tensor_tensor(ada[:, 16:16 + N_PIECE, 0], bank[4][:, 0:N_PIECE], vec[:, 0, V_BADA + 16:V_BADA + 16 + N_PIECE],
                            ALU.add).then_inc(ada2_read, 1)
            dve.wait_ge(ada2_read, 1)
            v.scalar_tensor_tensor(modF[:, :], ada[:, 32:40, 0], 1.0, vec[:, 0, V_GFFN:V_GFFN + 8], ALU.add, ALU.mult
                                   )
            dve.wait_ge(xl_in, 16)
            for m in range(KT):
                if m < 4:
                    high_weights("wo", 4 + m)
                src = got("wo", m)
                v.scalar_tensor_tensor(xl[:, m, :], src[:, :], ada[:, 16 + m, 0:1], xl[:, m, :], ALU.mult, ALU.add
                                       ).then_inc(dve_read, 1)
            for q in range(8):
                i, half = q // 2, q % 2
                src = got("xtok", q)
                v.tensor_copy(xltok[:, i, 512 * half:512 * half + 512], src[:, :]).then_inc(dve_read, 1)
            dve.wait_ge(root2, 1)
            link(v.reciprocal(rn2, rn2))
            dve.wait_ge(dve_read, read_no[place[("wo", 7)]][1])
            v.tensor_tensor(h2T, xl, rn2[:, None, :].to_broadcast([P, KT, T]), ALU.mult).then_inc(normed2, 1)
            for n in range(6, 8):
                dve.wait_ge(ada_done, n - 1)
                add_bias(n, 16 + 4 * n).then_inc(ada2_read, 1)
            dve.wait_ge(iota_ok, 1)
            dve.wait_ge(normed2, 1)
            X = AX.X
            link(v.tensor_scalar(rev, rowid[:, 0:8], -1.0, 8.0, ALU.mult, ALU.add))
            link(v.tensor_tensor(strict, triu[:, :], ident[:, :], ALU.subtract))
            dve.wait_ge(route_mm, 1)
            link(v.tensor_tensor(logit, bank[6][:, 0:NC_LAT * WIDE].rearrange("p (i n) -> p i n", i=NC_LAT)[:, :, 0:36],
                                 b_route[:, None, :].to_broadcast([P, NC_LAT, 36]), ALU.add))
            lg, le = logit[:, :, 0:4], logit[:, :, 4:36]

            def first_max(dst, best, src, n):
                link(v.tensor_reduce(best, src, X, ALU.max))
                sc = rtmp[:, :, 0:n]
                link(v.tensor_tensor(sc, src, best[:, :, None].to_broadcast([P, NC_LAT, n]), ALU.is_equal))
                link(v.tensor_tensor(sc, sc, rev[:, None, 0:n].to_broadcast([P, NC_LAT, n]), ALU.mult))
                link(v.tensor_reduce(rmax, sc, X, ALU.max))
                link(v.tensor_tensor(dst, sc, rmax[:, :, None].to_broadcast([P, NC_LAT, n]), ALU.is_equal))

            first_max(ghot, gmax, lg, 4)
            v.tensor_tensor(gsc, lg, gmax[:, :, None].to_broadcast([P, NC_LAT, 4]), ALU.subtract).then_inc(gexp_pre, 1)
            link(v.tensor_tensor(lmul.rearrange("p (i g) x -> p i g x", i=NC_LAT), le.rearrange("p i (g x) -> p i g x", g=4),
                                 ghot[:, :, :, None].to_broadcast([P, NC_LAT, 4, 8]), ALU.mult))
            link(v.tensor_reduce(lsel, lmul.rearrange("p (i g) x -> p i x g", i=NC_LAT), X, ALU.add))
            first_max(hot[0], top[0], lsel, 8)
            link(v.scalar_tensor_tensor(lsel, hot[0], -BIG, lsel, ALU.mult, ALU.add))
            first_max(hot[1], top[1], lsel, 8)
            v.tensor_tensor(etmp, top[1], top[0], ALU.subtract).then_inc(topexp_pre, 1)
            dve.wait_ge(gexp_ok, 1)
            link(v.tensor_reduce(pgrp, gsc, X, ALU.add))
            dve.wait_ge(topexp_ok, 1)
            link(v.tensor_scalar(wtok[0], etmp, 1.0, None, ALU.add))
            link(v.tensor_tensor(wtok[0], wtok[0], pgrp, ALU.mult))
            link(v.reciprocal(wtok[0], wtok[0]))
            link(v.tensor_tensor(wtok[1], wtok[0], etmp, ALU.mult))
            for j in range(2):
                ins = v.tensor_tensor(member[j].rearrange("p i (g x) -> p i g x", g=4),
                                      ghot[:, :, :, None].to_broadcast([P, NC_LAT, 4, 8]),
                                      hot[j][:, :, None, :].to_broadcast([P, NC_LAT, 4, 8]), ALU.mult)
            link(ins)
            v.tensor_tensor(both, member[0], member[1], ALU.add).then_inc(member_ok, 1)
            for q in range(Q_POOL, 8):
                i, at = q // 2, slice(512 * (q % 2), 512 * (q % 2) + 512)
                dve.wait_ge(split_mid, q + 1)
                v.tensor_tensor(parts[2][:, i, at], h2tok[:, i, at], parts[1][:, i, at], ALU.subtract).then_inc(split_ok, 1)
            dve.wait_ge(pos_mm, 1)
            b7 = bank[7]
            nt = SUBS - 1
            v.tensor_copy(mtot, b7[:, P:2 * P].rearrange("p (i e) -> p i e", i=NC_LAT))
            link(v.tensor_copy(ptmp, b7[:, 0:P].rearrange("p (i e) -> p i e", i=NC_LAT)))
            for i in range(1, NC_LAT):
                v.tensor_tensor(ptmp[:, i, :], ptmp[:, i, :], mtot[:, i - 1, :], ALU.add)
                link(v.tensor_tensor(mtot[:, i, :], mtot[:, i, :], mtot[:, i - 1, :], ALU.add))
            link(v.tensor_scalar(thr[:, 0, :], rowid[:, 1:1 + nt], float(BS), None, ALU.mult))
            link(v.tensor_copy(thr[:, 1:, :], thr[:, 0:1, :].to_broadcast([P, NE - 1, nt])))
            link(v.tensor_tensor(thr, mtot[:, NC_LAT - 1, :, None].to_broadcast([P, NE, nt]), thr, ALU.is_gt))
            link(v.tensor_reduce(nblk, thr, X, ALU.add))
            link(v.tensor_scalar(nblk, nblk, 1.0, None, ALU.add))
            link(v.memset(cumx[:, 0:1], 0.0))
            link(v.tensor_tensor_scan(cumx[:, 1:], ones[:, 0:NE], nblk, 0.0, ALU.mult, ALU.add))
            v.tensor_copy(table[:, :], cumx[0:1, :]).then_inc(table_ok, 1)
            link(v.scalar_tensor_tensor(row, cumx[:, None, 0:NE].to_broadcast([P, NC_LAT, NE]), float(BS), ptmp,
                                        ALU.mult, ALU.add))
            for j in range(2):
                link(v.tensor_tensor(member[j], member[j], row, ALU.mult))
                link(v.tensor_reduce(idxf[:, j::2], member[j], X, ALU.add))
            v.tensor_scalar(idx[:, :], idxf, float(BS), None, ALU.add).then_inc(idx_ok, 1)

            def fill_onehot(n):
                for j in range(2):
                    ins = v.tensor_tensor(eq[j], rowid[:, None, :].to_broadcast([P, NC_LAT, BS]),
                                          idxf[:, j::2, None].to_broadcast([P, NC_LAT, BS]), ALU.is_equal)
                ins.then_inc(eq_ok, 1)
                dve.wait_ge(eq_ok, n + 1)
                v.tensor_tensor(onehot, eq[0], eq[1], ALU.add).then_inc(hot_ok, 1)
                v.tensor_scalar(rowid, rowid, float(BS), None, ALU.add).then_inc(row_ok, 1)

            def split_gathered(n, half):
                dve.wait_ge(xg_hi, n * 2 + (half + 1))
                v.tensor_tensor(xg_low[:, 4 * half:4 * half + 4, :].rearrange("p k s -> p (k s)"),
                                bank[(0, 5)[half]][:, 0:4 * BS],
                                xg_high[:, 4 * half:4 * half + 4, :].rearrange("p k s -> p (k s)").bitcast(f32),
                                ALU.subtract).then_inc(xg_lo, 1)

            def last_rows(n):
                dve.wait_ge(slice_mm, n * SLICES + NSL)
                v.tensor_copy(y_sb[0:BS, 512:1024], bank[4][0:BS, :]).then_inc(y_hi, 1)

            fill_onehot(0)
            for half in range(2):
                split_gathered(0, half)
            dve.wait_ge(row_ok, 1)
            dve.wait_ge(hot_ok, 1)
            fill_onehot(1)
            with dve.Fori(0, NE // 2, 1) as ep:
                for par in range(2):
                    s0 = 3 * (1 - par)
                    first = dve.value_load(table[0:1, bass.ds(2 * ep + par, 1)], min_val=0, max_val=MAXB)
                    end = dve.value_load(table[0:1, bass.ds(2 * ep + (par + 1), 1)], min_val=1, max_val=MAXB)
                    with dve.Fori(first, end, 1) as blk:
                        for u in range(SLICES):
                            dve.wait_ge(slice_hi, blk * SLICES + (u + 1))
                            v.tensor_tensor(slice_low[u % NSL].rearrange("p k n -> p (k n)"),
                                            slot6[s0 + u // 4][:, 1024 * (u % 4):1024 * (u % 4) + 1024],
                                            slice_high[u % NSL].rearrange("p k n -> p (k n)").bitcast(f32),
                                            ALU.subtract).then_inc(slice_lo, 1)
                            if u == NSL - 1:
                                last_rows(blk)
                            if u == 10:
                                dve.wait_ge(sg_ok, blk + 1)
                                v.tensor_tensor(act_tok[0:BS, :], act_tok[0:BS, :], bank[2][0:BS, :], ALU.mult
                                                ).then_inc(a_ok, 1)
                            if u == 11:
                                dve.wait_ge(a_tr, blk + 1)
                                v.tensor_copy(aT_high.rearrange("p f s -> p (f s)"), bank[6][:, 0:4 * BS]).then_inc(a_hi, 1)
                                dve.wait_ge(a_hi, blk + 1)
                                v.tensor_tensor(aT_low.rearrange("p f s -> p (f s)"), bank[6][:, 0:4 * BS],
                                                aT_high.rearrange("p f s -> p (f s)").bitcast(f32), ALU.subtract
                                                ).then_inc(a_lo, 1)
                                for half in range(2):
                                    split_gathered(blk + 1, half)
                        dve.wait_ge(row_ok, blk + 2)
                        dve.wait_ge(hot_ok, blk + 2)
                        fill_onehot(blk + 2)
            n_blocks = dve.value_load(table[0:1, NE:NE + 1], min_val=NE, max_val=MAXB)
            dve.wait_ge(y_out, n_blocks * 16)
            last_rows(n_blocks)
            def finish(i):
                dve.wait_ge(froot, i + 1)
                dve.wait_ge(fin_ok_pre, i + 1)
                link(v.reciprocal(ms[:, i:i + 1], ms[:, i:i + 1]))
                v.scalar_tensor_tensor(yg[2 * i], yg[2 * i], ms[:, i:i + 1], g_last, ALU.mult, ALU.mult
                                       ).then_inc(fin_ok, 1)

            dve.wait_ge(mod_in_s, 32)
            for i in range(NC_LAT):
                dve.wait_ge(yg_in[i], 32)
                a, b = yg[2 * i], yg[2 * i + 1]
                link(v.tensor_scalar(a, a, wtok[0][:, i:i + 1], None, ALU.mult))
                link(v.scalar_tensor_tensor(a, b, wtok[1][:, i:i + 1], a, ALU.mult, ALU.add))
                link(v.tensor_tensor(a, a, mod_out, ALU.mult))
                v.tensor_tensor(a, a, xltok[:, i, :], ALU.add).then_inc(fin_ok_pre, 1)
                if i:
                    finish(i - 1)
            finish(NC_LAT - 1)


_INS = ['x', 'c', 'ctx', 'c_ctx', 'w_ada', 'b_ada', 'g_norm_mix', 'g_norm_ffn', 'w_in', 'pool_w', 'pool_scale',
        'mlstm_conv_w', 'mlstm_conv_b', 'mlstm_gate_b', 'mlstm_norm_g', 'ssd_conv_w', 'ssd_conv_b',
        'ssd_dt_bias', 'ssd_a_log', 'ssd_d', 'ssd_norm_g', 'w_branch', 'w_out', 'w_route_group', 'b_route_group',
        'w_route_expert', 'b_route_expert', 'w_exp_gate', 'w_exp_up', 'w_exp_down', 'g_final']

_OUTS = [((1, T, D), 'float32')]


def kernel(**inputs):
    import numpy as _np
    import concourse.bacc as _bacc
    from concourse import mybir as _mybir
    from concourse.bass_utils import run_bass_kernel_spmd as _run

    nc = _bacc.Bacc("TRN2", target_bir_lowering=False, num_devices=1)
    arrays, args = {}, []
    for name in _INS:
        a = _np.ascontiguousarray(inputs[name])
        arrays[f"in_{name}_dram"] = a
        args.append(nc.dram_tensor(f"in_{name}_dram", a.shape, _mybir.dt.from_np(a.dtype), kind="ExternalInput").ap())
    for i, (shape, dtype) in enumerate(_OUTS):
        dt = _mybir.dt.from_np(_np.dtype(dtype))
        args.append(nc.dram_tensor(f"out_{i}_dram", shape, dt, kind="ExternalOutput").ap())
    build(nc, *args)
    r = _run(nc, [arrays], core_ids=[0])
    got = tuple(r.results[0][f"out_{i}_dram"] for i in range(len(_OUTS)))
    return got[0]
```
